# Optimizing a Trainium2 kernel written in Bass

```python
import jax, jax.numpy as jnp
from jax import lax
import numpy as np

D_MODEL = 1024
BATCH = 1
SEQ = 256
DEPTH = 4

N_MEM = 256
HEAD_DIM = 64
N_MIX_HEADS = 12
MIX_WIDTH = N_MIX_HEADS * HEAD_DIM
N_MEM_HEADS = 4
MEM_WIDTH = N_MEM_HEADS * HEAD_DIM
D_FF = 2816
CHUNK = 128
BLOCK_Q = 128
ROPE_THETA = 10000.0
DILATED_GROUPS = ((128, 1), (512, 4), (2048, 16))
HEADS_PER_DIL_GROUP = N_MIX_HEADS // len(DILATED_GROUPS)
DIL_OUT_WIDTH = HEADS_PER_DIL_GROUP * HEAD_DIM
RMS_EPS = 1e-6
LN_EPS = 1e-5
NEG_INF = -1e30
ATTN_SCALE = HEAD_DIM ** -0.5
MAX_POS_OFFSET = 1024
N_NORMS = 6

N_A = (DEPTH + 2) // 3
N_B = (DEPTH + 1) // 3
N_C = DEPTH // 3
A_IN = 2 * MIX_WIDTH + MEM_WIDTH
A_OUT = MIX_WIDTH + MEM_WIDTH
B_IN = 3 * MIX_WIDTH + MEM_WIDTH
B_OUT = DIL_OUT_WIDTH + MEM_WIDTH
C_IN = 3 * MIX_WIDTH + N_MIX_HEADS + MEM_WIDTH
C_OUT = MIX_WIDTH + MEM_WIDTH


def rms_norm(x, g):
    xf = x.astype(jnp.float32)
    y = xf * lax.rsqrt(jnp.mean(xf * xf, axis=-1, keepdims=True) + RMS_EPS)
    return (y * g.astype(jnp.float32)).astype(x.dtype)

def layer_norm(x, g):
    xf = x.astype(jnp.float32)
    mu = jnp.mean(xf, axis=-1, keepdims=True)
    var = jnp.mean(jnp.square(xf - mu), axis=-1, keepdims=True)
    return ((xf - mu) * lax.rsqrt(var + LN_EPS) * g.astype(jnp.float32)).astype(x.dtype)

def swiglu_ffn(x, w_gate_up, w_down):
    gate, up = jnp.split(x @ w_gate_up, 2, axis=-1)
    return (jax.nn.silu(gate) * up) @ w_down

def rope_tables(positions):
    inv_freq = ROPE_THETA ** (-jnp.arange(0, HEAD_DIM, 2, dtype=jnp.float32) / HEAD_DIM)
    ang = positions.astype(jnp.float32)[..., None] * inv_freq
    return jnp.cos(ang), jnp.sin(ang)

def apply_rope(t, cos, sin):
    c = cos[:, :, None, :].astype(t.dtype)
    s = sin[:, :, None, :].astype(t.dtype)
    t1, t2 = jnp.split(t, 2, axis=-1)
    return jnp.concatenate([t1 * c - t2 * s, t2 * c + t1 * s], axis=-1)

def memory_attention(q_mem, mem_n, w_mem_kv):
    B, S, _ = q_mem.shape
    k, v = jnp.split(mem_n @ w_mem_kv, 2, axis=-1)
    q = q_mem.reshape(B, S, N_MEM_HEADS, HEAD_DIM)
    k = k.reshape(B, -1, N_MEM_HEADS, HEAD_DIM)
    v = v.reshape(B, -1, N_MEM_HEADS, HEAD_DIM)
    s = jnp.einsum('bqhd,bkhd->bhqk', q, k).astype(jnp.float32) * ATTN_SCALE
    p = jax.nn.softmax(s, axis=-1).astype(v.dtype)
    return jnp.einsum('bhqk,bkhd->bqhd', p, v).reshape(B, S, MEM_WIDTH)

def mixer_a(h, mem_n, w_mem_kv, w_in, spatial_w, spatial_b, v_norm_g, w_out):
    B, S, _ = h.shape
    proj = h @ w_in
    uv, q_mem = proj[..., :2 * MIX_WIDTH], proj[..., 2 * MIX_WIDTH:]
    u, v = jnp.split(jax.nn.gelu(uv), 2, axis=-1)
    v = layer_norm(v, v_norm_g).reshape(B, S // CHUNK, CHUNK, N_MIX_HEADS, HEAD_DIM)
    w_causal = spatial_w * jnp.tril(jnp.ones((CHUNK, CHUNK), spatial_w.dtype))
    mixed = jnp.einsum('gts,bcsgd->bctgd', w_causal, v) + spatial_b.T[None, None, :, :, None]
    gated = u * mixed.reshape(B, S, MIX_WIDTH)
    y = jnp.concatenate([gated, memory_attention(q_mem, mem_n, w_mem_kv)], axis=-1)
    return y @ w_out

def dilated_window_attention(q, k, v, window, dilation):
    B, S, H, Dh = q.shape
    span = window // dilation
    L = S // dilation
    nb = -(-L // span)
    Lp = nb * span

    def to_blocks(t):
        t = t.reshape(B, L, dilation, H, Dh).transpose(0, 2, 1, 3, 4)
        t = jnp.pad(t, ((0, 0), (0, 0), (0, Lp - L), (0, 0), (0, 0)))
        return t.reshape(B, dilation, nb, span, H, Dh)

    def with_prev(t):
        prev = jnp.pad(t, ((0, 0), (0, 0), (1, 0), (0, 0), (0, 0), (0, 0)))[:, :, :-1]
        return jnp.concatenate([prev, t], axis=3)

    qb = to_blocks(q)
    kk = with_prev(to_blocks(k))
    vv = with_prev(to_blocks(v))
    s = jnp.einsum('brnqhd,brnkhd->brnhqk', qb, kk).astype(jnp.float32) * ATTN_SCALE
    qi = jnp.arange(span)[:, None] + span
    ki = jnp.arange(2 * span)[None, :]
    dist = qi - ki
    band = (dist >= 0) & (dist <= span)
    first = jnp.arange(nb)[:, None, None] == 0
    valid = band[None] & ~(first & (ki < span)[None])
    s = jnp.where(valid[None, None, :, None], s, NEG_INF)
    m = jnp.max(s, axis=-1, keepdims=True)
    p = jnp.exp(s - m)
    denom = jnp.sum(p, axis=-1, keepdims=True)
    out = jnp.einsum('brnhqk,brnkhd->brnqhd', (p / denom).astype(v.dtype), vv)
    lse = (m + jnp.log(denom))[..., 0]
    out = out.reshape(B, dilation, Lp, H, Dh)[:, :, :L].transpose(0, 2, 1, 3, 4).reshape(B, S, H, Dh)
    lse = lse.transpose(0, 1, 2, 4, 3).reshape(B, dilation, Lp, H)[:, :, :L]
    lse = lse.transpose(0, 2, 1, 3).reshape(B, S, H)
    return out, lse

def mixer_b(h, mem_n, w_mem_kv, cos, sin, w_in, w_out):
    B, S, _ = h.shape
    q, k, v, q_mem = jnp.split(h @ w_in, [MIX_WIDTH, 2 * MIX_WIDTH, 3 * MIX_WIDTH], axis=-1)
    q = apply_rope(q.reshape(B, S, N_MIX_HEADS, HEAD_DIM), cos, sin)
    k = apply_rope(k.reshape(B, S, N_MIX_HEADS, HEAD_DIM), cos, sin)
    v = v.reshape(B, S, N_MIX_HEADS, HEAD_DIM)
    outs, lses = [], []
    for g, (window, dilation) in enumerate(DILATED_GROUPS):
        hs = slice(g * HEADS_PER_DIL_GROUP, (g + 1) * HEADS_PER_DIL_GROUP)
        o, l = dilated_window_attention(q[:, :, hs], k[:, :, hs], v[:, :, hs], window, dilation)
        outs.append(o)
        lses.append(l)
    wts = jax.nn.softmax(jnp.stack(lses, axis=0), axis=0)
    merged = jnp.sum(wts[..., None].astype(v.dtype) * jnp.stack(outs, axis=0), axis=0)
    merged = merged.reshape(B, S, DIL_OUT_WIDTH)
    y = jnp.concatenate([merged, memory_attention(q_mem, mem_n, w_mem_kv)], axis=-1)
    return y @ w_out

def forgetting_attention(q, k, v, log_f):
    B, S, H, Dh = q.shape
    c = jnp.cumsum(log_f.astype(jnp.float32), axis=1).transpose(0, 2, 1)
    q_idx = jnp.arange(BLOCK_Q)
    outs = []
    for i in range(S // BLOCK_Q):
        lo, hi = i * BLOCK_Q, (i + 1) * BLOCK_Q
        s = jnp.einsum('bqhd,bkhd->bhqk', q[:, lo:hi], k[:, :hi]).astype(jnp.float32) * ATTN_SCALE
        s = s + c[:, :, lo:hi, None] - c[:, :, None, :hi]
        causal = (lo + q_idx)[:, None] >= jnp.arange(hi)[None, :]
        p = jax.nn.softmax(jnp.where(causal, s, NEG_INF), axis=-1).astype(v.dtype)
        outs.append(jnp.einsum('bhqk,bkhd->bqhd', p, v[:, :hi]))
    return jnp.concatenate(outs, axis=1)

def mixer_c(h, mem_n, w_mem_kv, w_in, forget_bias, w_out):
    B, S, _ = h.shape
    q, k, v, f_logit, q_mem = jnp.split(
        h @ w_in, [MIX_WIDTH, 2 * MIX_WIDTH, 3 * MIX_WIDTH, 3 * MIX_WIDTH + N_MIX_HEADS], axis=-1)
    log_f = jax.nn.log_sigmoid(f_logit.astype(jnp.float32) + forget_bias.astype(jnp.float32))
    heads = lambda t: t.reshape(B, S, N_MIX_HEADS, HEAD_DIM)
    att = forgetting_attention(heads(q), heads(k), heads(v), log_f).reshape(B, S, MIX_WIDTH)
    y = jnp.concatenate([att, memory_attention(q_mem, mem_n, w_mem_kv)], axis=-1)
    return y @ w_out

def first_inputs(seed: int = 0) -> dict:
    key = jax.random.key(seed)
    ks = jax.random.split(key, 20)
    f32 = jnp.float32

    def dense(k, shape, fan_in):
        return jax.random.normal(k, shape, f32) * fan_in ** -0.5

    def gain(k, shape):
        return 1.0 + 0.02 * jax.random.normal(k, shape, f32)

    x = jax.random.normal(ks[0], (BATCH, SEQ, D_MODEL), f32)
    mem = jax.random.normal(ks[1], (BATCH, N_MEM, D_MODEL), f32)
    offset = jax.random.randint(ks[2], (BATCH, 1), 0, MAX_POS_OFFSET, dtype=jnp.int32)
    positions = (offset + jnp.arange(SEQ, dtype=jnp.int32)[None, :]).astype(jnp.int32)
    return {
        'x': x,
        'mem': mem,
        'positions': positions,
        'norm_g': gain(ks[3], (DEPTH, N_NORMS, D_MODEL)),
        'mem_norm_g': gain(ks[4], (DEPTH, D_MODEL)),
        'w_mem_kv': dense(ks[5], (DEPTH, D_MODEL, 2 * MEM_WIDTH), D_MODEL),
        'ffn_w_gate_up': dense(ks[6], (DEPTH, 2, D_MODEL, 2 * D_FF), D_MODEL),
        'ffn_w_down': dense(ks[7], (DEPTH, 2, D_FF, D_MODEL), D_FF),
        'a_w_in': dense(ks[8], (N_A, D_MODEL, A_IN), D_MODEL),
        'a_spatial_w': dense(ks[9], (N_A, N_MIX_HEADS, CHUNK, CHUNK), CHUNK),
        'a_spatial_b': gain(ks[10], (N_A, N_MIX_HEADS, CHUNK)),
        'a_v_norm_g': gain(ks[11], (N_A, MIX_WIDTH)),
        'a_w_out': dense(ks[12], (N_A, A_OUT, D_MODEL), A_OUT),
        'b_w_in': dense(ks[13], (N_B, D_MODEL, B_IN), D_MODEL),
        'b_w_out': dense(ks[14], (N_B, B_OUT, D_MODEL), B_OUT),
        'c_w_in': dense(ks[15], (N_C, D_MODEL, C_IN), D_MODEL),
        'c_forget_bias': jax.random.uniform(ks[16], (N_C, N_MIX_HEADS), f32, 1.0, 5.0),
        'c_w_out': dense(ks[17], (N_C, C_OUT, D_MODEL), C_OUT),
    }

def first_block(x, mem, positions, norm_g, mem_norm_g, w_mem_kv, ffn_w_gate_up, ffn_w_down,
              a_w_in, a_spatial_w, a_spatial_b, a_v_norm_g, a_w_out,
              b_w_in, b_w_out, c_w_in, c_forget_bias, c_w_out):
    cos, sin = rope_tables(positions)
    for i in range(DEPTH):
        kind, j = i % 3, i // 3
        g = norm_g[i]
        x = x + 0.5 * rms_norm(swiglu_ffn(rms_norm(x, g[0]), ffn_w_gate_up[i, 0], ffn_w_down[i, 0]), g[1])
        h = rms_norm(x, g[2])
        mem_n = rms_norm(mem, mem_norm_g[i])
        if kind == 0:
            y = mixer_a(h, mem_n, w_mem_kv[i], a_w_in[j], a_spatial_w[j], a_spatial_b[j],
                        a_v_norm_g[j], a_w_out[j])
        elif kind == 1:
            y = mixer_b(h, mem_n, w_mem_kv[i], cos, sin, b_w_in[j], b_w_out[j])
        else:
            y = mixer_c(h, mem_n, w_mem_kv[i], c_w_in[j], c_forget_bias[j], c_w_out[j])
        x = x + rms_norm(y, g[3])
        x = x + 0.5 * rms_norm(swiglu_ffn(rms_norm(x, g[4]), ffn_w_gate_up[i, 1], ffn_w_down[i, 1]), g[5])
    return x


N_MIXERS = 4
N_HEADS = 8
HEAD_DIM_2 = D_MODEL // N_HEADS
D_FF_2 = 4 * D_MODEL
NORM_EPS = 1e-6
NEG_INF_2 = -1e30

NSA_KV_GROUPS = 2
NSA_HEADS_PER_GROUP = N_HEADS // NSA_KV_GROUPS
NSA_CMP_BLOCK = 32
NSA_CMP_STRIDE = 16
NSA_SEL_BLOCK = 64
NSA_SEL_TOPK = 16
NSA_WINDOW = 512
NSA_QBLOCK = 64
NSA_FORCE_BONUS = 1000.0
NSA_IN_DIM = N_HEADS * HEAD_DIM_2 + 6 * NSA_KV_GROUPS * HEAD_DIM_2 + 3 * N_HEADS

SB_QBLOCK = 128

CONV_WIDTH = 31

MOBA_BLOCK = 256
MOBA_TOPK = 3
MOBA_QBLOCK = 32

N_NSA = (DEPTH + 3) // 4
N_SB = (DEPTH + 2) // 4
N_CONV = (DEPTH + 1) // 4
N_MOBA = DEPTH // 4


def _rms_norm(x, g):
    xf = x.astype(jnp.float32)
    y = xf * lax.rsqrt(jnp.mean(xf * xf, axis=-1, keepdims=True) + NORM_EPS)
    return (y * g.astype(jnp.float32)).astype(x.dtype)

def _rope_tables(seq):
    half = HEAD_DIM_2 // 2
    inv_freq = ROPE_THETA ** (-jnp.arange(half, dtype=jnp.float32) / half)
    ang = jnp.arange(seq, dtype=jnp.float32)[:, None] * inv_freq[None, :]
    return jnp.cos(ang), jnp.sin(ang)

def _apply_rope(x, cos, sin):
    xf = x.astype(jnp.float32)
    x1, x2 = jnp.split(xf, 2, axis=-1)
    c = cos[None, :, None, :]
    s = sin[None, :, None, :]
    return jnp.concatenate([x1 * c - x2 * s, x1 * s + x2 * c], axis=-1).astype(x.dtype)

def _masked_softmax(logits, mask):
    z = jnp.where(mask, logits.astype(jnp.float32), NEG_INF_2)
    return jnp.where(mask, jax.nn.softmax(z, axis=-1), 0.0)

def _nsa_mixer(h, w_in, q_gain, k_gain, cmp_pos, w_cmp, w_out, cos, sin):
    B, S, _ = h.shape
    H, G, HG, DH = N_HEADS, NSA_KV_GROUPS, NSA_HEADS_PER_GROUP, HEAD_DIM_2
    L, STR, SB, W, QB = NSA_CMP_BLOCK, NSA_CMP_STRIDE, NSA_SEL_BLOCK, NSA_WINDOW, NSA_QBLOCK
    sizes = [H * DH] + [G * DH] * 6
    q, kc, vc, ks, vs, kw, vw, gates = jnp.split(h @ w_in, np.cumsum(sizes).tolist(), axis=-1)
    q = _apply_rope(_rms_norm(q.reshape(B, S, H, DH), q_gain), cos, sin)
    kc, ks, kw = [_apply_rope(_rms_norm(k.reshape(B, S, G, DH), k_gain[i]), cos, sin)
                  for i, k in enumerate((kc, ks, kw))]
    vc, vs, vw = [v.reshape(B, S, G, DH) for v in (vc, vs, vw)]
    gates = jax.nn.sigmoid(gates.astype(jnp.float32)).reshape(B, S, 3, G, HG)
    n_cmp = (S - L) // STR + 1
    cmp_start = jnp.arange(n_cmp) * STR
    cidx = cmp_start[:, None] + jnp.arange(L)[None, :]
    kc = jnp.einsum('bnlgd,lde->bnge', kc[:, cidx] + cmp_pos[0][None, None, :, None, :], w_cmp[0])
    vc = jnp.einsum('bnlgd,lde->bnge', vc[:, cidx] + cmp_pos[1][None, None, :, None, :], w_cmp[1])
    cmp_end = cmp_start + L - 1
    n_sel = S // SB
    sel_start = jnp.arange(n_sel) * SB
    overlap = ((cmp_start[:, None] < sel_start[None, :] + SB)
               & (cmp_start[:, None] + L > sel_start[None, :])).astype(jnp.float32)
    topk = min(NSA_SEL_TOPK, n_sel)
    ks_blk = ks.reshape(B, n_sel, SB, G, DH).transpose(0, 3, 1, 2, 4)
    vs_blk = vs.reshape(B, n_sel, SB, G, DH).transpose(0, 3, 1, 2, 4)
    kw_pad = jnp.pad(kw, ((0, 0), (W, 0), (0, 0), (0, 0)))
    vw_pad = jnp.pad(vw, ((0, 0), (W, 0), (0, 0), (0, 0)))
    scale = DH ** -0.5
    b_ix = jnp.arange(B)[:, None, None, None]
    g_ix = jnp.arange(G)[None, None, :, None]
    blk = jnp.arange(n_sel)
    in_blk = jnp.arange(SB)
    win_off = jnp.arange(W + QB) - W

    def chunk(c0):
        t = c0 + jnp.arange(QB)
        qc = lax.dynamic_slice_in_dim(q, c0, QB, axis=1).reshape(B, QB, G, HG, DH)
        p_c = _masked_softmax(jnp.einsum('bqghd,bngd->bqghn', qc, kc) * scale,
                              (cmp_end[None, :] <= t[:, None])[None, :, None, None, :])
        o_c = jnp.einsum('bqghn,bngd->bqghd', p_c.astype(vc.dtype), vc)
        imp = jnp.einsum('bqgn,nj->bqgj', p_c.sum(axis=3), overlap)
        cur = c0 // SB
        forced = (blk == 0) | (blk == cur) | (blk == cur - 1)
        imp = jnp.where(blk <= cur, imp + NSA_FORCE_BONUS * forced, -1.0)
        _, idx = lax.top_k(imp, topk)
        k_sel = ks_blk[b_ix, g_ix, idx].reshape(B, QB, G, topk * SB, DH)
        v_sel = vs_blk[b_ix, g_ix, idx].reshape(B, QB, G, topk * SB, DH)
        pos = (idx[..., None] * SB + in_blk).reshape(B, QB, G, 1, topk * SB)
        p_s = _masked_softmax(jnp.einsum('bqghd,bqgmd->bqghm', qc, k_sel) * scale,
                              pos <= t[None, :, None, None, None])
        o_s = jnp.einsum('bqghm,bqgmd->bqghd', p_s.astype(v_sel.dtype), v_sel)
        pos_w = c0 + win_off
        diff = t[:, None] - pos_w[None, :]
        m_w = ((pos_w[None, :] >= 0) & (diff >= 0) & (diff < W))[None, :, None, None, :]
        kwc = lax.dynamic_slice_in_dim(kw_pad, c0, W + QB, axis=1)
        vwc = lax.dynamic_slice_in_dim(vw_pad, c0, W + QB, axis=1)
        p_w = _masked_softmax(jnp.einsum('bqghd,bkgd->bqghk', qc, kwc) * scale, m_w)
        o_w = jnp.einsum('bqghk,bkgd->bqghd', p_w.astype(vwc.dtype), vwc)
        g = lax.dynamic_slice_in_dim(gates, c0, QB, axis=1)[..., None]
        o = g[:, :, 0] * o_c + g[:, :, 1] * o_s + g[:, :, 2] * o_w
        return o.reshape(B, QB, H * DH).astype(h.dtype)

    out = lax.map(chunk, jnp.arange(S // QB) * QB)
    out = jnp.transpose(out, (1, 0, 2, 3)).reshape(B, S, H * DH)
    return out @ w_out

def _stick_breaking_mixer(h, w_in, w_out):
    B, S, _ = h.shape
    H, DH, QB = N_HEADS, HEAD_DIM_2, SB_QBLOCK
    q, k, v = [a.reshape(B, S, H, DH) for a in jnp.split(h @ w_in, 3, axis=-1)]
    scale = DH ** -0.5
    s_idx = jnp.arange(S)

    def chunk(c0):
        t = c0 + jnp.arange(QB)
        qc = lax.dynamic_slice_in_dim(q, c0, QB, axis=1)
        z = jnp.einsum('bqhd,bshd->bhqs', qc, k).astype(jnp.float32) * scale
        mask = (s_idx[None, :] < t[:, None])[None, None]
        log_beta = jax.nn.log_sigmoid(z)
        log_one_minus = jnp.where(mask, jax.nn.log_sigmoid(-z), 0.0)
        between = lax.cumsum(log_one_minus, axis=3, reverse=True) - log_one_minus
        a = jnp.where(mask, jnp.exp(log_beta + between), 0.0)
        o = jnp.einsum('bhqs,bshd->bqhd', a.astype(v.dtype), v)
        return o.reshape(B, QB, H * DH)

    out = lax.map(chunk, jnp.arange(S // QB) * QB)
    out = jnp.transpose(out, (1, 0, 2, 3)).reshape(B, S, H * DH)
    return out @ w_out

def _conformer_conv_mixer(h, w_in, dw_w, dw_b, ln_g, ln_b, w_out):
    a, b = jnp.split(h @ w_in, 2, axis=-1)
    u = a * jax.nn.sigmoid(b)
    u = lax.conv_general_dilated(u, dw_w[:, None, :], window_strides=(1,),
                                 padding=[(CONV_WIDTH - 1, 0)],
                                 dimension_numbers=('NWC', 'WIO', 'NWC'),
                                 feature_group_count=D_MODEL) + dw_b
    uf = u.astype(jnp.float32)
    mu = jnp.mean(uf, axis=-1, keepdims=True)
    var = jnp.mean(jnp.square(uf - mu), axis=-1, keepdims=True)
    un = (uf - mu) * lax.rsqrt(var + NORM_EPS) * ln_g.astype(jnp.float32) + ln_b.astype(jnp.float32)
    return jax.nn.silu(un).astype(h.dtype) @ w_out

def _moba_mixer(h, w_in, q_gain, k_gain, w_out, cos, sin):
    B, S, _ = h.shape
    H, DH, BS, QB = N_HEADS, HEAD_DIM_2, MOBA_BLOCK, MOBA_QBLOCK
    q, k, v = [a.reshape(B, S, H, DH) for a in jnp.split(h @ w_in, 3, axis=-1)]
    q = _apply_rope(_rms_norm(q, q_gain), cos, sin)
    k = _apply_rope(_rms_norm(k, k_gain), cos, sin)
    n_blk = -(-S // BS)
    pad = n_blk * BS - S
    kp = jnp.pad(k, ((0, 0), (0, pad), (0, 0), (0, 0)))
    vp = jnp.pad(v, ((0, 0), (0, pad), (0, 0), (0, 0)))
    k_blocks = kp.reshape(B, n_blk, BS, H, DH)
    k_mean = jnp.mean(k_blocks.astype(jnp.float32), axis=2)
    kb_t = k_blocks.transpose(0, 3, 1, 2, 4)
    vb_t = vp.reshape(B, n_blk, BS, H, DH).transpose(0, 3, 1, 2, 4)
    topk = min(MOBA_TOPK, n_blk)
    scale = DH ** -0.5
    b_ix = jnp.arange(B)[:, None, None, None]
    h_ix = jnp.arange(H)[None, None, :, None]
    blk = jnp.arange(n_blk)

    def chunk(c0):
        t = c0 + jnp.arange(QB)
        qc = lax.dynamic_slice_in_dim(q, c0, QB, axis=1)
        cur = c0 // BS
        gate = jnp.einsum('bqhd,bnhd->bqhn', qc.astype(jnp.float32), k_mean)
        gate = jnp.where(blk < cur, gate, NEG_INF_2)
        _, idx = lax.top_k(gate, topk)
        valid = idx < cur
        k_sel = kb_t[b_ix, h_ix, idx].reshape(B, QB, H, topk * BS, DH)
        v_sel = vb_t[b_ix, h_ix, idx].reshape(B, QB, H, topk * BS, DH)
        s_past = jnp.einsum('bqhd,bqhmd->bqhm', qc, k_sel) * scale
        m_past = jnp.broadcast_to(valid[..., None], (B, QB, H, topk, BS)).reshape(B, QB, H, topk * BS)
        own0 = cur * BS
        k_own = lax.dynamic_slice_in_dim(kp, own0, BS, axis=1)
        v_own = lax.dynamic_slice_in_dim(vp, own0, BS, axis=1)
        s_own = jnp.einsum('bqhd,bkhd->bqhk', qc, k_own) * scale
        m_own = jnp.broadcast_to(((own0 + jnp.arange(BS))[None, :] <= t[:, None])[None, :, None, :],
                                 (B, QB, H, BS))
        p = _masked_softmax(jnp.concatenate([s_past, s_own], axis=-1),
                            jnp.concatenate([m_past, m_own], axis=-1))
        p = p.astype(v.dtype)
        o = (jnp.einsum('bqhm,bqhmd->bqhd', p[..., :topk * BS], v_sel)
             + jnp.einsum('bqhk,bkhd->bqhd', p[..., topk * BS:], v_own))
        return o.reshape(B, QB, H * DH)

    out = lax.map(chunk, jnp.arange(S // QB) * QB)
    out = jnp.transpose(out, (1, 0, 2, 3)).reshape(B, S, H * DH)
    return out @ w_out

def second_inputs(seed: int = 0) -> dict:
    key = jax.random.key(seed)
    keys = iter(jax.random.split(key, 32))

    def w(shape, fan_in):
        return jax.random.normal(next(keys), shape, jnp.float32) * (fan_in ** -0.5)

    def gain(shape):
        return 1.0 + 0.05 * jax.random.normal(next(keys), shape, jnp.float32)

    def small(shape, s):
        return s * jax.random.normal(next(keys), shape, jnp.float32)

    D, DH, L = D_MODEL, HEAD_DIM_2, NSA_CMP_BLOCK
    return {
        'x': jax.random.normal(next(keys), (BATCH, SEQ, D), jnp.float32),
        'attn_norm': gain((DEPTH, D)),
        'mlp_norm': gain((DEPTH, D)),
        'mlp_w_up': w((DEPTH, D, D_FF_2), D),
        'mlp_w_down': w((DEPTH, D_FF_2, D), D_FF_2),
        'nsa_w_in': w((N_NSA, D, NSA_IN_DIM), D),
        'nsa_q_norm': gain((N_NSA, DH)),
        'nsa_k_norm': gain((N_NSA, 3, DH)),
        'nsa_cmp_pos': small((N_NSA, 2, L, DH), 0.1),
        'nsa_w_cmp': w((N_NSA, 2, L, DH, DH), L * DH),
        'nsa_w_out': w((N_NSA, N_HEADS * DH, D), N_HEADS * DH),
        'sb_w_in': w((N_SB, D, 3 * N_HEADS * DH), D),
        'sb_w_out': w((N_SB, N_HEADS * DH, D), N_HEADS * DH),
        'conv_w_in': w((N_CONV, D, 2 * D), D),
        'conv_dw_w': w((N_CONV, CONV_WIDTH, D), CONV_WIDTH),
        'conv_dw_b': small((N_CONV, D), 0.02),
        'conv_ln_g': gain((N_CONV, D)),
        'conv_ln_b': small((N_CONV, D), 0.02),
        'conv_w_out': w((N_CONV, D, D), D),
        'moba_w_in': w((N_MOBA, D, 3 * N_HEADS * DH), D),
        'moba_q_norm': gain((N_MOBA, DH)),
        'moba_k_norm': gain((N_MOBA, DH)),
        'moba_w_out': w((N_MOBA, N_HEADS * DH, D), N_HEADS * DH),
    }

def second_block(x, attn_norm, mlp_norm, mlp_w_up, mlp_w_down,
              nsa_w_in, nsa_q_norm, nsa_k_norm, nsa_cmp_pos, nsa_w_cmp, nsa_w_out,
              sb_w_in, sb_w_out,
              conv_w_in, conv_dw_w, conv_dw_b, conv_ln_g, conv_ln_b, conv_w_out,
              moba_w_in, moba_q_norm, moba_k_norm, moba_w_out):
    cos, sin = _rope_tables(x.shape[1])
    for i in range(DEPTH):
        m, j = i % N_MIXERS, i // N_MIXERS
        h = _rms_norm(x, attn_norm[i])
        if m == 0:
            y = _nsa_mixer(h, nsa_w_in[j], nsa_q_norm[j], nsa_k_norm[j], nsa_cmp_pos[j],
                           nsa_w_cmp[j], nsa_w_out[j], cos, sin)
        elif m == 1:
            y = _stick_breaking_mixer(h, sb_w_in[j], sb_w_out[j])
        elif m == 2:
            y = _conformer_conv_mixer(h, conv_w_in[j], conv_dw_w[j], conv_dw_b[j],
                                      conv_ln_g[j], conv_ln_b[j], conv_w_out[j])
        else:
            y = _moba_mixer(h, moba_w_in[j], moba_q_norm[j], moba_k_norm[j], moba_w_out[j], cos, sin)
        x = x + y.astype(x.dtype)
        hm = _rms_norm(x, mlp_norm[i])
        x = x + jnp.square(jax.nn.relu(hm @ mlp_w_up[i])) @ mlp_w_down[i]
    return x


def setup_inputs(seed=0):
    out = dict(first_inputs(seed))
    for name, value in second_inputs(seed + 1).items():
        if name != "x":
            out[name + "_2"] = value
    return out


def reference(
    x, mem, positions, norm_g, mem_norm_g, w_mem_kv, ffn_w_gate_up, ffn_w_down, a_w_in,
    a_spatial_w, a_spatial_b, a_v_norm_g, a_w_out, b_w_in, b_w_out, c_w_in, c_forget_bias,
    c_w_out, attn_norm_2, mlp_norm_2, mlp_w_up_2, mlp_w_down_2, nsa_w_in_2, nsa_q_norm_2,
    nsa_k_norm_2, nsa_cmp_pos_2, nsa_w_cmp_2, nsa_w_out_2, sb_w_in_2, sb_w_out_2, conv_w_in_2,
    conv_dw_w_2, conv_dw_b_2, conv_ln_g_2, conv_ln_b_2, conv_w_out_2, moba_w_in_2,
    moba_q_norm_2, moba_k_norm_2, moba_w_out_2,
):
    x = first_block(
        x, mem, positions, norm_g, mem_norm_g, w_mem_kv, ffn_w_gate_up, ffn_w_down, a_w_in,
        a_spatial_w, a_spatial_b, a_v_norm_g, a_w_out, b_w_in, b_w_out, c_w_in, c_forget_bias,
        c_w_out,
    )
    return second_block(
        x, attn_norm_2, mlp_norm_2, mlp_w_up_2, mlp_w_down_2, nsa_w_in_2, nsa_q_norm_2,
        nsa_k_norm_2, nsa_cmp_pos_2, nsa_w_cmp_2, nsa_w_out_2, sb_w_in_2, sb_w_out_2,
        conv_w_in_2, conv_dw_w_2, conv_dw_b_2, conv_ln_g_2, conv_ln_b_2, conv_w_out_2,
        moba_w_in_2, moba_q_norm_2, moba_k_norm_2, moba_w_out_2,
    )


_drawn_inputs = setup_inputs


def setup_inputs(seed=0):
    import zlib

    import numpy as np

    out = dict(_drawn_inputs(seed))
    spreads = {}
    factors = {'mem_norm_g': 6.599,
     'a_spatial_b': 3.338,
     'a_v_norm_g': 5.512,
     'nsa_q_norm_2': 8.0,
     'nsa_k_norm_2': 8.0,
     'nsa_cmp_pos_2': 2.851,
     'conv_dw_b_2': 7.079,
     'conv_ln_g_2': 4.868,
     'conv_ln_b_2': 8.0,
     'moba_q_norm_2': 8.0,
     'moba_k_norm_2': 8.0}
    for name, (base, spread) in spreads.items():
        noise = np.random.default_rng([zlib.crc32(name.encode()), seed]).standard_normal(out[name].shape)
        drawn = base * np.exp(spread * noise) if base else spread * noise
        out[name] = __import__('jax').numpy.asarray(drawn.astype(out[name].dtype))
    for name, factor in factors.items():
        out[name] = (out[name] * factor).astype(out[name].dtype)
    return out
```

```python
from contextlib import ExitStack

import numpy as np

import concourse.bass as bass
from concourse import mybir

ALU = mybir.AluOpType
ACT = mybir.ActivationFunctionType
F32 = mybir.dt.float32
I32 = mybir.dt.int32
AX_X = mybir.AxisListType.X

P = 128
SEQ = 256
TT = SEQ // P
D = 1024
KT = D // P
DEPTH = 4
HALF = 512
RING = 8
UNIT_K = 2
CHUNK_UNITS = KT // UNIT_K
LOADED = 16

N_MEM = 256
DH1 = 64
HEADS1 = 12
MIX = HEADS1 * DH1
MEM_HEADS = 4
MEMW = MEM_HEADS * DH1
FF1 = 2816
A_IN = 2 * MIX + MEMW
B_IN = 3 * MIX + MEMW
C_IN = 3 * MIX + HEADS1 + MEMW
DIL_OUT = 4 * DH1
B_OUT = DIL_OUT + MEMW
RMS_EPS, LN_EPS = 1e-6, 1e-5
NEG = -1e30
SCALE1 = DH1 ** -0.5
WINDOW = 128

H2 = 8
DH2 = 128
FF2 = 4096
KVG = 2
HPG = H2 // KVG
CMP_L, CMP_STRIDE = 32, 16
N_CMP = (SEQ - CMP_L) // CMP_STRIDE + 1
NSA_IN = D + 6 * KVG * DH2 + 3 * H2
SCALE2 = DH2 ** -0.5
CONV_W = 31
PAD = CONV_W - 1

TWO_PI = 6.283185307179586
PI_A, PI_B = 6.28125, 0.0019350051879882812
PI_C = TWO_PI - PI_A - PI_B
PI_TOP = 3.1415925
ROUND = 12582912.0


def constants():
    q = np.arange(SEQ)[:, None]
    k = np.arange(SEQ)[None, :]
    s = np.arange(P)

    def additive(keep):
        m = np.where(keep, 0.0, NEG).astype(np.float32)
        return m.reshape(TT, P, -1).transpose(1, 0, 2).reshape(P, -1)

    dist = q - k
    cmp_end = np.arange(N_CMP)[None, :] * CMP_STRIDE + CMP_L - 1
    half2 = DH2 // 2
    inv2 = (np.float32(10000.0) ** (-np.arange(half2, dtype=np.float32) / np.float32(half2))).astype(np.float32)
    ang2 = (np.arange(SEQ, dtype=np.float32)[:, None] * inv2[None, :]).astype(np.float32)
    inv1 = (np.float32(10000.0) ** (-np.arange(0, DH1, 2, dtype=np.float32) / np.float32(DH1))).astype(np.float32)

    def rows(t):
        return t.astype(np.float32).reshape(TT, P, -1).transpose(1, 0, 2).reshape(P, -1)

    strict = (k > q)
    parts = [
        ("ident", np.eye(P)),
        ("upto", (s[:, None] <= np.arange(SEQ)[None, :])),
        ("from_on", (s[:, None] >= s[None, :])),
        ("ones", np.ones((P, P))),
        ("causal", additive(dist >= 0)),
        ("band", additive((dist >= 0) & (dist <= WINDOW))),
        ("dil4", additive((dist >= 0) & (dist % 4 == 0))),
        ("dil16", additive((dist >= 0) & (dist % 16 == 0))),
        ("cmp", additive(cmp_end <= q)),
        ("cmp_any", rows((q >= CMP_L - 1))),
        ("strict_add", additive(strict)),
        ("strict_one", rows(strict)),
        ("cos2", rows(np.cos(ang2.astype(np.float64)))),
        ("sin2", rows(np.sin(ang2.astype(np.float64)))),
        ("inv_freq", np.broadcast_to(inv1[None, :], (P, DH1 // 2))),
        ("minus_half", np.full((P, 16), -0.5)),
    ]
    where, at = {}, 0
    for name, a in parts:
        where[name] = (at, a.shape[1])
        at += a.shape[1]
    return where, np.ascontiguousarray(np.concatenate([np.asarray(a, np.float32) for _, a in parts], 1))


WHERE, CONSTS = constants()


class Counts(dict):

    def __missing__(self, key):
        return 0

    def up(self, key, by=1):
        self[key] = self[key] + by
        return self[key]


def build(nc, a, out, stages):
    with ExitStack() as ctx:
        def sb(name, shape, dt=F32):
            return ctx.enter_context(nc.sbuf_tensor(name + "_sb", shape, dt))

        def sem(name):
            return ctx.enter_context(nc.semaphore(name))

        ring = sb("ring", [P, RING, 2, HALF])
        con = sb("con", [P, CONSTS.shape[1]])
        x = sb("x", [P, TT, D])
        nrm = sb("nrm", [P, TT, D])
        act_t = sb("act_t", [P, KT, SEQ])
        hid_t = sb("hid_t", [P, 32, SEQ])
        mem_ts = sb("mem_ts", [P, 2 * KT * SEQ])
        mem_t = mem_ts[:, 0:KT * SEQ].rearrange("p (k s) -> p k s", k=KT)
        memn_t = mem_ts[:, KT * SEQ:2 * KT * SEQ].rearrange("p (k s) -> p k s", k=KT)
        conv_in = mem_ts[:, 0:KT * (PAD + SEQ)].rearrange("p (k s) -> p k s", k=KT)
        work = sb("work", [P, 4, 2 * HALF])
        gated = work[:, 0:2, :].rearrange("p a (t n) -> p a t n", t=TT)
        hid = work[:, 2:4, :].rearrange("p a (t n) -> p a t n", t=TT)
        qk = work[:, 0, :].rearrange("p (b n) -> p b n", b=2)
        sc = work[:, 1, :].rearrange("p (b t n) -> p b t n", b=2, t=TT)
        pr = work[:, 2, :].rearrange("p (b t n) -> p b t n", b=2, t=TT)
        pt = work[:, 3, :].rearrange("p (b n) -> p b n", b=2)
        proj = sb("proj", [P, TT, 3072])
        memkv = sb("memkv", [P, TT, 2 * MEMW])
        ymix = sb("ymix", [P, TT, D])
        scratch = sb("scratch", [P, D])
        scratch_v = sb("scratch_v", [P, 2, D])
        pre_cols = sb("pre_cols", [P, 6 * DEPTH, KT])
        mem_cols = sb("mem_cols", [P, DEPTH, KT])
        an_cols = sb("an_cols", [P, DEPTH, KT])
        mn_cols = sb("mn_cols", [P, DEPTH, KT])
        small = sb("small", [P, 64])
        sums = sb("sums", [P, 64])
        den = sb("den", [P, 64])
        mx = sb("mx", [P, 64])
        spat_w = sb("spat_w", [P, HEADS1, P])
        head_gain = sb("head_gain", [P, 6, DH2])
        head_sum = sb("head_sum", [P, H2])
        head_rs = sb("head_rs", [P, H2])
        pool_tmp = sb("pool_tmp", [P, 16])
        bn = sb("bn", [P, 12])
        mean_var = sb("mean_var", [P, TT, 2])
        recip = sb("recip", [P, TT])
        shares = sb("shares", [P, 5, TT * HEADS1])
        pos_f = sb("pos_f", [P, TT])
        spat_b = sb("spat_b", [P, 2, HEADS1])
        forget_b = sb("forget_b", [P, HEADS1])
        pos_i = sb("pos_i", [P, TT], I32)
        rope1 = sb("rope1", [P, 2, TT, DH1 // 2])
        rtmp = sb("rtmp", [P, 4, TT, DH1 // 2])
        fgt = sb("fgt", [P, 4, TT, HEADS1])
        tabs = sb("tabs", [P, 4, TT, DH2 // 2])
        nsa_pos = sb("nsa_pos", [P, 2, CMP_L])
        conv_cols = sb("conv_cols", [P, 3, KT])
        conv_taps = sb("conv_taps", [P, KT, CONV_W])
        kv_t = spat_w[:, 0:8, :].rearrange("p a b -> p (a b)").rearrange("p (s g n) -> p s g n", s=2, g=KVG)
        kc_t = sb("kc_t", [P, KVG, N_CMP])
        vc = sb("vc", [P, KVG, DH2])
        gates = sb("gates", [P, TT, 3 * H2])

        hid_flat = hid_t[:, :, :].rearrange("p a b -> p (a b)")
        gain_row = hid_flat[:, (FF1 // P) * SEQ:(FF1 // P) * SEQ + D]
        v_gain = hid_flat[:, (FF1 // P) * SEQ + D:(FF1 // P) * SEQ + D + 2 * MIX].rearrange("p (j m) -> p j m", j=2)

        cmp_in = hid_t[:, 8:24, :].rearrange("p a b -> p (a b)")[:, 0:2 * CMP_L * KVG * N_CMP] \
            .rearrange("p (s l g n) -> p s l g n", s=2, l=CMP_L, g=KVG)
        conv_acc = hid_t[:, 8:16, :]
        parts_o = hid_t[:, 8:16, :].rearrange("p a b -> p (a b)")[:, 0:TT * MIX] \
            .rearrange("p (t m) -> p t m", t=TT)

        def C(name):
            at, n = WHERE[name]
            return con[:, at:at + n]

        ident = C("ident")
        upto, from_on, ones = C("upto"), C("from_on"), C("ones")
        mask = {n: C(n).rearrange("p (t k) -> p t k", t=TT)
                for n in ("causal", "band", "dil4", "dil16", "cmp", "strict_add", "strict_one")}
        cos2 = C("cos2").rearrange("p (t k) -> p t k", t=TT)
        sin2 = C("sin2").rearrange("p (t k) -> p t k", t=TT)
        cmp_any = C("cmp_any")
        minus_half = C("minus_half")

        G = ctx.enter_context(nc.psum_tensor("G", [P, TT, 2, HALF], F32))
        T = [ctx.enter_context(nc.psum_tensor(f"T{b}", [P, HALF], F32)) for b in range(2)]
        S = ctx.enter_context(nc.psum_tensor("S", [P, TT, SEQ], F32))
        O = ctx.enter_context(nc.psum_tensor("O", [P, TT, SEQ], F32))
        gflat = G[:, :, :, :].rearrange("p a b c -> p (a b c)")

        unit_full = [sem(f"unit_full{s}") for s in range(RING)]
        unit_used = sem("unit_used")
        first_done = sem("first_done")
        g_taken = [sem(f"g_taken{t}") for t in range(TT)]
        t_full = sem("t_full")
        t_taken = [sem(f"t_taken{b}") for b in range(2)]
        gated_ready = sem("gated_ready")
        ssy_ready = sem("ssy_ready")
        ssx_ready = sem("ssx_ready")
        ry_ready = sem("ry_ready")
        rx_ready = sem("rx_ready")
        x_ready = sem("x_ready")
        nrm_ready = sem("nrm_ready")
        row_full = sem("row_full")
        row_used = sem("row_used")
        consts_in = sem("consts_in")
        memn_ready = sem("memn_ready")
        small_ready = sem("small_ready")
        sq_ready = sem("sq_ready")
        prep_ready = sem("prep_ready")
        s_full = sem("s_full")
        s_taken = sem("s_taken")
        mx_ready = sem("mx_ready")
        p_ready = sem("p_ready")
        o_full = sem("o_full")
        o_taken = sem("o_taken")
        gelu_ready = sem("gelu_ready")
        mix_full = sem("mix_full")
        mix_ready = sem("mix_ready")
        sum_ready = sem("sum_ready")
        arg_ready = sem("arg_ready")
        spat_in = sem("spat_in")
        spat_ready = sem("spat_ready")
        fn_in = sem("fn_in")
        fn_out = sem("fn_out")
        a_link = sem("a_link")
        v_link = sem("v_link")
        p_link = sem("p_link")
        out_done = sem("out_done")
        gains_in = sem("gains_in")

        def every(row):
            return row.partition_broadcast(P).rearrange("p a d -> p (a d)")

        loads = [(pre_cols[:, :, :], a["pre_cols"]), (mem_cols[:, :, :], a["mem_cols"]),
                 (an_cols[:, :, :], a["an_cols"]), (mn_cols[:, :, :], a["mn_cols"]),
                 (conv_cols[:, :, :], a["conv_cols"]), (conv_taps[:, :, :], a["conv_taps"]),
                 (spat_b[:, :, :], a["a_spatial_bt"]), (nsa_pos[:, :, :], a["nsa_pos"]),
                 (pos_i[:, :], a["pos"]), (forget_b[:, :], every(a["c_forget_bias"]))]
        loads += [(v_gain[:, j, :], every(a["a_v_norm_g"][j:j + 1, :])) for j in range(2)]
        loads += [(head_gain[:, j, :], every(r)) for j, r in enumerate(
            [a["nsa_q_norm_2"]] + [a["nsa_k_norm_2"][0, k:k + 1, :] for k in range(3)]
            + [a["moba_q_norm_2"], a["moba_k_norm_2"]])]
        ALL_GAINS = LOADED * len(loads)

        def chunks_of(width):
            return [(c0, min(HALF, width - c0)) for c0 in range(0, width, HALF)]

        ALL_CONSTS = 3 * LOADED
        POST = {"ffn", "mix_a", "mix_b", "mix_c"}

        def pre_gain(s):
            kind, *arg = stages[s]
            if kind == "ffn":
                return pre_cols[:, 6 * arg[0] + 4 * arg[1], :]
            if kind == "mlp":
                return mn_cols[:, arg[0], :]
            if kind in ("mix_a", "mix_b", "mix_c"):
                return pre_cols[:, 6 * arg[0] + 2, :]
            return an_cols[:, arg[0], :]

        def post_gain(s):
            kind, *arg = stages[s]
            return (arg[0], 4 * arg[1] + 1, 0.5) if kind == "ffn" else (arg[0], 3, 1.0)

        stages_x = sum(kind != "mem_kv" for kind, *_ in stages)

        block = ctx.enter_context(nc.Block())

        @block.sync
        def _(sp):
            c = Counts()

            def load(src, dst_cols, n, step=0, i=0, whole=True):
                slot = n % RING
                if n >= RING:
                    sp.wait_ge(unit_used, (n + 1 - RING) + step * i)
                for k in range(UNIT_K):
                    sp.dma_start(dst_cols(slot, k), src(k)).then_inc(unit_full[slot], LOADED)

            def plain_chunk(w, c0, width, n, step=0, i=0):
                for u in range(CHUNK_UNITS):
                    load(lambda k: w[(2 * u + k) * P:(2 * u + k + 1) * P, bass.ds(c0, width)],
                         lambda s, k: ring[:, s, k, 0:width], n + u, step, i)

            def linear(w, width):
                full, rest = width // HALF, width % HALF
                pairs = full // 2
                n = c["unit"]
                if pairs:
                    with sp.Fori(0, pairs) as i:
                        for par in range(2):
                            plain_chunk(w, i * (2 * HALF) + par * HALF, HALF, n + par * CHUNK_UNITS, RING, i)
                n += pairs * RING
                if full % 2:
                    plain_chunk(w, pairs * 2 * HALF, HALF, n)
                    n += CHUNK_UNITS
                if rest:
                    plain_chunk(w, full * HALF, rest, n)
                    n += CHUNK_UNITS
                c["unit"] = n

            def pair_chunk(w, col, n, step=0, i=0):
                v = w.rearrange("p (two f) -> p two f", two=2)
                for u in range(CHUNK_UNITS):
                    load(lambda k: v[(2 * u + k) * P:(2 * u + k + 1) * P, :, bass.ds(col, SEQ)],
                         lambda s, k: ring[:, s, k, :].rearrange("p (two f) -> p two f", two=2), n + u, step, i)

            def up(w, n_chunks, paired):
                cols = SEQ if paired else HALF
                n = c["unit"]

                def one(col, n, step=0, i=0):
                    if paired:
                        pair_chunk(w, col, n, step, i)
                    else:
                        plain_chunk(w, col, HALF, n, step, i)

                one(0, n)
                pairs = (n_chunks - 1) // 2
                with sp.Fori(0, pairs) as i:
                    for par in range(2):
                        one(i * (2 * cols) + (par + 1) * cols, n + (par + 1) * CHUNK_UNITS, RING, i)
                if (n_chunks - 1) % 2:
                    one((n_chunks - 1) * cols, n + (n_chunks - 1) * CHUNK_UNITS)
                c["unit"] = n + n_chunks * CHUNK_UNITS

            def down(w, nk):
                for k in range(nk):
                    load(lambda h: w[k * P:(k + 1) * P, h * HALF:(h + 1) * HALF],
                         lambda s, h: ring[:, s, h, :], c["unit"])
                    c.up("unit")

            def compress(w):
                for kind in range(2):
                    for u in range(4):
                        load(lambda h: w[:, kind, 8 * u + 4 * h:8 * u + 4 * h + 4, :],
                             lambda s, h: ring[:, s, h, :].rearrange("p (l e) -> p l e", e=P), c["unit"])
                        c.up("unit")

            for kind, *arg in stages:
                if kind == "mem_kv":
                    linear(a["w_mem_kv"][arg[0]], 2 * MEMW)
                elif kind == "ffn":
                    i, j = arg
                    up(a["ffn_w_gate_up"][i, j], FF1 // SEQ, True)
                    down(a["ffn_w_down"][i, j], FF1 // P)
                elif kind == "mlp":
                    up(a["mlp_w_up_2"][arg[0]], FF2 // HALF, False)
                    down(a["mlp_w_down_2"][arg[0]], FF2 // P)
                elif kind == "mix_a":
                    linear(a["a_w_in"][arg[1]], A_IN)
                    down(a["a_w_out"][arg[1]], KT)
                elif kind == "mix_b":
                    linear(a["b_w_in"][0], B_IN)
                    down(a["b_w_out"][0], B_OUT // P)
                elif kind == "mix_c":
                    linear(a["c_w_in"][0], C_IN)
                    down(a["c_w_out"][0], KT)
                elif kind == "nsa":
                    linear(a["nsa_w_in_2"][0], NSA_IN)
                    compress(a["nsa_w_cmp_l"])
                    down(a["nsa_w_out_2"][0], KT)
                elif kind == "stick":
                    linear(a["sb_w_in_2"][0], 3 * D)
                    down(a["sb_w_out_2"][0], KT)
                elif kind == "conv":
                    linear(a["conv_w_in_2"][0], 2 * D)
                    down(a["conv_w_out_2"][0], KT)
                elif kind == "moba":
                    linear(a["moba_w_in_2"][0], 3 * D)
                    down(a["moba_w_out_2"][0], KT)
            for t in range(TT):
                sp.wait_ge(x_ready, (stages_x - 1) * TT + t + 1)
                sp.dma_start(out[0, t * P:(t + 1) * P, :], x[:, t, :]).then_inc(out_done, LOADED)
            sp.wait_ge(out_done, TT * LOADED)

        def mem_heads(off, y_off):
            return [dict(q=off + h * DH1, k=("memkv", h * DH1), v=("memkv", MEMW + h * DH1), dh=DH1,
                         mask=None, y=y_off + h * DH1, scale=SCALE1) for h in range(MEM_HEADS)]

        def plan(kind):
            if kind == "mix_a":
                return mem_heads(2 * MIX, MIX)
            if kind == "mix_b":
                hs = [dict(q=h * DH1, k=("proj", MIX + h * DH1), v=("proj", 2 * MIX + h * DH1), dh=DH1,
                           mask=("band", "dil4", "dil16")[h // 4], y=h * DH1, scale=SCALE1, part=True)
                      for h in range(HEADS1)]
                return hs + mem_heads(3 * MIX, DIL_OUT)
            if kind == "mix_c":
                hs = [dict(q=h * DH1, k=("proj", MIX + h * DH1), v=("proj", 2 * MIX + h * DH1), dh=DH1,
                           mask="causal", y=h * DH1, scale=SCALE1, forget=h) for h in range(HEADS1)]
                return hs + mem_heads(3 * MIX + HEADS1, MIX)
            if kind == "moba":
                return [dict(q=h * DH2, k=("proj", D + h * DH2), v=("proj", 2 * D + h * DH2), dh=DH2,
                             mask="causal", y=h * DH2, scale=SCALE2) for h in range(H2)]
            if kind == "nsa":
                hs = []
                kvw = KVG * DH2
                for h in range(H2):
                    g = h // HPG
                    hs.append(dict(q=h * DH2, k=("cmp", g), v=("cmp", g), dh=DH2, mask="cmp", y=h * DH2,
                                   scale=SCALE2, gate=h, first=True))
                    for n, br in ((2, 1), (4, 2)):
                        hs.append(dict(q=h * DH2, k=("proj", D + n * kvw + g * DH2),
                                       v=("proj", D + (n + 1) * kvw + g * DH2), dh=DH2, mask="causal",
                                       y=h * DH2, scale=SCALE2, gate=br * H2 + h, first=False))
                return hs

        def rows_of(where, t, dh):
            buf, off = where
            return {"proj": proj, "memkv": memkv}[buf][:, t, off:off + dh]

        MIXERS = ("mix_a", "mix_b", "mix_c", "nsa", "stick", "conv", "moba")
        WIDTH = {"mix_a": A_IN, "mix_b": B_IN, "mix_c": C_IN, "nsa": NSA_IN, "stick": 3 * D,
                 "conv": 2 * D, "moba": 3 * D}
        OUT_K = {k: KT for k in MIXERS}
        OUT_K["mix_b"] = B_OUT // P

        @block.tensor
        def _(pe):
            c = Counts()
            mm = nc.tensor.matmul

            def t_open(n, step=0, i=0):
                if n >= 2:
                    pe.wait_ge(t_taken[n % 2], n // 2 + (step // 2) * i)
                return T[n % 2]

            def transposes(tiles, n, step=0, i=0):
                bank, at = t_open(n, step, i), 0
                for k, src in enumerate(tiles):
                    m = src.shape[1]
                    last = nc.tensor.transpose(bank[0:m, at:at + P], src, ident)
                    at += P
                last.then_inc(t_full, 1)

            def turn_rows(t, rows, n_tiles):
                for b in range(n_tiles // 4):
                    transposes([rows[:, t, (4 * b + j) * P:(4 * b + j + 1) * P] for j in range(4)], c["T"])
                    c.up("T")

            def copied(n):
                pe.wait_ge(t_taken[n % 2], n // 2 + 1)

            def chunk(lhs, par, width, n, g_wait, step=0, i=0, before=None):
                for t in range(TT):
                    if before:
                        before(t)
                    pe.wait_ge(g_taken[t], g_wait)
                    for u in range(CHUNK_UNITS):
                        m = n + u
                        if t == 0:
                            pe.wait_ge(unit_full[m % RING], 2 * LOADED * (m // RING + 1)
                                       + 2 * LOADED * (step // RING) * i)
                        for k in range(UNIT_K):
                            kt = UNIT_K * u + k
                            last = mm(G[:, t, par, 0:width], lhs[:, kt, t * P:(t + 1) * P],
                                      ring[:, m % RING, k, 0:width], start=(kt == 0), stop=(kt == KT - 1))
                        if t == TT - 1:
                            last.then_inc(unit_used, 1)
                    if t == 0:
                        last.then_inc(first_done, 1)

            def normed(t):
                pe.wait_ge(nrm_ready, c.up("nrm"))
                turn_rows(t, nrm, KT)
                copied(c["T"] - 2)
                copied(c["T"] - 1)

            def linear(lhs, width, before=None):
                n, g = c["unit"], c["g"]
                full, rest = width // HALF, width % HALF
                plan_ = [HALF] * full + ([rest] if rest else [])
                chunk(lhs, 0, plan_[0], n, g, before=before)
                pairs = (full - 1) // 2
                if pairs:
                    with pe.Fori(0, pairs) as i:
                        for par in (1, 0):
                            d = 1 if par == 1 else 2
                            chunk(lhs, par, HALF, n + d * CHUNK_UNITS, g + d - 1 + 2 * i, RING, i)
                for d in range(1 + 2 * pairs, len(plan_)):
                    chunk(lhs, d % 2, plan_[d], n + d * CHUNK_UNITS, g + d - 1)
                c["unit"] = n + len(plan_) * CHUNK_UNITS
                c["g"] = g + len(plan_)

            def turn_hidden(par, paired, n, step, i, g_wait):
                for t in range(TT):
                    pe.wait_ge(g_taken[t], g_wait)
                for b in range(1 if paired else 2):
                    transposes([hid[:, par, t, (2 * b + f) * P:(2 * b + f + 1) * P]
                                for f in range(2) for t in range(TT)], n + b, step, i)

            def up_down(n_chunks, paired, nk):
                n, g, tb = c["unit"], c["g"], None
                chunk(act_t, 0, HALF, n, g, before=normed)
                tb = c["T"]
                per = 1 if paired else 2
                pairs = (n_chunks - 1) // 2
                with pe.Fori(0, pairs) as i:
                    for d in (1, 2):
                        chunk(act_t, d % 2, HALF, n + d * CHUNK_UNITS, g + d - 1 + 2 * i, RING, i)
                        turn_hidden((d - 1) % 2, paired, tb + (d - 1) * per, 2 * per, i, g + d + 2 * i)
                if (n_chunks - 1) % 2:
                    d = n_chunks - 1
                    chunk(act_t, d % 2, HALF, n + d * CHUNK_UNITS, g + d - 1)
                    turn_hidden((d - 1) % 2, paired, tb + (d - 1) * per, 0, 0, g + d)
                d = n_chunks - 1
                c["unit"] = n + n_chunks * CHUNK_UNITS
                c["g"] = g + n_chunks

                def late():
                    turn_hidden(d % 2, paired, tb + d * per, 0, 0, g + n_chunks)
                c["T"] = tb + n_chunks * per
                ready = [(tb + d * per + 1 - b) // 2 for b in range(2)]
                down(hid_t, nk, late, ready)

            def down(lhs, nk, late=None, ready=None):
                n = c["unit"]
                for grp in range(0, nk, 4):
                    ks = range(grp, min(grp + 4, nk))
                    for t in range(TT):
                        if grp == 0:
                            pe.wait_ge(g_taken[t], c["g"])
                            for b in range(2):
                                v = ready[b] if ready else (c["T"] + 1 - b) // 2
                                if t == 0 or not ready:
                                    pe.wait_ge(t_taken[b], v)
                        if late and grp + 4 >= nk and t == 0:
                            for b in range(2):
                                pe.wait_ge(t_taken[b], (c["T"] + 1 - b) // 2)
                        for k in ks:
                            m = n + k
                            if t == 0:
                                pe.wait_ge(unit_full[m % RING], 2 * LOADED * (m // RING + 1))
                            for h in range(2):
                                last = mm(G[:, t, h, :], lhs[:, k, t * P:(t + 1) * P], ring[:, m % RING, h, :],
                                          start=(k == 0), stop=(k == nk - 1))
                            if t == TT - 1:
                                last.then_inc(unit_used, 1)
                        if t == 0 and ks[-1] == nk - 1:
                            last.then_inc(first_done, 1)
                    if grp == 0 and late:
                        late()
                c.up("unit", nk)
                c.up("g")

            def mixer_out(nk):
                for t in range(TT):
                    turn_rows(t, ymix, nk)
                down(hid_t, nk)

            def attention(heads):
                base = c["att"]
                n_heads = len(heads)
                turned_qk, turned_p = [], []

                def turn_qk(j):
                    h = heads[j]
                    tiles = [proj[:, t, h["q"]:h["q"] + h["dh"]] for t in range(TT)]
                    if h["k"][0] != "cmp":
                        tiles += [rows_of(h["k"], t, h["dh"]) for t in range(TT)]
                    transposes(tiles, c["T"])
                    turned_qk.append(c["T"])
                    c.up("T")

                def score(j):
                    h, b, dh = heads[j], j % 2, heads[j]["dh"]
                    copied(turned_qk[j])
                    if base + j >= 1:
                        pe.wait_ge(s_taken, base + j)
                    for t in range(TT):
                        q = qk[0:dh, b, t * P:(t + 1) * P]
                        if h["k"][0] == "cmp":
                            last = mm(S[:, t, 0:N_CMP], q, kc_t[:, h["k"][1], :], start=True, stop=True,
                                      skip_group_check=True)
                            continue
                        f = h.get("forget")
                        last = mm(S[:, t, :], q, qk[0:dh, b, TT * P:2 * TT * P], start=(t == 0),
                                  stop=(f is None), skip_group_check=True)
                        if f is not None:
                            for st in range(TT):
                                n = SEQ - st * P
                                last = mm(S[:, t, st * P:SEQ], fgt_rows[:, st, f:f + 1].to_broadcast([P, P]),
                                          upto[:, 0:n], start=False, stop=(st == TT - 1), skip_group_check=True)
                    last.then_inc(s_full, 1)

                def turn_p(j):
                    h, b = heads[j], j % 2
                    pe.wait_ge(p_ready, base + j + 1)
                    if h["k"][0] == "cmp":
                        tiles = [pr[:, b, t, 0:N_CMP] for t in range(TT)]
                    elif h["mask"]:
                        tiles = [pr[:, b, 0, 0:P], pr[:, b, 1, 0:P], pr[:, b, 1, P:SEQ]]
                    else:
                        tiles = [pr[:, b, t, kt * P:(kt + 1) * P] for kt in range(2) for t in range(TT)]
                    transposes(tiles, c["T"])
                    turned_p.append(c["T"])
                    c.up("T")

                def weigh(j):
                    h, b, dh = heads[j], j % 2, heads[j]["dh"]
                    copied(turned_p[j])
                    if base + j >= 1:
                        pe.wait_ge(o_taken, base + j)
                    for t in range(TT):
                        if h["k"][0] == "cmp":
                            last = mm(O[:, t, 0:dh], pt[0:N_CMP, b, t * P:(t + 1) * P],
                                      vc[0:N_CMP, h["v"][1], :], start=True, stop=True, skip_group_check=True)
                            continue
                        kts = [0] if h["mask"] and t == 0 else [0, 1]
                        for kt in kts:
                            at = (0, P, 2 * P)[t + kt] if h["mask"] else (kt * TT + t) * P
                            last = mm(O[:, t, 0:dh], pt[:, b, at:at + P], rows_of(h["v"], kt, dh),
                                      start=(kt == 0), stop=(kt == kts[-1]), skip_group_check=True)
                    last.then_inc(o_full, 1)

                for step in range(n_heads + 3):
                    if step < n_heads:
                        turn_qk(step)
                    if 0 <= step - 2 < n_heads:
                        turn_p(step - 2)
                    if 0 <= step - 1 < n_heads:
                        score(step - 1)
                    if 0 <= step - 3 < n_heads:
                        weigh(step - 3)
                c["att"] = base + n_heads
                pe.wait_ge(o_taken, c["att"])

            fgt_rows = fgt[:, 3, :, :]

            def prepared():
                pe.wait_ge(prep_ready, c.up("prep"))

            def mix_a():
                linear(act_t, A_IN, before=normed)
                prepared()
                for g in range(HEADS1):
                    last = mm(gflat[:, g * P:(g + 1) * P].rearrange("p (t d) -> p t d", t=TT),
                              spat_w[:, g, :], scratch_v[:, :, g * DH1:(g + 1) * DH1],
                              start=True, stop=True, skip_group_check=True)
                last.then_inc(mix_full, 1)
                attention(plan("mix_a"))
                mixer_out(KT)

            def mix_bc(kind):
                linear(act_t, WIDTH[kind], before=normed)
                prepared()
                attention(plan(kind))
                if kind == "mix_b":
                    pe.wait_ge(mix_ready, c.up("mix"))
                mixer_out(OUT_K[kind])

            def nsa():
                linear(act_t, NSA_IN, before=normed)
                prepared()
                kvw = KVG * DH2
                for s in range(2):
                    transposes([proj[:, t, D + s * kvw + g * DH2:D + s * kvw + (g + 1) * DH2]
                                for g in range(KVG) for t in range(TT)], c["T"])
                    c.up("T")
                prepared()
                n = c["unit"]
                for s in range(2):
                    for u in range(4):
                        m = n + 4 * s + u
                        pe.wait_ge(unit_full[m % RING], 2 * LOADED * (m // RING + 1))
                        for h in range(2):
                            for j in range(4):
                                l = 8 * u + 4 * h + j
                                w = ring[:, m % RING, h, j * P:(j + 1) * P]
                                if s == 0:
                                    last = mm(S[:, 0, 0:KVG * N_CMP], w,
                                              cmp_in[:, 0, l, :, :].rearrange("p g n -> p (g n)"),
                                              start=(l == 0), stop=(l == CMP_L - 1))
                                else:
                                    for g in range(KVG):
                                        last = mm(G[0:N_CMP, g, 0, 0:DH2], cmp_in[:, 1, l, g, :], w,
                                                  start=(l == 0), stop=(l == CMP_L - 1))
                        last.then_inc(unit_used, 1)
                c["unit"] = n + 8
                prepared()
                attention(plan("nsa"))
                mixer_out(KT)

            def stick():
                linear(act_t, 3 * D, before=normed)
                pe.wait_ge(g_taken[0], c["g"])
                pe.wait_ge(g_taken[1], c["g"])
                for pair in range(H2 // 2):
                    hs = [2 * pair, 2 * pair + 1]
                    for j, h in enumerate(hs):
                        transposes([proj[:, t, o + h * DH2:o + (h + 1) * DH2] for o in (0, D) for t in range(TT)],
                                   c["T"])
                        c.up("T")
                    for j, h in enumerate(hs):
                        copied(c["T"] - 2 + j)
                        c.up("att")
                        if c["att"] >= 2:
                            pe.wait_ge(s_taken, c["att"] - 1)
                        for st in range(TT):
                            last = mm(S[:, st, :], qk[:, j, (TT + st) * P:(TT + st + 1) * P], qk[:, j, 0:TT * P],
                                      start=(st == 0), stop=True, skip_group_check=True)
                        last.then_inc(s_full, 1)
                    for j, h in enumerate(hs):
                        prepared()
                        mm(G[:, j, 0, 0:SEQ], from_on, pt[:, j, 0:SEQ], start=True, stop=False)
                        mm(G[:, j, 0, 0:SEQ], ones, pt[:, j, SEQ:2 * SEQ], start=False, stop=True)
                        last = mm(G[:, j, 1, 0:SEQ], from_on, pt[:, j, SEQ:2 * SEQ], start=True, stop=True)
                        last.then_inc(mix_full, 1)
                    for j, h in enumerate(hs):
                        pe.wait_ge(p_ready, c["att"] - 1 + j)
                        if c["att"] - 2 + j >= 1:
                            pe.wait_ge(o_taken, c["att"] - 2 + j)
                        for t in range(TT):
                            for st in range(t + 1):
                                last = mm(O[:, t, 0:DH2], pr[:, j, st, t * P:(t + 1) * P],
                                          proj[:, st, 2 * D + h * DH2:2 * D + (h + 1) * DH2],
                                          start=(st == 0), stop=(st == t), skip_group_check=True)
                        last.then_inc(o_full, 1)
                pe.wait_ge(o_taken, c["att"])
                mixer_out(KT)

            def conv():
                linear(act_t, 2 * D, before=normed)
                for t in range(TT):
                    prepared()
                    turn_rows(t, ymix, KT)
                prepared()
                for t in range(TT):
                    for b in range(2):
                        transposes([conv_acc[:, 4 * b + j, t * P:(t + 1) * P] for j in range(4)], c["T"])
                        c.up("T")
                for t in range(TT):
                    pe.wait_ge(mix_ready, c.up("mix"))
                    turn_rows(t, ymix, KT)
                down(hid_t, KT)

            pe.wait_ge(consts_in, ALL_CONSTS)
            for t in range(TT):
                pe.wait_ge(nrm_ready, c.up("nrm"))
                turn_rows(t, nrm, KT)
            c["g"] = 1
            for kind, *arg in stages:
                if kind == "mem_kv":
                    pe.wait_ge(memn_ready, c.up("memn"))
                    linear(memn_t, 2 * MEMW)
                elif kind == "ffn":
                    up_down(FF1 // SEQ, True, FF1 // P)
                elif kind == "mlp":
                    up_down(FF2 // HALF, False, FF2 // P)
                elif kind == "mix_a":
                    mix_a()
                elif kind in ("mix_b", "mix_c", "moba"):
                    mix_bc(kind)
                elif kind == "nsa":
                    nsa()
                elif kind == "stick":
                    stick()
                elif kind == "conv":
                    conv()

        @block.scalar
        def _(act):
            c = Counts()
            fn = nc.scalar.activation

            def products(t):
                if t == 0:
                    act.wait_ge(first_done, c.up("chunk"))
                else:
                    act.wait_ge(unit_used, c["unit"])

            def link(ins):
                ins.then_inc(a_link, 1)
                act.wait_ge(a_link, c.up("link"))

            def t_read(n, step=0, i=0):
                act.wait_ge(t_full, n + 1 + step * i)
                return T[n % 2]

            def copy_t(dst, src, n, step=0, i=0):
                fn(dst, src, ACT.Copy).then_inc(t_taken[n % 2], 1)

            last_square = []

            def square(src, w, done_, accum):
                if last_square:
                    act.wait_ge(*last_square)
                fn(scratch[:, 0:w], src, ACT.Square, **accum).then_inc(done_, 1)
                last_square[:] = [done_, c.up(done_.name)]

            def norm_x(t, first=False):
                if not first:
                    act.wait_ge(x_ready, c.up("x"))
                square(x[:, t, :], D, ssx_ready, dict(accum_out=sums[:, 2 + t:3 + t]))
                act.wait_ge(rx_ready, c.up("rx"))
                fn(nrm[:, t, :], x[:, t, :], ACT.Copy, scale=small[:, 2 + t:3 + t]).then_inc(nrm_ready, 1)

            def residual(post, last):
                c.up("g")
                for t in range(TT):
                    if post:
                        products(t)
                        square(G[:, t, :, :].rearrange("p h n -> p (h n)"), D, ssy_ready,
                               dict(accum_out=sums[:, t:t + 1]))
                    elif t == 0:
                        c.up("chunk")
                    if not last:
                        norm_x(t)

            def up(n_chunks, paired):
                n, ch, tb = c["unit"], c["chunk"], c["T"]
                per = 1 if paired else 2
                f = ACT.Silu if paired else ACT.Relu
                w = SEQ if paired else HALF

                def gate(par, d, step=0, i=0):
                    act.wait_ge(first_done, ch + d + 1 + (step // CHUNK_UNITS) * i)
                    fn(gated[:, par, 0, 0:w], G[:, 0, par, 0:w], f).then_inc(gated_ready, 1)
                    act.wait_ge(unit_used, n + (d + 1) * CHUNK_UNITS + step * i)
                    fn(gated[:, par, 1, 0:w], G[:, 1, par, 0:w], f).then_inc(gated_ready, 1)

                def copies(d, step=0, i=0):
                    for b in range(per):
                        m = tb + d * per + b
                        bank = t_read(m, step, i)
                        at = (d * per + b) * 2 * SEQ + step * 2 * SEQ * i
                        copy_t(hid_flat[:, bass.ds(at, 2 * SEQ)], bank[:, :], m)

                gate(0, 0)
                pairs = (n_chunks - 1) // 2
                with act.Fori(0, pairs) as i:
                    for d in (1, 2):
                        gate(d % 2, d, RING, i)
                        copies(d - 1, 2 * per, i)
                if (n_chunks - 1) % 2:
                    gate((n_chunks - 1) % 2, n_chunks - 1)
                    copies(n_chunks - 2)
                copies(n_chunks - 1)
                c["unit"], c["chunk"], c["T"] = n + n_chunks * CHUNK_UNITS, ch + n_chunks, tb + n_chunks * per
                c.up("g", n_chunks)

            def linear(width):
                nch = len(chunks_of(width))
                c.up("unit", nch * CHUNK_UNITS)
                c.up("chunk", nch)
                c.up("g", nch)

            def normed():
                c.up("T", 4)

            def turn_out(nk):
                for t in range(TT):
                    for b in range(nk // 4):
                        n = c["T"]
                        bank = t_read(n)
                        copy_t(hid_t[:, 4 * b:4 * b + 4, t * P:(t + 1) * P],
                               bank[:, :].rearrange("p (k n) -> p k n", k=4), n)
                        c.up("T")
                c.up("unit", nk)

            def attention(heads):
                base = c["att"]
                n_heads = len(heads)

                def copy_qk(j):
                    h, n = heads[j], c["T"]
                    w = TT * P if h["k"][0] == "cmp" else 2 * TT * P
                    bank = t_read(n)
                    copy_t(qk[0:h["dh"], j % 2, 0:w], bank[0:h["dh"], 0:w], n)
                    c.up("T")

                def exps(j):
                    h, b = heads[j], j % 2
                    act.wait_ge(mx_ready, base + j + 1)
                    w = N_CMP if h["k"][0] == "cmp" else SEQ
                    for t in range(TT):
                        col = TT * j + t
                        last = fn(pr[:, b, t, 0:w], sc[:, b, t, 0:w], ACT.Exp, bias=mx[:, col:col + 1],
                                  accum_out=den[:, col:col + 1])
                    last.then_inc(p_ready, 1)

                def copy_p(j):
                    h, n = heads[j], c["T"]
                    bank = t_read(n)
                    r, w = (N_CMP, 2 * P) if h["k"][0] == "cmp" else (P, 3 * P if h["mask"] else 4 * P)
                    copy_t(pt[0:r, j % 2, 0:w], bank[0:r, 0:w], n)
                    c.up("T")

                for step in range(n_heads + 3):
                    if step < n_heads:
                        copy_qk(step)
                    if 0 <= step - 2 < n_heads:
                        copy_p(step - 2)
                    if 0 <= step - 1 < n_heads:
                        exps(step - 1)
                c["att"] = base + n_heads

            def squares(blocks):
                for t, c0, w in blocks:
                    if c["sum"]:
                        act.wait_ge(sum_ready, c["sum"])
                    square(proj[:, t, c0:c0 + w], w, sq_ready, {})
                    c.up("sum")

            def proj_complete():
                for t in range(TT):
                    act.wait_ge(g_taken[t], c["g"])

            def mix_a():
                normed()
                linear(A_IN)
                proj_complete()
                for t in range(TT):
                    fn(proj[:, t, 0:2 * MIX], proj[:, t, 0:2 * MIX], ACT.Gelu_apprx_tanh).then_inc(gelu_ready, 1)
                c.up("sum", TT)
                attention(plan("mix_a"))
                turn_out(KT)

            act.dma_start(con[:, :], a["consts"]).then_inc(consts_in, LOADED)
            act.dma_start(x[:, :, :], a["x"][0].rearrange("(t p) d -> p t d", p=P)).then_inc(consts_in, LOADED)
            act.dma_start(ymix[:, :, :], a["mem"][0].rearrange("(t p) d -> p t d", p=P)).then_inc(consts_in, LOADED)
            act.wait_ge(consts_in, ALL_CONSTS)
            for t in range(TT):
                square(ymix[:, t, :], D, ssy_ready, dict(accum_out=sums[:, t:t + 1]))
                act.wait_ge(ry_ready, t + 1)
                fn(nrm[:, t, :], ymix[:, t, :], ACT.Copy, scale=small[:, t:t + 1]).then_inc(nrm_ready, 1)
            for t in range(TT):
                for b in range(2):
                    n = c["T"]
                    bank = t_read(n)
                    copy_t(mem_t[:, 4 * b:4 * b + 4, t * P:(t + 1) * P], bank[:, :].rearrange("p (k n) -> p k n", k=4), n)
                    c.up("T")
            for t in range(TT):
                norm_x(t, first=True)
            c["g"] = 1
            act.wait_ge(fn_in, c.up("fn_in"))
            for j in range(2):
                fn(rope1[:, j, :, :], rtmp[:, 2 + j, :, :], ACT.Sin).then_inc(fn_out, 1)

            n_stage = len(stages)
            for s, (kind, *arg) in enumerate(stages):
                last = s == n_stage - 1
                if kind == "mem_kv":
                    linear(2 * MEMW)
                    continue
                if kind in ("ffn", "mlp"):
                    normed()
                    if kind == "ffn":
                        up(FF1 // SEQ, True)
                        c.up("unit", FF1 // P)
                    else:
                        up(FF2 // HALF, False)
                        c.up("unit", FF2 // P)
                elif kind == "mix_a":
                    mix_a()
                elif kind == "mix_b":
                    normed()
                    linear(B_IN)
                    attention(plan("mix_b"))
                    act.wait_ge(fn_in, c.up("fn_in"))
                    fn(shares[:, 0, :], den[:, 0:TT * HEADS1], ACT.Ln).then_inc(fn_out, 1)
                    act.wait_ge(fn_in, c.up("fn_in"))
                    fn(shares[:, 2, :], shares[:, 1, :], ACT.Exp).then_inc(fn_out, 1)
                    turn_out(B_OUT // P)
                elif kind == "mix_c":
                    normed()
                    linear(C_IN)
                    act.wait_ge(fn_in, c.up("fn_in"))
                    link(fn(fgt[:, 2, :, :], fgt[:, 1, :, :], ACT.Exp))
                    fn(fgt[:, 1, :, :], fgt[:, 2, :, :], ACT.Ln, bias=1.0).then_inc(fn_out, 1)
                    attention(plan("mix_c"))
                    turn_out(KT)
                elif kind == "moba":
                    normed()
                    linear(3 * D)
                    proj_complete()
                    squares([(t, c0, D) for t in range(TT) for c0 in (0, D)])
                    attention(plan("moba"))
                    turn_out(KT)
                elif kind == "nsa":
                    normed()
                    linear(NSA_IN)
                    proj_complete()
                    fn(gates[:, :, :], proj[:, :, NSA_IN - 3 * H2:NSA_IN], ACT.Sigmoid).then_inc(fn_out, 1)
                    kvw = KVG * DH2
                    squares([(t, c0, w) for t in range(TT)
                             for c0, w in ((0, D), (D, kvw), (D + 2 * kvw, kvw), (D + 4 * kvw, kvw))])
                    for s2 in range(2):
                        n = c["T"]
                        bank = t_read(n)
                        copy_t(kv_t[:, s2, :, :].rearrange("p g n -> p (g n)"), bank[:, :], n)
                        c.up("T")
                    c.up("unit", 8)
                    attention(plan("nsa"))
                    turn_out(KT)
                elif kind == "stick":
                    normed()
                    linear(3 * D)
                    for pair in range(H2 // 2):
                        for j in range(2):
                            n = c["T"]
                            bank = t_read(n)
                            copy_t(qk[:, j, :], bank[:, :], n)
                            c.up("T")
                        for j in range(2):
                            act.wait_ge(mx_ready, c.up("att"))
                            link(fn(pt[:, j, :], pt[:, j, :], ACT.Exp))
                            fn(pt[:, j, :], pt[:, j, :], ACT.Ln, bias=1.0).then_inc(fn_out, 1)
                        for j in range(2):
                            act.wait_ge(arg_ready, c.up("arg"))
                            fn(pr[:, j, :, :], pr[:, j, :, :], ACT.Exp).then_inc(p_ready, 1)
                    turn_out(KT)
                elif kind == "conv":
                    normed()
                    linear(2 * D)
                    proj_complete()
                    for t in range(TT):
                        fn(proj[:, t, D:2 * D], proj[:, t, D:2 * D], ACT.Sigmoid).then_inc(fn_out, 1)
                    c.up("sum", TT)
                    for t in range(TT):
                        for b in range(2):
                            n = c["T"]
                            bank = t_read(n)
                            copy_t(conv_in[:, 4 * b:4 * b + 4, PAD + t * P:PAD + (t + 1) * P],
                                   bank[:, :].rearrange("p (k n) -> p k n", k=4), n)
                            c.up("T")
                    for t in range(TT):
                        for b in range(2):
                            n = c["T"]
                            bank = t_read(n)
                            copy_t(nrm[:, t, b * HALF:(b + 1) * HALF], bank[:, :], n)
                            c.up("T")
                    for t in range(TT):
                        for b in range(2):
                            n = c["T"]
                            bank = t_read(n)
                            for j in range(4):
                                k = 4 * b + j
                                ins = fn(hid_t[:, k, t * P:(t + 1) * P], bank[:, j * P:(j + 1) * P], ACT.Silu,
                                         bias=conv_cols[:, 2, k:k + 1], scale=conv_cols[:, 1, k:k + 1])
                            ins.then_inc(t_taken[n % 2], 1)
                            c.up("T")
                    c.up("unit", KT)
                residual(kind in ("ffn", "mix_a", "mix_b", "mix_c"), last)

        @block.vector
        def _(dve):
            c = Counts()
            v = nc.vector

            def products(t):
                if t == 0:
                    dve.wait_ge(first_done, c.up("chunk"))
                else:
                    dve.wait_ge(unit_used, c["unit"])

            def link(ins):
                ins.then_inc(v_link, 1)
                dve.wait_ge(v_link, c.up("link"))

            def normed(s):
                cols = pre_gain(s)
                for t in range(TT):
                    for b in range(2):
                        n = c["T"]
                        dve.wait_ge(t_full, n + 1)
                        v.tensor_tensor(
                            act_t[:, 4 * b:4 * b + 4, t * P:(t + 1) * P],
                            T[n % 2][:, :].rearrange("p (k n) -> p k n", k=4),
                            cols[:, 4 * b:4 * b + 4].unsqueeze(2).to_broadcast([P, 4, P]), ALU.mult)\
                            .then_inc(t_taken[n % 2], 1)
                        c.up("T")
                    yield

            def linear(width, dst, before=None):
                plan_ = chunks_of(width)
                for c0, w in plan_:
                    c.up("unit", CHUNK_UNITS)
                    for t in range(TT):
                        if c0 == 0 and before is not None:
                            next(before)
                        products(t)
                        v.tensor_copy(dst[:, t, c0:c0 + w], G[:, t, (c0 // HALF) % 2, 0:w]).then_inc(g_taken[t], 1)
                c.up("g", len(plan_))

            def up(s, n_chunks, paired):
                n, ch = c["unit"], c["chunk"]
                w = SEQ if paired else HALF
                lo = SEQ if paired else 0
                before = normed(s)

                gr = c["gated"]

                def one(par, d, step=0, i=0):
                    for t in range(TT):
                        dve.wait_ge(gated_ready, gr + TT * d + t + 1 + (TT * step // CHUNK_UNITS) * i)
                        v.tensor_tensor(hid[:, par, t, 0:w], G[:, t, par, lo:lo + w], gated[:, par, t, 0:w],
                                        ALU.mult).then_inc(g_taken[t], 1)

                next(before)
                next(before)
                one(0, 0)
                pairs = (n_chunks - 1) // 2
                with dve.Fori(0, pairs) as i:
                    for d in (1, 2):
                        one(d % 2, d, RING, i)
                if (n_chunks - 1) % 2:
                    one((n_chunks - 1) % 2, n_chunks - 1)
                c["unit"], c["chunk"] = n + n_chunks * CHUNK_UNITS, ch + n_chunks
                c.up("T", n_chunks * (1 if paired else 2))
                c.up("gated", TT * n_chunks)
                c.up("g", n_chunks)

            def residual(s):
                post = stages[s][0] in POST
                c.up("g")
                for t in range(TT):
                    y = G[:, t, :, :].rearrange("p h n -> p (h n)")
                    if post:
                        if t == 0:
                            c.up("chunk")
                            dve.wait_ge(row_full, LOADED * c.up("row"))
                        dve.wait_ge(ry_ready, c.up("ry"))
                        factor = post_gain(s)[2]
                        v.scalar_tensor_tensor(scratch_v[:, t, :], y, small[:, t:t + 1], gain_row[:, :],
                                               ALU.mult, ALU.mult).then_inc(g_taken[t], 1)
                        dve.wait_ge(g_taken[t], c["g"])
                        v.scalar_tensor_tensor(x[:, t, :], scratch_v[:, t, :], factor, x[:, t, :],
                                               ALU.mult, ALU.add).then_inc(x_ready, 1)
                    else:
                        products(t)
                        v.tensor_tensor(x[:, t, :], y, x[:, t, :], ALU.add).then_inc(x_ready, 1)
                        dve.wait_ge(x_ready, c["x"] + 1)
                        dve.sem_inc(g_taken[t], 1)
                    c.up("x")

            def attention(heads):
                base = c["att"]
                n_heads = len(heads)

                def score(j):
                    h, b = heads[j], j % 2
                    w = N_CMP if h["k"][0] == "cmp" else SEQ
                    dve.wait_ge(s_full, base + j + 1)
                    dst, src = sc[:, b, :, 0:w], S[:, :, 0:w]
                    if h["mask"]:
                        ins = v.scalar_tensor_tensor(dst, src, h["scale"], mask[h["mask"]], ALU.mult, ALU.add)
                    else:
                        ins = v.tensor_scalar(dst, src, h["scale"], None, ALU.mult)
                    ins.then_inc(s_taken, 1)
                    dve.wait_ge(s_taken, base + j + 1)
                    v.tensor_reduce(mx[:, TT * j:TT * j + TT], dst, AX_X, ALU.max, negate=True)\
                     .then_inc(mx_ready, 1)

                def place(j):
                    h, dh = heads[j], heads[j]["dh"]
                    dve.wait_ge(o_full, base + j + 1)
                    link(v.reciprocal(recip[:, :], den[:, TT * j:TT * j + TT]))
                    if "gate" in h:
                        link(v.tensor_tensor(recip[:, :], recip[:, :], gates[:, :, h["gate"]], ALU.mult))
                        if h["first"]:
                            link(v.tensor_tensor(recip[:, :], recip[:, :], cmp_any, ALU.mult))
                    y = parts_o if h.get("part") else ymix
                    at = h["y"]
                    if h.get("first", True):
                        ins = v.tensor_tensor(y[:, :, at:at + dh], O[:, :, 0:dh],
                                              recip[:, :].unsqueeze(2).to_broadcast([P, TT, dh]), ALU.mult)
                    else:
                        for t in range(TT):
                            ins = v.scalar_tensor_tensor(y[:, t, at:at + dh], O[:, t, 0:dh], recip[:, t:t + 1],
                                                         y[:, t, at:at + dh], ALU.mult, ALU.add)
                    ins.then_inc(o_taken, 1)
                    dve.wait_ge(o_taken, base + j + 1)

                for step in range(n_heads + 3):
                    if 0 <= step - 1 < n_heads:
                        score(step - 1)
                    if 0 <= step - 3 < n_heads:
                        place(step - 3)
                c["att"] = base + n_heads
                c.up("T", 2 * n_heads)

            def rope(block_, nh, ca, sa, cb, sb_):
                half = block_.shape[3]
                x1, x2 = block_[:, :, 0, :], block_[:, :, 1, :]
                tmp = scratch_v[:, :, :].rearrange("p a b -> p (a b)")[:, 0:4 * nh * half] \
                    .rearrange("p (k h n) -> p k h n", k=4, h=nh)

                def wide(tab):
                    return tab.unsqueeze(1).to_broadcast([P, nh, half])
                v.tensor_tensor(tmp[:, 0], x1, wide(ca), ALU.mult)
                v.tensor_tensor(tmp[:, 1], x2, wide(sa), ALU.mult)
                v.tensor_tensor(tmp[:, 2], x2, wide(cb), ALU.mult)
                link(v.tensor_tensor(tmp[:, 3], x1, wide(sb_), ALU.mult))
                v.tensor_tensor(x1, tmp[:, 0], tmp[:, 1], ALU.subtract)
                link(v.tensor_tensor(x2, tmp[:, 2], tmp[:, 3], ALU.add))

            def gain_tables(g):
                def half(n):
                    return head_gain[:, g, n * 64:(n + 1) * 64].unsqueeze(1).to_broadcast([P, TT, 64])
                v.tensor_tensor(tabs[:, 0], cos2, half(0), ALU.mult)
                v.tensor_tensor(tabs[:, 1], sin2, half(1), ALU.mult)
                v.tensor_tensor(tabs[:, 2], cos2, half(1), ALU.mult)
                link(v.tensor_tensor(tabs[:, 3], sin2, half(0), ALU.mult))

            def rs_wait():
                dve.wait_ge(small_ready, c.up("small"))

            def norm_rope(blocks):
                for t, c0, w, g in blocks:
                    nh = w // DH2
                    gain_tables(g)
                    dve.wait_ge(sq_ready, c.up("sq"))
                    v.tensor_reduce(head_sum[:, 0:nh], scratch[:, 0:w].rearrange("p (h d) -> p h d", h=nh),
                                    AX_X, ALU.add).then_inc(sum_ready, 1)
                    c.up("sum")
                    rs_wait()
                    blk = proj[:, t, c0:c0 + w].rearrange("p (h d) -> p h d", h=nh)
                    link(v.tensor_tensor(blk, blk, head_rs[:, 0:nh].unsqueeze(2).to_broadcast([P, nh, DH2]),
                                         ALU.mult))
                    rope(proj[:, t, c0:c0 + w].rearrange("p (h two d) -> p h two d", h=nh, two=2), nh,
                         *[tabs[:, k, t, :] for k in range(4)])

            def done():
                dve.sem_inc(prep_ready, 1)

            def layer_norm(t, src, n, piece, dst):
                k = n // piece
                for j in range(k):
                    ins = v.bn_stats(bn[:, 6 * j:6 * j + 6], src[:, j * piece:(j + 1) * piece])
                link(ins)
                v.bn_aggr(mean_var[:, t, :], bn[:, 0:6 * k]).then_inc(sum_ready, 1)
                c.up("sum")
                rs_wait()
                return v.tensor_scalar(dst, src, mean_var[:, t, 0:1], head_rs[:, 0:1], ALU.subtract, ALU.mult)

            def turned(n_banks):
                c.up("T", n_banks)

            def mix_a(s):
                j = stages[s][2]
                linear(A_IN, proj, normed(s))
                for t in range(TT):
                    dve.wait_ge(gelu_ready, c.up("gelu"))
                    link(layer_norm(t, proj[:, t, MIX:2 * MIX], MIX, MIX // 2, scratch_v[:, t, 0:MIX]))
                    link(v.tensor_tensor(scratch_v[:, t, 0:MIX], scratch_v[:, t, 0:MIX], v_gain[:, j, :],
                                         ALU.mult))
                dve.wait_ge(spat_ready, c.up("spat"))
                done()
                dve.wait_ge(mix_full, c.up("mixf"))
                for g in range(HEADS1):
                    at = g * DH1
                    v.scalar_tensor_tensor(ymix[:, :, at:at + DH1],
                                           gflat[:, g * P:(g + 1) * P].rearrange("p (t d) -> p t d", t=TT),
                                           spat_b[:, j, g:g + 1], proj[:, :, at:at + DH1], ALU.add, ALU.mult)
                attention(plan("mix_a"))
                turned(TT * 2)

            def mix_b(s):
                linear(B_IN, proj, normed(s))
                for t in range(TT):
                    for o in (0, MIX):
                        cs, sn = rope1[:, 0, t, :], rope1[:, 1, t, :]
                        rope(proj[:, t, o:o + MIX].rearrange("p (h two d) -> p h two d", h=HEADS1, two=2),
                             HEADS1, cs, sn, cs, sn)
                done()
                attention(plan("mix_b"))
                n = TT * HEADS1 // 3
                dve.sem_inc(fn_in, 1)
                dve.wait_ge(fn_out, c.up("fn_out"))
                link(v.tensor_tensor(shares[:, 0, :], shares[:, 0, :], mx[:, 0:TT * HEADS1], ALU.subtract))
                l = [shares[:, 0, g * n:(g + 1) * n] for g in range(3)]
                top = shares[:, 3, 0:n]
                link(v.tensor_tensor(top, l[0], l[1], ALU.max))
                link(v.tensor_tensor(top, top, l[2], ALU.max))
                v.tensor_tensor(shares[:, 1, :].rearrange("p (g n) -> p g n", g=3),
                                shares[:, 0, :].rearrange("p (g n) -> p g n", g=3),
                                top.unsqueeze(1).to_broadcast([P, 3, n]), ALU.subtract).then_inc(fn_in, 1)
                dve.wait_ge(fn_out, c.up("fn_out"))
                e = [shares[:, 2, g * n:(g + 1) * n] for g in range(3)]
                link(v.tensor_tensor(top, e[0], e[1], ALU.add))
                link(v.tensor_tensor(top, top, e[2], ALU.add))
                link(v.reciprocal(top, top))
                link(v.tensor_tensor(shares[:, 4, :].rearrange("p (g n) -> p g n", g=3),
                                     shares[:, 2, :].rearrange("p (g n) -> p g n", g=3),
                                     top.unsqueeze(1).to_broadcast([P, 3, n]), ALU.mult))
                share = shares[:, 4, :].rearrange("p (h t) -> p h t", t=TT)
                for t in range(TT):
                    o = parts_o[:, t, :].rearrange("p (h d) -> p h d", h=HEADS1)
                    link(v.tensor_tensor(o, o, share[:, :, t].unsqueeze(2).to_broadcast([P, HEADS1, DH1]),
                                         ALU.mult))
                link(v.tensor_tensor(ymix[:, :, 0:DIL_OUT], parts_o[:, :, 0:DIL_OUT],
                                     parts_o[:, :, DIL_OUT:2 * DIL_OUT], ALU.add))
                v.tensor_tensor(ymix[:, :, 0:DIL_OUT], ymix[:, :, 0:DIL_OUT],
                                parts_o[:, :, 2 * DIL_OUT:3 * DIL_OUT], ALU.add).then_inc(mix_ready, 1)
                turned(TT)

            def mix_c(s):
                linear(C_IN, proj, normed(s))
                f = proj[:, :, 3 * MIX:3 * MIX + HEADS1]
                fb = forget_b[:, :].unsqueeze(1).to_broadcast([P, TT, HEADS1])
                for t in range(TT):
                    dve.wait_ge(g_taken[t], c["g"])
                link(v.tensor_tensor(fgt[:, 0], f, fb, ALU.add))
                v.scalar_tensor_tensor(fgt[:, 1], fgt[:, 0], -1.0, fgt[:, 0], ALU.mult, ALU.min).then_inc(fn_in, 1)
                dve.wait_ge(fn_out, c.up("fn_out"))
                link(v.tensor_scalar(fgt[:, 2], fgt[:, 0], -1.0 / SCALE1, 0.0, ALU.mult, ALU.max))
                link(v.scalar_tensor_tensor(fgt[:, 3], fgt[:, 1], 1.0 / SCALE1, fgt[:, 2], ALU.mult, ALU.add))
                done()
                attention(plan("mix_c"))
                turned(TT * 2)

            def moba(s):
                linear(3 * D, proj, normed(s))
                norm_rope([(t, c0, D, 4 + c0 // D) for t in range(TT) for c0 in (0, D)])
                done()
                attention(plan("moba"))
                turned(TT * 2)

            def nsa(s):
                linear(NSA_IN, proj, normed(s))
                c.up("fn_out")
                kvw = KVG * DH2
                norm_rope([(t, c0, w, g) for t in range(TT)
                           for c0, w, g in ((0, D, 0), (D, kvw, 1), (D + 2 * kvw, kvw, 2), (D + 4 * kvw, kvw, 3))])
                done()
                for s2 in range(2):
                    n = c["T"]
                    dve.wait_ge(t_taken[n % 2], n // 2 + 1)
                    c.up("T")
                for s2 in range(2):
                    for g in range(KVG):
                        seq = kv_t[:, s2, g, :].rearrange("p (m b) -> p b m", b=CMP_STRIDE)
                        for half in range(2):
                            ls = slice(half * CMP_STRIDE, (half + 1) * CMP_STRIDE)
                            ins = v.tensor_tensor(
                                cmp_in[:, s2, ls, g, :], seq[:, :, half:half + N_CMP],
                                nsa_pos[:, s2, ls].unsqueeze(2).to_broadcast([P, CMP_STRIDE, N_CMP]), ALU.add)
                link(ins)
                done()
                c.up("unit", 8)
                dve.wait_ge(unit_used, c["unit"])
                v.tensor_copy(kc_t[:, :, :].rearrange("p g n -> p (g n)"), S[:, 0, 0:KVG * N_CMP])
                link(v.tensor_copy(vc[0:N_CMP, :, :], G[0:N_CMP, :, 0, 0:DH2]))
                dve.wait_ge(fn_out, c["fn_out"])
                done()
                attention(plan("nsa"))
                turned(TT * 2)

            def stick(s):
                linear(3 * D, proj, normed(s))
                for pair in range(H2 // 2):
                    turned(2)
                    for j in range(2):
                        dve.wait_ge(s_full, c.up("att"))
                        v.scalar_tensor_tensor(sc[:, j, :, :], S[:, :, :], SCALE2, mask["strict_add"],
                                               ALU.mult, ALU.add).then_inc(s_taken, 1)
                        dve.wait_ge(s_taken, c["att"])
                        flat = sc[:, j, :, :].rearrange("p t n -> p (t n)")
                        v.scalar_tensor_tensor(pt[:, j, :], flat, -1.0, flat, ALU.mult, ALU.min)\
                         .then_inc(mx_ready, 1)
                    for j in range(2):
                        flat = sc[:, j, :, :].rearrange("p t n -> p (t n)")
                        dve.wait_ge(fn_out, c.up("fn_out"))
                        link(v.scalar_tensor_tensor(pt[:, j, :], flat, 0.0, pt[:, j, :], ALU.max, ALU.add))
                        v.tensor_tensor(pt[:, j, :], pt[:, j, :], C("strict_one"), ALU.mult)\
                         .then_inc(prep_ready, 1)
                    for j in range(2):
                        dve.wait_ge(mix_full, c.up("mixf"))
                        v.tensor_tensor(pr[:, j, :, :], sc[:, j, :, :], G[:, j, :, 0:SEQ], ALU.subtract)\
                         .then_inc(arg_ready, 1)
                    for j in range(2):
                        h = 2 * pair + j
                        dve.wait_ge(o_full, c["att"] - 1 + j)
                        v.tensor_copy(ymix[:, :, h * DH2:(h + 1) * DH2], O[:, :, 0:DH2]).then_inc(o_taken, 1)
                turned(TT * 2)

            def conv(s):
                v.memset(conv_in[:, :, 0:PAD], 0.0)
                linear(2 * D, proj, normed(s))
                for t in range(TT):
                    dve.wait_ge(fn_out, c.up("fn_out"))
                    v.tensor_tensor(ymix[:, t, :], proj[:, t, 0:D], proj[:, t, D:2 * D], ALU.mult)\
                     .then_inc(prep_ready, 1)
                for k in range(4):
                    n = c["T"]
                    dve.wait_ge(t_taken[n % 2], n // 2 + 1)
                    c.up("T")
                for k in range(KT):
                    ins = v.tensor_scalar(conv_acc[:, k, :], conv_in[:, k, 0:SEQ], conv_taps[:, k, 0:1],
                                          conv_cols[:, 0, k:k + 1], ALU.mult, ALU.add)
                link(ins)
                base = c["link"]
                with dve.Fori(0, CONV_W - 1) as i:
                    for k in range(KT):
                        ins = v.scalar_tensor_tensor(conv_acc[:, k, :], conv_in[:, k, bass.ds(i + 1, SEQ)],
                                                     conv_taps[:, k, bass.ds(i + 1, 1)], conv_acc[:, k, :],
                                                     ALU.mult, ALU.add)
                    ins.then_inc(v_link, 1)
                    dve.wait_ge(v_link, base + 1 + i)
                c["link"] = base + CONV_W - 1
                done()
                for k in range(4):
                    n = c["T"]
                    dve.wait_ge(t_taken[n % 2], n // 2 + 1)
                    c.up("T")
                for t in range(TT):
                    ins = layer_norm(t, nrm[:, t, :], D, HALF, ymix[:, t, :])
                    ins.then_inc(mix_ready, 1)
                turned(TT * 2)

            for t in range(TT):
                dve.sem_inc(g_taken[t], 1)
            c["g"] = 1
            c["ry"] = TT
            dve.wait_ge(gains_in, ALL_GAINS)
            dve.wait_ge(consts_in, ALL_CONSTS)
            link(v.tensor_copy(pos_f[:, :], pos_i[:, :]))
            for t in range(TT):
                ins = v.tensor_scalar(rtmp[:, 0, t, :], C("inv_freq"), pos_f[:, t:t + 1], None, ALU.mult)
            link(ins)
            ang = rtmp[:, 0]
            for j, quarter in ((0, 0.25), (1, 0.0)):
                k, r = rtmp[:, 1], rtmp[:, 2 + j]
                link(v.tensor_scalar(k, ang, 1.0 / TWO_PI, quarter, ALU.mult, ALU.add))
                link(v.tensor_scalar(k, k, ROUND, None, ALU.add))
                link(v.tensor_scalar(k, k, -ROUND, None, ALU.add))
                link(v.scalar_tensor_tensor(r, k, -PI_A, ang, ALU.mult, ALU.add))
                link(v.scalar_tensor_tensor(r, k, -PI_B, r, ALU.mult, ALU.add))
                link(v.scalar_tensor_tensor(r, k, -PI_C, r, ALU.mult, ALU.add))
                link(v.tensor_scalar(r, r, quarter * TWO_PI, PI_TOP, ALU.add, ALU.min))
                link(v.tensor_scalar(r, r, -PI_TOP, None, ALU.max))
            dve.sem_inc(fn_in, 1)
            dve.wait_ge(fn_out, c.up("fn_out", 2))
            c["T"] = 4

            for s, (kind, *arg) in enumerate(stages):
                if kind == "mem_kv":
                    for b in (0, 1):
                        if s == 0:
                            for n in (b, b + 2):
                                dve.wait_ge(t_taken[n % 2], n // 2 + 1)
                    v.tensor_tensor(memn_t, mem_t, mem_cols[:, arg[0], :].unsqueeze(2).to_broadcast([P, KT, SEQ]),
                                    ALU.mult).then_inc(memn_ready, 1)
                    linear(2 * MEMW, memkv)
                    continue
                if kind == "ffn":
                    up(s, FF1 // SEQ, True)
                    c.up("unit", FF1 // P)
                elif kind == "mlp":
                    up(s, FF2 // HALF, False)
                    c.up("unit", FF2 // P)
                else:
                    {"mix_a": mix_a, "mix_b": mix_b, "mix_c": mix_c, "moba": moba, "nsa": nsa,
                     "stick": stick, "conv": conv}[kind](s)
                    c.up("unit", OUT_K[kind])
                residual(s)

        @block.gpsimd
        def _(pool):
            c = Counts()
            g_ = nc.gpsimd

            last_power = []

            def rsqrt(dst, src, scale, eps, n, done_):
                if last_power:
                    pool.wait_ge(*last_power)
                g_.tensor_scalar(pool_tmp[:, 0:n], src, scale, eps, ALU.mult, ALU.add).then_inc(p_link, 1)
                pool.wait_ge(p_link, c.up("link"))
                g_.tensor_tensor(dst, pool_tmp[:, 0:n], minus_half[:, 0:n], ALU.pow).then_inc(done_, 1)
                last_power[:] = [done_, c.up(done_.name)]

            def head(n, width):
                pool.wait_ge(sum_ready, c.up("sum"))
                rsqrt(head_rs[:, 0:n], head_sum[:, 0:n], 1.0 / width, RMS_EPS, n, small_ready)

            def variance(t, eps):
                pool.wait_ge(sum_ready, c.up("sum"))
                rsqrt(head_rs[:, 0:1], mean_var[:, t, 1:2], 1.0, eps, 1, small_ready)

            def row(s):
                i, j, _ = post_gain(s)
                if c["row"]:
                    pool.wait_ge(x_ready, c["row_x"])
                pool.dma_start(gain_row[:, :], a["norm_g"][i, j:j + 1, :].partition_broadcast(P)
                               .rearrange("p a d -> p (a d)")).then_inc(row_full, LOADED)
                c.up("row")

            def spatial(j):
                pool.dma_start(spat_w[:, :, :], a["a_spatial_t"][j]).then_inc(spat_in, LOADED)
                pool.wait_ge(spat_in, LOADED * c.up("spat"))
                g_.affine_select(out=spat_w[:, :, :], in_=spat_w[:, :, :], compare_op=ALU.is_ge, fill=0.0, base=0,
                                 pattern=[[0, HEADS1], [1, P]], channel_multiplier=-1).then_inc(spat_ready, 1)

            for dst, src in loads:
                pool.dma_start(dst, src).then_inc(gains_in, LOADED)
            pool.wait_ge(consts_in, ALL_CONSTS)
            for t in range(TT):
                pool.wait_ge(ssy_ready, c.up("ssy"))
                rsqrt(small[:, t:t + 1], sums[:, t:t + 1], 1.0 / D, RMS_EPS, 1, ry_ready)
            for t in range(TT):
                pool.wait_ge(ssx_ready, c.up("ssx"))
                rsqrt(small[:, 2 + t:3 + t], sums[:, 2 + t:3 + t], 1.0 / D, RMS_EPS, 1, rx_ready)
            n_spat = 0
            seen_x = 0
            for s, (kind, *arg) in enumerate(stages):
                if kind == "mem_kv":
                    continue
                if kind in POST:
                    c["row_x"] = seen_x
                    row(s)
                if kind == "mix_a":
                    if n_spat:
                        pool.wait_ge(mix_full, n_spat)
                    spatial(arg[1])
                    n_spat += 1
                    for t in range(TT):
                        variance(t, LN_EPS)
                elif kind == "moba":
                    for _ in range(2 * TT):
                        head(H2, DH2)
                elif kind == "nsa":
                    for t in range(TT):
                        for n in (H2, KVG, KVG, KVG):
                            head(n, DH2)
                elif kind == "conv":
                    for t in range(TT):
                        variance(t, RMS_EPS)
                last = s == len(stages) - 1
                for t in range(TT):
                    if kind in POST:
                        pool.wait_ge(ssy_ready, c.up("ssy"))
                        rsqrt(small[:, t:t + 1], sums[:, t:t + 1], 1.0 / D, RMS_EPS, 1, ry_ready)
                    if not last:
                        pool.wait_ge(ssx_ready, c.up("ssx"))
                        rsqrt(small[:, 2 + t:3 + t], sums[:, 2 + t:3 + t], 1.0 / D, RMS_EPS, 1, rx_ready)
                seen_x += TT


STAGES = []
for _i, _kind in enumerate(("mix_a", "mix_b", "mix_c", "mix_a")):
    STAGES += ([("mem_kv", 0), ("ffn", 0, 0)] if _i == 0 else [("ffn", _i, 0), ("mem_kv", _i)]) \
        + [(_kind, _i, _i // 3), ("ffn", _i, 1)]
for _i, _kind in enumerate(("nsa", "stick", "conv", "moba")):
    STAGES += [(_kind, _i), ("mlp", _i)]

N_STAGES = len(STAGES)


def kernel(**inputs):
    from concourse import bacc
    from concourse.bass_utils import run_bass_kernel_spmd

    n = {k: np.asarray(v) for k, v in inputs.items()}
    raw = ("x", "mem", "norm_g", "w_mem_kv", "ffn_w_gate_up", "ffn_w_down", "a_w_in", "a_w_out", "b_w_in",
           "b_w_out", "c_w_in", "c_w_out", "c_forget_bias", "a_v_norm_g", "mlp_w_up_2", "mlp_w_down_2",
           "nsa_w_in_2", "nsa_w_out_2", "nsa_q_norm_2", "nsa_k_norm_2", "sb_w_in_2", "sb_w_out_2",
           "conv_w_in_2", "conv_w_out_2", "moba_w_in_2", "moba_w_out_2", "moba_q_norm_2", "moba_k_norm_2")
    arrays = {k: n[k] for k in raw}

    def cols(v):
        v = v.reshape(-1, KT, P)
        return v.transpose(2, 0, 1)

    arrays["consts"] = CONSTS
    arrays["pos"] = n["positions"].reshape(TT, P).T
    arrays["pre_cols"] = cols(n["norm_g"])
    arrays["mem_cols"] = cols(n["mem_norm_g"])
    arrays["an_cols"] = cols(n["attn_norm_2"])
    arrays["mn_cols"] = cols(n["mlp_norm_2"])
    arrays["conv_cols"] = np.concatenate([cols(n[k]) for k in ("conv_dw_b_2", "conv_ln_g_2", "conv_ln_b_2")], 1)
    arrays["conv_taps"] = n["conv_dw_w_2"][0].reshape(CONV_W, KT, P).transpose(2, 1, 0)
    arrays["a_spatial_t"] = n["a_spatial_w"].transpose(0, 3, 1, 2)
    arrays["a_spatial_bt"] = n["a_spatial_b"].transpose(2, 0, 1)
    arrays["nsa_pos"] = n["nsa_cmp_pos_2"][0].transpose(2, 0, 1)
    arrays["nsa_w_cmp_l"] = n["nsa_w_cmp_2"][0].transpose(2, 0, 1, 3)
    nc = bacc.Bacc("TRN2", target_bir_lowering=False, num_devices=1)
    arrays = {k: np.ascontiguousarray(v) for k, v in arrays.items()}
    a = {k: nc.dram_tensor(k, v.shape, mybir.dt.from_np(v.dtype), kind="ExternalInput").ap()
         for k, v in arrays.items()}
    out = nc.dram_tensor("out", (1, SEQ, D), F32, kind="ExternalOutput").ap()
    build(nc, a, out, STAGES[:N_STAGES])
    r = run_bass_kernel_spmd(nc, [arrays], core_ids=[0])
    return r.results[0]["out"]
```

```python
from contextlib import ExitStack

import numpy as np

import concourse.bass as bass
from concourse import mybir

ALU = mybir.AluOpType
ACT = mybir.ActivationFunctionType
F32 = mybir.dt.float32
F32R = mybir.dt.float32r
I32 = mybir.dt.int32
AX_X = mybir.AxisListType.X

P = 128
SEQ = 256
TT = SEQ // P
D = 1024
KT = D // P
DEPTH = 4
HALF = 512
RING = 8
UNIT_K = 2
CHUNK_UNITS = KT // UNIT_K
LOADED = 16

N_MEM = 256
DH1 = 64
HEADS1 = 12
MIX = HEADS1 * DH1
MEM_HEADS = 4
MEMW = MEM_HEADS * DH1
FF1 = 2816
A_IN = 2 * MIX + MEMW
B_IN = 3 * MIX + MEMW
C_IN = 3 * MIX + HEADS1 + MEMW
DIL_OUT = 4 * DH1
B_OUT = DIL_OUT + MEMW
RMS_EPS, LN_EPS = 1e-6, 1e-5
NEG = -1e30
SCALE1 = DH1 ** -0.5
WINDOW = 128

H2 = 8
DH2 = 128
FF2 = 4096
KVG = 2
HPG = H2 // KVG
CMP_L, CMP_STRIDE = 32, 16
N_CMP = (SEQ - CMP_L) // CMP_STRIDE + 1
NSA_IN = D + 6 * KVG * DH2 + 3 * H2
SCALE2 = DH2 ** -0.5
CONV_W = 31
PAD = CONV_W - 1

TWO_PI = 6.283185307179586
PI_A, PI_B = 6.28125, 0.0019350051879882812
PI_C = TWO_PI - PI_A - PI_B
PI_TOP = 3.1415925
ROUND = 12582912.0


def tables(names):
    q = np.arange(SEQ)[:, None]
    k = np.arange(SEQ)[None, :]
    s = np.arange(P)

    def additive(keep):
        m = np.where(keep, 0.0, NEG).astype(np.float32)
        return m.reshape(TT, P, -1).transpose(1, 0, 2).reshape(P, -1)

    dist = q - k
    cmp_end = np.arange(N_CMP)[None, :] * CMP_STRIDE + CMP_L - 1
    half2 = DH2 // 2
    inv2 = (np.float32(10000.0) ** (-np.arange(half2, dtype=np.float32) / np.float32(half2))).astype(np.float32)
    ang2 = (np.arange(SEQ, dtype=np.float32)[:, None] * inv2[None, :]).astype(np.float32)
    inv1 = (np.float32(10000.0) ** (-np.arange(0, DH1, 2, dtype=np.float32) / np.float32(DH1))).astype(np.float32)

    def rows(t):
        return t.astype(np.float32).reshape(TT, P, -1).transpose(1, 0, 2).reshape(P, -1)

    strict = (k > q)
    parts = [
        ("ident", np.eye(P)),
        ("upto", (s[:, None] <= np.arange(SEQ)[None, :])),
        ("from_on", (s[:, None] >= s[None, :])),
        ("ones", np.ones((P, P))),
        ("causal", additive(dist >= 0)),
        ("band", additive((dist >= 0) & (dist <= WINDOW))),
        ("dil4", additive((dist >= 0) & (dist % 4 == 0))),
        ("dil16", additive((dist >= 0) & (dist % 16 == 0))),
        ("cmp", additive(cmp_end <= q)),
        ("cmp_any", rows((q >= CMP_L - 1))),
        ("strict_add", additive(strict)),
        ("strict_one", rows(strict)),
        ("cos2", rows(np.cos(ang2.astype(np.float64)))),
        ("sin2", rows(np.sin(ang2.astype(np.float64)))),
        ("inv_freq", np.broadcast_to(inv1[None, :], (P, DH1 // 2))),
        ("minus_half", np.full((P, 16), -0.5)),
    ]
    where, at = {}, 0
    parts = [(name, a) for name, a in parts if name in names]
    for name, a in parts:
        where[name] = (at, a.shape[1])
        at += a.shape[1]
    return where, np.ascontiguousarray(np.concatenate([np.asarray(a, np.float32) for _, a in parts], 1))


WHERE, CONSTS = tables(("ident", "upto", "from_on", "ones", "causal", "cmp", "cmp_any", "inv_freq", "minus_half"))
WHERE_1, CONSTS_1 = tables(("band", "dil4", "dil16"))
WHERE_2, CONSTS_2 = tables(("strict_add", "strict_one", "cos2", "sin2"))


class Counts(dict):

    def __missing__(self, key):
        return 0

    def up(self, key, by=1):
        self[key] = self[key] + by
        return self[key]


def build(nc, a, out, stages):
    with ExitStack() as ctx:
        def sem(name):
            return ctx.enter_context(nc.semaphore(name))

        where = {}
        top = [-(-nc.sbuf_base // 32) * 32]

        def sb(name, shape, dt=F32, over=None, skip=0):
            size = int(np.prod(shape[1:])) * 4
            if over is None:
                at = top[0]
                top[0] += -(-size // 32) * 32
            else:
                at = where[over] + skip
            where[name] = at
            return nc.alloc_sbuf_tensor_at(name + "_sb", shape, dt, offset=at)

        ring = sb("ring", [P, RING, 2, HALF])
        ring_lo = sb("ring_lo", [P, RING, 2, HALF], F32R, over="ring")
        ring_hi = sb("ring_hi", [P, RING, 2, HALF], F32R)
        con = sb("con", [P, CONSTS.shape[1]])
        x = sb("x", [P, TT, D])
        nrm = sb("nrm", [P, TT, D])
        ymix = nrm
        act_hi = sb("act_hi", [P, KT, SEQ], F32R)
        act_lo = sb("act_lo", [P, KT, SEQ], F32R)
        hid_hi = sb("hid_hi", [P, 32, SEQ], F32R)
        proj = sb("proj", [P, TT, 3072])
        mem_t = sb("mem_t", [P, KT, SEQ])
        memn_hi = sb("memn_hi", [P, KT, SEQ], F32R)
        con_1 = sb("con_1", [P, CONSTS_1.shape[1]])
        memkv = sb("memkv", [P, TT, 2 * MEMW])
        work = sb("work", [P, 4, 2 * HALF])
        gated = work[:, 0:2, :].rearrange("p a (t n) -> p a t n", t=TT)
        hid = work[:, 2:4, :].rearrange("p a (t n) -> p a t n", t=TT)
        qk = work[:, 0, :].rearrange("p (b n) -> p b n", b=2)
        sc = work[:, 1, :].rearrange("p (b t n) -> p b t n", b=2, t=TT)
        pr = work[:, 2, :].rearrange("p (b t n) -> p b t n", b=2, t=TT)
        pt = work[:, 3, :].rearrange("p (b n) -> p b n", b=2)
        scratch_v = work[:, 2:4, :]
        memn_lo = sb("memn_lo", [P, KT, SEQ], F32R, over="work")
        conv_out = work[:, 0:2, :].rearrange("p a (k n) -> p (a k) n", n=SEQ)
        hid_lo = sb("hid_lo", [P, 32, SEQ], F32R, over="proj")
        conv_in = sb("conv_in", [P, KT, PAD + SEQ], over="mem_t")
        LATE = 2048
        con_2 = sb("con_2", [P, CONSTS_2.shape[1]], over="memn_hi", skip=LATE)
        head_gain = sb("head_gain", [P, 6, DH2], over="con_2", skip=4 * CONSTS_2.shape[1])
        tabs = sb("tabs", [P, 4, TT, DH2 // 2], over="head_gain", skip=4 * 6 * DH2)
        TILE = 4 * SEQ
        gain_row = sb("gain_row", [P, D], over="hid_hi", skip=FF1 // P * TILE)
        v_gain = sb("v_gain", [P, 2, MIX], over="gain_row", skip=4 * D)
        spat_w = sb("spat_w", [P, HEADS1, P], over="hid_hi", skip=8 * TILE)
        parts_o = sb("parts_o", [P, TT, MIX], over="hid_hi", skip=8 * TILE)
        cmp_in = sb("cmp_in", [P, 2, CMP_L, KVG, N_CMP], over="hid_hi", skip=8 * TILE)
        conv_acc = sb("conv_acc", [P, KT, SEQ], over="hid_hi", skip=8 * TILE)
        kv_t = sb("kv_t", [P, 2, KVG, SEQ], over="act_hi")
        pre_cols = sb("pre_cols", [P, 6 * DEPTH, KT])
        mem_cols = sb("mem_cols", [P, DEPTH, KT])
        an_cols = sb("an_cols", [P, DEPTH, KT])
        mn_cols = sb("mn_cols", [P, DEPTH, KT])
        small = sb("small", [P, 64])
        sums = sb("sums", [P, 64])
        den = sb("den", [P, 64])
        mx = sb("mx", [P, 64])
        head_sum = sb("head_sum", [P, H2])
        head_rs = sb("head_rs", [P, H2])
        pool_tmp = sb("pool_tmp", [P, 16])
        bn = sb("bn", [P, 12])
        mean_var = sb("mean_var", [P, TT, 2])
        recip = sb("recip", [P, TT])
        shares = sb("shares", [P, 5, TT * HEADS1])
        pos_f = sb("pos_f", [P, TT])
        spat_b = sb("spat_b", [P, 2, HEADS1])
        forget_b = sb("forget_b", [P, HEADS1])
        pos_i = sb("pos_i", [P, TT], I32)
        rope1 = sb("rope1", [P, 2, TT, DH1 // 2])
        rtmp = sb("rtmp", [P, 4, TT, DH1 // 2])
        fgt = sb("fgt", [P, 4, TT, HEADS1])
        nsa_pos = sb("nsa_pos", [P, 2, CMP_L])
        conv_cols = sb("conv_cols", [P, 3, KT])
        conv_taps = sb("conv_taps", [P, KT, CONV_W])
        kc_t = sb("kc_t", [P, KVG, N_CMP])
        vc = sb("vc", [P, KVG, DH2])
        gates = sb("gates", [P, TT, 3 * H2])

        def C(name):
            for t, w in ((con, WHERE), (con_1, WHERE_1), (con_2, WHERE_2)):
                if name in w:
                    at, n = w[name]
                    return t[:, at:at + n]

        ident = C("ident")
        upto, from_on, ones = C("upto"), C("from_on"), C("ones")
        mask = {n: C(n).rearrange("p (t k) -> p t k", t=TT)
                for n in ("causal", "band", "dil4", "dil16", "cmp", "strict_add", "strict_one")}
        cos2 = C("cos2").rearrange("p (t k) -> p t k", t=TT)
        sin2 = C("sin2").rearrange("p (t k) -> p t k", t=TT)
        cmp_any = C("cmp_any")
        minus_half = C("minus_half")

        G = ctx.enter_context(nc.psum_tensor("G", [P, TT, 2, HALF], F32))
        T = [ctx.enter_context(nc.psum_tensor(f"T{b}", [P, HALF], F32)) for b in range(2)]
        S = ctx.enter_context(nc.psum_tensor("S", [P, TT, SEQ], F32))
        O = ctx.enter_context(nc.psum_tensor("O", [P, TT, SEQ], F32))
        gflat = G[:, :, :, :].rearrange("p a b c -> p (a b c)")

        unit_full = [sem(f"unit_full{s}") for s in range(RING)]
        hi_ready = sem("hi_ready")
        lo_ready = sem("lo_ready")
        act_hi_in = sem("act_hi_in")
        turn_hi = sem("turn_hi")
        unit_used = sem("unit_used")
        first_done = sem("first_done")
        g_taken = [sem(f"g_taken{t}") for t in range(TT)]
        t_full = sem("t_full")
        t_taken = [sem(f"t_taken{b}") for b in range(2)]
        gated_ready = sem("gated_ready")
        ssy_ready = sem("ssy_ready")
        ssx_ready = sem("ssx_ready")
        ry_ready = sem("ry_ready")
        rx_ready = sem("rx_ready")
        x_ready = sem("x_ready")
        nrm_ready = sem("nrm_ready")
        row_full = sem("row_full")
        row_used = sem("row_used")
        consts_in = sem("consts_in")
        memn_ready = sem("memn_ready")
        small_ready = sem("small_ready")
        sq_ready = sem("sq_ready")
        prep_ready = sem("prep_ready")
        s_full = sem("s_full")
        s_taken = sem("s_taken")
        mx_ready = sem("mx_ready")
        p_ready = sem("p_ready")
        o_full = sem("o_full")
        o_taken = sem("o_taken")
        gelu_ready = sem("gelu_ready")
        mix_full = sem("mix_full")
        mix_ready = sem("mix_ready")
        sum_ready = sem("sum_ready")
        arg_ready = sem("arg_ready")
        spat_in = sem("spat_in")
        spat_ready = sem("spat_ready")
        fn_in = sem("fn_in")
        fn_out = sem("fn_out")
        a_link = sem("a_link")
        v_link = sem("v_link")
        p_link = sem("p_link")
        out_done = sem("out_done")
        early_done = sem("early_done")
        late_in = sem("late_in")
        gains_in = sem("gains_in")

        def every(row):
            return row.partition_broadcast(P).rearrange("p a d -> p (a d)")

        loads = [(pre_cols[:, :, :], a["pre_cols"]), (mem_cols[:, :, :], a["mem_cols"]),
                 (an_cols[:, :, :], a["an_cols"]), (mn_cols[:, :, :], a["mn_cols"]),
                 (conv_cols[:, :, :], a["conv_cols"]), (conv_taps[:, :, :], a["conv_taps"]),
                 (spat_b[:, :, :], a["a_spatial_bt"]), (nsa_pos[:, :, :], a["nsa_pos"]),
                 (con_1[:, :], a["consts_1"]), (pos_i[:, :], a["pos"]), (forget_b[:, :], every(a["c_forget_bias"]))]
        loads += [(v_gain[:, j, :], every(a["a_v_norm_g"][j:j + 1, :])) for j in range(2)]
        late_loads = [(con_2[:, :], a["consts_2"])]
        late_loads += [(head_gain[:, j, :], every(r)) for j, r in enumerate(
            [a["nsa_q_norm_2"]] + [a["nsa_k_norm_2"][0, k:k + 1, :] for k in range(3)]
            + [a["moba_q_norm_2"], a["moba_k_norm_2"]])]
        ALL_GAINS = LOADED * len(loads)

        def chunks_of(width):
            return [(c0, min(HALF, width - c0)) for c0 in range(0, width, HALF)]

        ALL_CONSTS = 3 * LOADED
        MIXERS = ("mix_a", "mix_b", "mix_c", "nsa", "stick", "conv", "moba")
        WIDTH = {"mix_a": A_IN, "mix_b": B_IN, "mix_c": C_IN, "nsa": NSA_IN, "stick": 3 * D,
                 "conv": 2 * D, "moba": 3 * D}
        OUT_K = {k: KT for k in MIXERS}
        OUT_K["mix_b"] = B_OUT // P

        unit_cols = []
        for kind, *arg in stages:
            if kind in ("ffn", "mlp"):
                n_chunks, nk = (FF1 // SEQ, FF1 // P) if kind == "ffn" else (FF2 // HALF, FF2 // P)
                unit_cols += [HALF] * (CHUNK_UNITS * n_chunks + nk)
                continue
            for _, w in chunks_of(2 * MEMW if kind == "mem_kv" else WIDTH[kind]):
                unit_cols += [w] * CHUNK_UNITS
            if kind == "nsa":
                unit_cols += [0] * 8
            if kind != "mem_kv":
                unit_cols += [HALF] * OUT_K[kind]
        split_no = [0]
        for w in unit_cols:
            split_no.append(split_no[-1] + (w > 0))
        first_late = min([s for s, (kind, *_) in enumerate(stages) if kind in ("nsa", "stick", "conv", "moba", "mlp")]
                         + [len(stages)])

        def split_ahead(engine, c, one, limit):
            limit = min(limit, len(unit_cols))
            rounds = (limit - c["split"]) // RING
            if rounds >= 2 and set(unit_cols[c["split"]:c["split"] + rounds * RING]) == {HALF}:
                with engine.Fori(0, rounds) as i:
                    for j in range(RING):
                        one(c["split"] + j, RING, i)
                c.up("split", rounds * RING)
            while c["split"] < limit:
                if unit_cols[c["split"]]:
                    one(c["split"])
                c.up("split")

        def last_group(nk):
            return nk % CHUNK_UNITS or CHUNK_UNITS
        POST = {"ffn", "mix_a", "mix_b", "mix_c"}

        def pre_gain(s):
            kind, *arg = stages[s]
            if kind == "ffn":
                return pre_cols[:, 6 * arg[0] + 4 * arg[1], :]
            if kind == "mlp":
                return mn_cols[:, arg[0], :]
            if kind in ("mix_a", "mix_b", "mix_c"):
                return pre_cols[:, 6 * arg[0] + 2, :]
            return an_cols[:, arg[0], :]

        def post_gain(s):
            kind, *arg = stages[s]
            return (arg[0], 4 * arg[1] + 1, 0.5) if kind == "ffn" else (arg[0], 3, 1.0)

        stages_x = sum(kind != "mem_kv" for kind, *_ in stages)

        block = ctx.enter_context(nc.Block())

        @block.sync
        def _(sp):
            c = Counts()

            def load(src, dst_cols, n, step=0, i=0, whole=True):
                slot = n % RING
                if n >= RING:
                    sp.wait_ge(unit_used, (n + 1 - RING) + step * i)
                for k in range(UNIT_K):
                    sp.dma_start(dst_cols(slot, k), src(k)).then_inc(unit_full[slot], LOADED)

            def plain_chunk(w, c0, width, n, step=0, i=0):
                for u in range(CHUNK_UNITS):
                    load(lambda k: w[(2 * u + k) * P:(2 * u + k + 1) * P, bass.ds(c0, width)],
                         lambda s, k: ring[:, s, k, 0:width], n + u, step, i)

            def linear(w, width):
                full, rest = width // HALF, width % HALF
                pairs = full // 2
                n = c["unit"]
                if pairs:
                    with sp.Fori(0, pairs) as i:
                        for par in range(2):
                            plain_chunk(w, i * (2 * HALF) + par * HALF, HALF, n + par * CHUNK_UNITS, RING, i)
                n += pairs * RING
                if full % 2:
                    plain_chunk(w, pairs * 2 * HALF, HALF, n)
                    n += CHUNK_UNITS
                if rest:
                    plain_chunk(w, full * HALF, rest, n)
                    n += CHUNK_UNITS
                c["unit"] = n

            def pair_chunk(w, col, n, step=0, i=0):
                v = w.rearrange("p (two f) -> p two f", two=2)
                for u in range(CHUNK_UNITS):
                    load(lambda k: v[(2 * u + k) * P:(2 * u + k + 1) * P, :, bass.ds(col, SEQ)],
                         lambda s, k: ring[:, s, k, :].rearrange("p (two f) -> p two f", two=2), n + u, step, i)

            def up(w, n_chunks, paired):
                cols = SEQ if paired else HALF
                n = c["unit"]

                def one(col, n, step=0, i=0):
                    if paired:
                        pair_chunk(w, col, n, step, i)
                    else:
                        plain_chunk(w, col, HALF, n, step, i)

                one(0, n)
                pairs = (n_chunks - 1) // 2
                with sp.Fori(0, pairs) as i:
                    for par in range(2):
                        one(i * (2 * cols) + (par + 1) * cols, n + (par + 1) * CHUNK_UNITS, RING, i)
                if (n_chunks - 1) % 2:
                    one((n_chunks - 1) * cols, n + (n_chunks - 1) * CHUNK_UNITS)
                c["unit"] = n + n_chunks * CHUNK_UNITS

            def down(w, nk):
                for k in range(nk):
                    load(lambda h: w[k * P:(k + 1) * P, h * HALF:(h + 1) * HALF],
                         lambda s, h: ring[:, s, h, :], c["unit"])
                    c.up("unit")

            def compress(w):
                for kind in range(2):
                    for u in range(4):
                        load(lambda h: w[:, kind, 8 * u + 4 * h:8 * u + 4 * h + 4, :],
                             lambda s, h: ring[:, s, h, :].rearrange("p (l e) -> p l e", e=P), c["unit"])
                        c.up("unit")

            for kind, *arg in stages:
                if kind == "mem_kv":
                    linear(a["w_mem_kv"][arg[0]], 2 * MEMW)
                elif kind == "ffn":
                    i, j = arg
                    up(a["ffn_w_gate_up"][i, j], FF1 // SEQ, True)
                    down(a["ffn_w_down"][i, j], FF1 // P)
                elif kind == "mlp":
                    up(a["mlp_w_up_2"][arg[0]], FF2 // HALF, False)
                    down(a["mlp_w_down_2"][arg[0]], FF2 // P)
                elif kind == "mix_a":
                    linear(a["a_w_in"][arg[1]], A_IN)
                    down(a["a_w_out"][arg[1]], KT)
                elif kind == "mix_b":
                    linear(a["b_w_in"][0], B_IN)
                    down(a["b_w_out"][0], B_OUT // P)
                elif kind == "mix_c":
                    linear(a["c_w_in"][0], C_IN)
                    down(a["c_w_out"][0], KT)
                elif kind == "nsa":
                    linear(a["nsa_w_in_2"][0], NSA_IN)
                    compress(a["nsa_w_cmp_l"])
                    down(a["nsa_w_out_2"][0], KT)
                elif kind == "stick":
                    linear(a["sb_w_in_2"][0], 3 * D)
                    down(a["sb_w_out_2"][0], KT)
                elif kind == "conv":
                    linear(a["conv_w_in_2"][0], 2 * D)
                    down(a["conv_w_out_2"][0], KT)
                elif kind == "moba":
                    linear(a["moba_w_in_2"][0], 3 * D)
                    down(a["moba_w_out_2"][0], KT)
            for t in range(TT):
                sp.wait_ge(x_ready, (stages_x - 1) * TT + t + 1)
                sp.dma_start(out[0, t * P:(t + 1) * P, :], x[:, t, :]).then_inc(out_done, LOADED)
            sp.wait_ge(out_done, TT * LOADED)

        def mem_heads(off, y_off):
            return [dict(q=off + h * DH1, k=("memkv", h * DH1), v=("memkv", MEMW + h * DH1), dh=DH1,
                         mask=None, y=y_off + h * DH1, scale=SCALE1) for h in range(MEM_HEADS)]

        def plan(kind):
            if kind == "mix_a":
                return mem_heads(2 * MIX, MIX)
            if kind == "mix_b":
                hs = [dict(q=h * DH1, k=("proj", MIX + h * DH1), v=("proj", 2 * MIX + h * DH1), dh=DH1,
                           mask=("band", "dil4", "dil16")[h // 4], y=h * DH1, scale=SCALE1, part=True)
                      for h in range(HEADS1)]
                return hs + mem_heads(3 * MIX, DIL_OUT)
            if kind == "mix_c":
                hs = [dict(q=h * DH1, k=("proj", MIX + h * DH1), v=("proj", 2 * MIX + h * DH1), dh=DH1,
                           mask="causal", y=h * DH1, scale=SCALE1, forget=h) for h in range(HEADS1)]
                return hs + mem_heads(3 * MIX + HEADS1, MIX)
            if kind == "moba":
                return [dict(q=h * DH2, k=("proj", D + h * DH2), v=("proj", 2 * D + h * DH2), dh=DH2,
                             mask="causal", y=h * DH2, scale=SCALE2) for h in range(H2)]
            if kind == "nsa":
                hs = []
                kvw = KVG * DH2
                for h in range(H2):
                    g = h // HPG
                    hs.append(dict(q=h * DH2, k=("cmp", g), v=("cmp", g), dh=DH2, mask="cmp", y=h * DH2,
                                   scale=SCALE2, gate=h, first=True))
                    for n, br in ((2, 1), (4, 2)):
                        hs.append(dict(q=h * DH2, k=("proj", D + n * kvw + g * DH2),
                                       v=("proj", D + (n + 1) * kvw + g * DH2), dh=DH2, mask="causal",
                                       y=h * DH2, scale=SCALE2, gate=br * H2 + h, first=False))
                return hs

        def rows_of(where, t, dh):
            buf, off = where
            return {"proj": proj, "memkv": memkv}[buf][:, t, off:off + dh]

        @block.tensor
        def _(pe):
            c = Counts()
            mm = nc.tensor.matmul

            def t_open(n, step=0, i=0):
                if n >= 2:
                    pe.wait_ge(t_taken[n % 2], n // 2 + (step // 2) * i)
                return T[n % 2]

            def transposes(tiles, n, step=0, i=0):
                bank, at = t_open(n, step, i), 0
                for k, src in enumerate(tiles):
                    m = src.shape[1]
                    last = nc.tensor.transpose(bank[0:m, at:at + P], src, ident)
                    at += P
                last.then_inc(t_full, 1)

            def turn_rows(t, rows, n_tiles):
                for b in range(n_tiles // 4):
                    transposes([rows[:, t, (4 * b + j) * P:(4 * b + j + 1) * P] for j in range(4)], c["T"])
                    c.up("T")

            def copied(n):
                pe.wait_ge(t_taken[n % 2], n // 2 + 1)

            def unit_split(m, step=0, i=0):
                pe.wait_ge(lo_ready, split_no[m] + 1 + step * i)

            ACT_PAIR, MEM_PAIR, HID_PAIR = (act_hi, act_lo), (memn_hi, memn_lo), (hid_hi, hid_lo)

            def hi_products(dst, lhs, kt, ts, slot, k, w, start):
                mm(dst, lhs[0][:, kt, ts], ring_hi[:, slot, k, 0:w], start=start, stop=False)
                mm(dst, lhs[0][:, kt, ts], ring_lo[:, slot, k, 0:w], start=False, stop=False)

            def lo_product(dst, lhs, kt, ts, slot, k, w, stop):
                return mm(dst, lhs[1][:, kt, ts], ring_hi[:, slot, k, 0:w], start=False, stop=stop)

            def chunk(lhs, par, width, n, g_wait, step=0, i=0, before=None):
                for t in range(TT):
                    ts, dst = slice(t * P, (t + 1) * P), G[:, t, par, 0:width]
                    lo_later = before and t == 0
                    if before:
                        before(t)
                    pe.wait_ge(g_taken[t], g_wait)
                    for u in range(CHUNK_UNITS):
                        slot = (n + u) % RING
                        if t == 0:
                            unit_split(n + u, step, i)
                        for k in range(UNIT_K):
                            kt = UNIT_K * u + k
                            hi_products(dst, lhs, kt, ts, slot, k, width, kt == 0)
                            if not lo_later:
                                last = lo_product(dst, lhs, kt, ts, slot, k, width, kt == KT - 1)
                        if t == TT - 1:
                            last.then_inc(unit_used, 1)
                    if lo_later:
                        copied(c["T"] - 2)
                        copied(c["T"] - 1)
                        for kt in range(KT):
                            last = lo_product(dst, lhs, kt, ts, (n + kt // UNIT_K) % RING, kt % UNIT_K, width,
                                              kt == KT - 1)
                    if t == 0:
                        last.then_inc(first_done, 1)

            def normed(t):
                pe.wait_ge(nrm_ready, c.up("nrm"))
                turn_rows(t, nrm, KT)
                pe.wait_ge(act_hi_in, c.up("act_hi", 2))
                if t:
                    copied(c["T"] - 2)
                    copied(c["T"] - 1)

            def linear(lhs, width, before=None):
                n, g = c["unit"], c["g"]
                full, rest = width // HALF, width % HALF
                plan_ = [HALF] * full + ([rest] if rest else [])
                chunk(lhs, 0, plan_[0], n, g, before=before)
                pairs = (full - 1) // 2
                if pairs:
                    with pe.Fori(0, pairs) as i:
                        for par in (1, 0):
                            d = 1 if par == 1 else 2
                            chunk(lhs, par, HALF, n + d * CHUNK_UNITS, g + d - 1 + 2 * i, RING, i)
                for d in range(1 + 2 * pairs, len(plan_)):
                    chunk(lhs, d % 2, plan_[d], n + d * CHUNK_UNITS, g + d - 1)
                c["unit"] = n + len(plan_) * CHUNK_UNITS
                c["g"] = g + len(plan_)

            def turn_hidden(par, paired, n, step, i, g_wait):
                for t in range(TT):
                    pe.wait_ge(g_taken[t], g_wait)
                for b in range(1 if paired else 2):
                    transposes([hid[:, par, t, (2 * b + f) * P:(2 * b + f + 1) * P]
                                for f in range(2) for t in range(TT)], n + b, step, i)

            def up_down(n_chunks, paired, nk):
                n, g, tb = c["unit"], c["g"], None
                chunk(ACT_PAIR, 0, HALF, n, g, before=normed)
                tb = c["T"]
                per = 1 if paired else 2
                pairs = (n_chunks - 1) // 2
                with pe.Fori(0, pairs) as i:
                    for d in (1, 2):
                        chunk(ACT_PAIR, d % 2, HALF, n + d * CHUNK_UNITS, g + d - 1 + 2 * i, RING, i)
                        turn_hidden((d - 1) % 2, paired, tb + (d - 1) * per, 2 * per, i, g + d + 2 * i)
                if (n_chunks - 1) % 2:
                    d = n_chunks - 1
                    chunk(ACT_PAIR, d % 2, HALF, n + d * CHUNK_UNITS, g + d - 1)
                    turn_hidden((d - 1) % 2, paired, tb + (d - 1) * per, 0, 0, g + d)
                d = n_chunks - 1
                c["unit"] = n + n_chunks * CHUNK_UNITS
                c["g"] = g + n_chunks

                def late():
                    turn_hidden(d % 2, paired, tb + d * per, 0, 0, g + n_chunks)
                c["T"] = tb + n_chunks * per
                ready = [(tb + d * per + 1 - b) // 2 for b in range(2)]
                down(HID_PAIR, nk, late, ready)

            def down(lhs, nk, late=None, ready=None):
                n = c["unit"]
                for grp in range(0, nk, 4):
                    ks = range(grp, min(grp + 4, nk))
                    for t in range(TT):
                        if grp == 0:
                            pe.wait_ge(g_taken[t], c["g"])
                            for b in range(2):
                                v = ready[b] if ready else (c["T"] + 1 - b) // 2
                                if t == 0 or not ready:
                                    pe.wait_ge(t_taken[b], v)
                        if late and grp + 4 >= nk and t == 0:
                            for b in range(2):
                                pe.wait_ge(t_taken[b], (c["T"] + 1 - b) // 2)
                        for k in ks:
                            m = n + k
                            ts = slice(t * P, (t + 1) * P)
                            if t == 0:
                                unit_split(m)
                            for h in range(2):
                                hi_products(G[:, t, h, :], lhs, k, ts, m % RING, h, HALF, k == 0)
                                last = lo_product(G[:, t, h, :], lhs, k, ts, m % RING, h, HALF, k == nk - 1)
                            if t == TT - 1:
                                last.then_inc(unit_used, 1)
                        if t == 0 and ks[-1] == nk - 1:
                            last.then_inc(first_done, 1)
                    if grp == 0 and late:
                        late()
                c.up("unit", nk)
                c.up("g")

            def mixer_out(nk):
                for t in range(TT):
                    turn_rows(t, ymix, nk)
                down(HID_PAIR, nk)

            def attention(heads):
                base = c["att"]
                n_heads = len(heads)
                turned_qk, turned_p = [], []

                def turn_qk(j):
                    h = heads[j]
                    tiles = [proj[:, t, h["q"]:h["q"] + h["dh"]] for t in range(TT)]
                    if h["k"][0] != "cmp":
                        tiles += [rows_of(h["k"], t, h["dh"]) for t in range(TT)]
                    transposes(tiles, c["T"])
                    turned_qk.append(c["T"])
                    c.up("T")

                def score(j):
                    h, b, dh = heads[j], j % 2, heads[j]["dh"]
                    copied(turned_qk[j])
                    if base + j >= 1:
                        pe.wait_ge(s_taken, base + j)
                    for t in range(TT):
                        q = qk[0:dh, b, t * P:(t + 1) * P]
                        if h["k"][0] == "cmp":
                            last = mm(S[:, t, 0:N_CMP], q, kc_t[:, h["k"][1], :], start=True, stop=True,
                                      skip_group_check=True)
                            continue
                        f = h.get("forget")
                        last = mm(S[:, t, :], q, qk[0:dh, b, TT * P:2 * TT * P], start=(t == 0),
                                  stop=(f is None), skip_group_check=True)
                        if f is not None:
                            for st in range(TT):
                                n = SEQ - st * P
                                last = mm(S[:, t, st * P:SEQ], fgt_rows[:, st, f:f + 1].to_broadcast([P, P]),
                                          upto[:, 0:n], start=False, stop=(st == TT - 1), skip_group_check=True)
                    last.then_inc(s_full, 1)

                def turn_p(j):
                    h, b = heads[j], j % 2
                    pe.wait_ge(p_ready, base + j + 1)
                    if h["k"][0] == "cmp":
                        tiles = [pr[:, b, t, 0:N_CMP] for t in range(TT)]
                    elif h["mask"]:
                        tiles = [pr[:, b, 0, 0:P], pr[:, b, 1, 0:P], pr[:, b, 1, P:SEQ]]
                    else:
                        tiles = [pr[:, b, t, kt * P:(kt + 1) * P] for kt in range(2) for t in range(TT)]
                    transposes(tiles, c["T"])
                    turned_p.append(c["T"])
                    c.up("T")

                def weigh(j):
                    h, b, dh = heads[j], j % 2, heads[j]["dh"]
                    copied(turned_p[j])
                    if base + j >= 1:
                        pe.wait_ge(o_taken, base + j)
                    for t in range(TT):
                        if h["k"][0] == "cmp":
                            last = mm(O[:, t, 0:dh], pt[0:N_CMP, b, t * P:(t + 1) * P],
                                      vc[0:N_CMP, h["v"][1], :], start=True, stop=True, skip_group_check=True)
                            continue
                        kts = [0] if h["mask"] and t == 0 else [0, 1]
                        for kt in kts:
                            at = (0, P, 2 * P)[t + kt] if h["mask"] else (kt * TT + t) * P
                            last = mm(O[:, t, 0:dh], pt[:, b, at:at + P], rows_of(h["v"], kt, dh),
                                      start=(kt == 0), stop=(kt == kts[-1]), skip_group_check=True)
                    last.then_inc(o_full, 1)

                for step in range(n_heads + 3):
                    if step < n_heads:
                        turn_qk(step)
                    if 0 <= step - 2 < n_heads:
                        turn_p(step - 2)
                    if 0 <= step - 1 < n_heads:
                        score(step - 1)
                    if 0 <= step - 3 < n_heads:
                        weigh(step - 3)
                c["att"] = base + n_heads
                pe.wait_ge(o_taken, c["att"])

            fgt_rows = fgt[:, 3, :, :]

            def prepared():
                pe.wait_ge(prep_ready, c.up("prep"))

            def mix_a():
                linear(ACT_PAIR, A_IN, before=normed)
                prepared()
                for g in range(HEADS1):
                    last = mm(gflat[:, g * P:(g + 1) * P].rearrange("p (t d) -> p t d", t=TT),
                              spat_w[:, g, :], scratch_v[:, :, g * DH1:(g + 1) * DH1],
                              start=True, stop=True, skip_group_check=True)
                last.then_inc(mix_full, 1)
                attention(plan("mix_a"))
                mixer_out(KT)

            def mix_bc(kind):
                linear(ACT_PAIR, WIDTH[kind], before=normed)
                prepared()
                attention(plan(kind))
                if kind == "mix_b":
                    pe.wait_ge(mix_ready, c.up("mix"))
                mixer_out(OUT_K[kind])

            def nsa():
                linear(ACT_PAIR, NSA_IN, before=normed)
                prepared()
                kvw = KVG * DH2
                for s in range(2):
                    transposes([proj[:, t, D + s * kvw + g * DH2:D + s * kvw + (g + 1) * DH2]
                                for g in range(KVG) for t in range(TT)], c["T"])
                    c.up("T")
                prepared()
                n = c["unit"]
                for s in range(2):
                    for u in range(4):
                        m = n + 4 * s + u
                        pe.wait_ge(unit_full[m % RING], 2 * LOADED * (m // RING + 1))
                        for h in range(2):
                            for j in range(4):
                                l = 8 * u + 4 * h + j
                                w = ring[:, m % RING, h, j * P:(j + 1) * P]
                                if s == 0:
                                    last = mm(S[:, 0, 0:KVG * N_CMP], w,
                                              cmp_in[:, 0, l, :, :].rearrange("p g n -> p (g n)"),
                                              start=(l == 0), stop=(l == CMP_L - 1))
                                else:
                                    for g in range(KVG):
                                        last = mm(G[0:N_CMP, g, 0, 0:DH2], cmp_in[:, 1, l, g, :], w,
                                                  start=(l == 0), stop=(l == CMP_L - 1))
                        last.then_inc(unit_used, 1)
                c["unit"] = n + 8
                prepared()
                attention(plan("nsa"))
                mixer_out(KT)

            def stick():
                linear(ACT_PAIR, 3 * D, before=normed)
                pe.wait_ge(g_taken[0], c["g"])
                pe.wait_ge(g_taken[1], c["g"])
                for pair in range(H2 // 2):
                    hs = [2 * pair, 2 * pair + 1]
                    for j, h in enumerate(hs):
                        transposes([proj[:, t, o + h * DH2:o + (h + 1) * DH2] for o in (0, D) for t in range(TT)],
                                   c["T"])
                        c.up("T")
                    for j, h in enumerate(hs):
                        copied(c["T"] - 2 + j)
                        c.up("att")
                        if c["att"] >= 2:
                            pe.wait_ge(s_taken, c["att"] - 1)
                        for st in range(TT):
                            last = mm(S[:, st, :], qk[:, j, (TT + st) * P:(TT + st + 1) * P], qk[:, j, 0:TT * P],
                                      start=(st == 0), stop=True, skip_group_check=True)
                        last.then_inc(s_full, 1)
                    for j, h in enumerate(hs):
                        prepared()
                        mm(G[:, j, 0, 0:SEQ], from_on, pt[:, j, 0:SEQ], start=True, stop=False)
                        mm(G[:, j, 0, 0:SEQ], ones, pt[:, j, SEQ:2 * SEQ], start=False, stop=True)
                        last = mm(G[:, j, 1, 0:SEQ], from_on, pt[:, j, SEQ:2 * SEQ], start=True, stop=True)
                        last.then_inc(mix_full, 1)
                    for j, h in enumerate(hs):
                        pe.wait_ge(p_ready, c["att"] - 1 + j)
                        if c["att"] - 2 + j >= 1:
                            pe.wait_ge(o_taken, c["att"] - 2 + j)
                        for t in range(TT):
                            for st in range(t + 1):
                                last = mm(O[:, t, 0:DH2], pr[:, j, st, t * P:(t + 1) * P],
                                          proj[:, st, 2 * D + h * DH2:2 * D + (h + 1) * DH2],
                                          start=(st == 0), stop=(st == t), skip_group_check=True)
                        last.then_inc(o_full, 1)
                pe.wait_ge(o_taken, c["att"])
                mixer_out(KT)

            def conv():
                linear(ACT_PAIR, 2 * D, before=normed)
                for t in range(TT):
                    prepared()
                    turn_rows(t, ymix, KT)
                prepared()
                for t in range(TT):
                    for b in range(2):
                        transposes([conv_acc[:, 4 * b + j, t * P:(t + 1) * P] for j in range(4)], c["T"])
                        c.up("T")
                for t in range(TT):
                    pe.wait_ge(mix_ready, c.up("mix"))
                    turn_rows(t, ymix, KT)
                down(HID_PAIR, KT)

            pe.wait_ge(consts_in, ALL_CONSTS)
            for t in range(TT):
                pe.wait_ge(nrm_ready, c.up("nrm"))
                turn_rows(t, nrm, KT)
            c["g"] = 1
            for kind, *arg in stages:
                if kind == "mem_kv":
                    pe.wait_ge(memn_ready, c.up("memn"))
                    linear(MEM_PAIR, 2 * MEMW)
                elif kind == "ffn":
                    up_down(FF1 // SEQ, True, FF1 // P)
                elif kind == "mlp":
                    up_down(FF2 // HALF, False, FF2 // P)
                elif kind == "mix_a":
                    mix_a()
                elif kind in ("mix_b", "mix_c", "moba"):
                    mix_bc(kind)
                elif kind == "nsa":
                    nsa()
                elif kind == "stick":
                    stick()
                elif kind == "conv":
                    conv()

        @block.scalar
        def _(act):
            c = Counts()
            fn = nc.scalar.activation

            def products(t):
                if t == 0:
                    act.wait_ge(first_done, c.up("chunk"))
                else:
                    act.wait_ge(unit_used, c["unit"])

            def link(ins):
                ins.then_inc(a_link, 1)
                act.wait_ge(a_link, c.up("link"))

            def t_read(n, step=0, i=0):
                act.wait_ge(t_full, n + 1 + step * i)
                return T[n % 2]

            def copy_t(dst, src, n, step=0, i=0):
                fn(dst, src, ACT.Copy).then_inc(t_taken[n % 2], 1)

            def split_one(m, step=0, i=0):
                s_, w = m % RING, unit_cols[m]
                act.wait_ge(unit_full[s_], 2 * LOADED * (m // RING + 1) + 2 * LOADED * (step // RING) * i)
                fn(ring_hi[:, s_, :, 0:w], ring[:, s_, :, 0:w], ACT.Copy).then_inc(hi_ready, 1)

            def ahead(limit):
                split_ahead(act, c, split_one, limit)

            last_square = []

            def square(src, w, done_, accum, t=0):
                if last_square:
                    act.wait_ge(*last_square)
                fn(nrm[:, t, 0:w], src, ACT.Square, **accum).then_inc(done_, 1)
                last_square[:] = [done_, c.up(done_.name)]

            def norm_x(t, first=False):
                if not first:
                    act.wait_ge(x_ready, c.up("x"))
                square(x[:, t, :], D, ssx_ready, dict(accum_out=sums[:, 2 + t:3 + t]), t)
                act.wait_ge(rx_ready, c.up("rx"))
                fn(nrm[:, t, :], x[:, t, :], ACT.Copy, scale=small[:, 2 + t:3 + t]).then_inc(nrm_ready, 1)

            def residual(post, last):
                c.up("g")
                for t in range(TT):
                    if post:
                        products(t)
                        square(G[:, t, :, :].rearrange("p h n -> p (h n)"), D, ssy_ready,
                               dict(accum_out=sums[:, t:t + 1]), t)
                    elif t == 0:
                        c.up("chunk")
                    if not last:
                        norm_x(t)

            def up(n_chunks, paired):
                n, ch, tb = c["unit"], c["chunk"], c["T"]
                per = 1 if paired else 2
                f = ACT.Silu if paired else ACT.Relu
                w = SEQ if paired else HALF

                def gate(par, d, step=0, i=0):
                    act.wait_ge(first_done, ch + d + 1 + (step // CHUNK_UNITS) * i)
                    fn(gated[:, par, 0, 0:w], G[:, 0, par, 0:w], f).then_inc(gated_ready, 1)
                    act.wait_ge(unit_used, n + (d + 1) * CHUNK_UNITS + step * i)
                    fn(gated[:, par, 1, 0:w], G[:, 1, par, 0:w], f).then_inc(gated_ready, 1)

                def copies(d, step=0, i=0):
                    for b in range(per):
                        m = tb + d * per + b
                        bank = t_read(m, step, i)
                        at = (d * per + b) * 2 + step * 2 * i
                        fn(hid_hi[:, bass.ds(at, 2), :], bank[:, :].rearrange("p (k s) -> p k s", k=2), ACT.Copy)\
                            .then_inc(turn_hi, 1)

                def split_chunk(d, step=0, i=0):
                    for u in range(CHUNK_UNITS):
                        split_one(n + d * CHUNK_UNITS + u, step, i)

                ahead(n + RING)
                gate(0, 0)
                split_chunk(2)
                pairs = (n_chunks - 1) // 2
                with act.Fori(0, pairs) as i:
                    for d in (1, 2):
                        gate(d % 2, d, RING, i)
                        copies(d - 1, 2 * per, i)
                        split_chunk(d + 2, RING, i)
                if (n_chunks - 1) % 2:
                    gate((n_chunks - 1) % 2, n_chunks - 1)
                    copies(n_chunks - 2)
                    split_chunk(n_chunks + 1)
                copies(n_chunks - 1)
                c["split"] = n + (n_chunks + 2) * CHUNK_UNITS
                c["unit"], c["chunk"], c["T"] = n + n_chunks * CHUNK_UNITS, ch + n_chunks, tb + n_chunks * per
                c.up("g", n_chunks)

            def linear(width):
                nch = len(chunks_of(width))
                c.up("unit", nch * CHUNK_UNITS)
                ahead(c["unit"] + CHUNK_UNITS)
                c.up("chunk", nch)
                c.up("g", nch)

            def normed():
                c.up("T", 4)

            def turn_out(nk):
                for t in range(TT):
                    for b in range(nk // 4):
                        n = c["T"]
                        bank = t_read(n)
                        fn(hid_hi[:, 4 * b:4 * b + 4, t * P:(t + 1) * P],
                           bank[:, :].rearrange("p (k n) -> p k n", k=4), ACT.Copy).then_inc(turn_hi, 1)
                        c.up("T")
                c.up("unit", nk)

            def attention(heads):
                target = c["unit"] + RING
                base = c["att"]
                n_heads = len(heads)

                def copy_qk(j):
                    h, n = heads[j], c["T"]
                    w = TT * P if h["k"][0] == "cmp" else 2 * TT * P
                    bank = t_read(n)
                    copy_t(qk[0:h["dh"], j % 2, 0:w], bank[0:h["dh"], 0:w], n)
                    c.up("T")

                def exps(j):
                    h, b = heads[j], j % 2
                    act.wait_ge(mx_ready, base + j + 1)
                    w = N_CMP if h["k"][0] == "cmp" else SEQ
                    for t in range(TT):
                        col = TT * j + t
                        last = fn(pr[:, b, t, 0:w], sc[:, b, t, 0:w], ACT.Exp, bias=mx[:, col:col + 1],
                                  accum_out=den[:, col:col + 1])
                    last.then_inc(p_ready, 1)

                def copy_p(j):
                    h, n = heads[j], c["T"]
                    bank = t_read(n)
                    r, w = (N_CMP, 2 * P) if h["k"][0] == "cmp" else (P, 3 * P if h["mask"] else 4 * P)
                    copy_t(pt[0:r, j % 2, 0:w], bank[0:r, 0:w], n)
                    c.up("T")

                for step in range(n_heads + 3):
                    if step < n_heads:
                        copy_qk(step)
                    if 0 <= step - 2 < n_heads:
                        copy_p(step - 2)
                    if 0 <= step - 1 < n_heads:
                        exps(step - 1)
                    ahead(min(c["split"] + 1, target))
                ahead(target)
                c["att"] = base + n_heads

            def squares(blocks):
                for t, c0, w in blocks:
                    if c["sum"]:
                        act.wait_ge(sum_ready, c["sum"])
                    square(proj[:, t, c0:c0 + w], w, sq_ready, {}, 0)
                    c.up("sum")

            def proj_complete():
                for t in range(TT):
                    act.wait_ge(g_taken[t], c["g"])

            def mix_a():
                normed()
                linear(A_IN)
                proj_complete()
                for t in range(TT):
                    fn(proj[:, t, 0:2 * MIX], proj[:, t, 0:2 * MIX], ACT.Gelu_apprx_tanh).then_inc(gelu_ready, 1)
                c.up("sum", TT)
                attention(plan("mix_a"))
                turn_out(KT)

            mem_rows = proj[:, :, 0:D]
            act.dma_start(con[:, :], a["consts"]).then_inc(consts_in, LOADED)
            act.dma_start(x[:, :, :], a["x"][0].rearrange("(t p) d -> p t d", p=P)).then_inc(consts_in, LOADED)
            act.dma_start(mem_rows, a["mem"][0].rearrange("(t p) d -> p t d", p=P)).then_inc(consts_in, LOADED)
            ahead(CHUNK_UNITS)
            act.wait_ge(consts_in, ALL_CONSTS)
            for t in range(TT):
                square(mem_rows[:, t, :], D, ssy_ready, dict(accum_out=sums[:, t:t + 1]), t)
                act.wait_ge(ry_ready, t + 1)
                fn(nrm[:, t, :], mem_rows[:, t, :], ACT.Copy, scale=small[:, t:t + 1]).then_inc(nrm_ready, 1)
            for t in range(TT):
                for b in range(2):
                    n = c["T"]
                    bank = t_read(n)
                    copy_t(mem_t[:, 4 * b:4 * b + 4, t * P:(t + 1) * P], bank[:, :].rearrange("p (k n) -> p k n", k=4), n)
                    c.up("T")
            for t in range(TT):
                norm_x(t, first=True)
            c["g"] = 1
            act.wait_ge(fn_in, c.up("fn_in"))
            for j in range(2):
                fn(rope1[:, j, :, :], rtmp[:, 2 + j, :, :], ACT.Sin).then_inc(fn_out, 1)

            n_stage = len(stages)
            for s, (kind, *arg) in enumerate(stages):
                last = s == n_stage - 1
                if kind == "mem_kv":
                    linear(2 * MEMW)
                    continue
                if kind in ("ffn", "mlp"):
                    normed()
                    if kind == "ffn":
                        up(FF1 // SEQ, True)
                        c.up("unit", FF1 // P)
                    else:
                        up(FF2 // HALF, False)
                        c.up("unit", FF2 // P)
                    ahead(c["unit"] - last_group(FF1 // P if kind == "ffn" else FF2 // P) + RING)
                elif kind == "mix_a":
                    mix_a()
                elif kind == "mix_b":
                    normed()
                    linear(B_IN)
                    attention(plan("mix_b"))
                    act.wait_ge(fn_in, c.up("fn_in"))
                    fn(shares[:, 0, :], den[:, 0:TT * HEADS1], ACT.Ln).then_inc(fn_out, 1)
                    act.wait_ge(fn_in, c.up("fn_in"))
                    fn(shares[:, 2, :], shares[:, 1, :], ACT.Exp).then_inc(fn_out, 1)
                    turn_out(B_OUT // P)
                elif kind == "mix_c":
                    normed()
                    linear(C_IN)
                    act.wait_ge(fn_in, c.up("fn_in"))
                    link(fn(fgt[:, 2, :, :], fgt[:, 1, :, :], ACT.Exp))
                    fn(fgt[:, 1, :, :], fgt[:, 2, :, :], ACT.Ln, bias=1.0).then_inc(fn_out, 1)
                    attention(plan("mix_c"))
                    turn_out(KT)
                elif kind == "moba":
                    normed()
                    linear(3 * D)
                    proj_complete()
                    squares([(t, c0, D) for t in range(TT) for c0 in (0, D)])
                    attention(plan("moba"))
                    turn_out(KT)
                elif kind == "nsa":
                    normed()
                    linear(NSA_IN)
                    proj_complete()
                    fn(gates[:, :, :], proj[:, :, NSA_IN - 3 * H2:NSA_IN], ACT.Sigmoid).then_inc(fn_out, 1)
                    kvw = KVG * DH2
                    squares([(t, c0, w) for t in range(TT)
                             for c0, w in ((0, D), (D, kvw), (D + 2 * kvw, kvw), (D + 4 * kvw, kvw))])
                    for s2 in range(2):
                        n = c["T"]
                        bank = t_read(n)
                        copy_t(kv_t[:, s2, :, :].rearrange("p g n -> p (g n)"), bank[:, :], n)
                        c.up("T")
                    c.up("unit", 8)
                    attention(plan("nsa"))
                    turn_out(KT)
                elif kind == "stick":
                    normed()
                    linear(3 * D)
                    for pair in range(H2 // 2):
                        for j in range(2):
                            n = c["T"]
                            bank = t_read(n)
                            copy_t(qk[:, j, :], bank[:, :], n)
                            c.up("T")
                        for j in range(2):
                            act.wait_ge(mx_ready, c.up("att"))
                            link(fn(pt[:, j, :], pt[:, j, :], ACT.Exp))
                            fn(pt[:, j, :], pt[:, j, :], ACT.Ln, bias=1.0).then_inc(fn_out, 1)
                        for j in range(2):
                            act.wait_ge(arg_ready, c.up("arg"))
                            fn(pr[:, j, :, :], pr[:, j, :, :], ACT.Exp).then_inc(p_ready, 1)
                        ahead(c["split"] + 1)
                    turn_out(KT)
                elif kind == "conv":
                    normed()
                    linear(2 * D)
                    proj_complete()
                    for t in range(TT):
                        fn(proj[:, t, D:2 * D], proj[:, t, D:2 * D], ACT.Sigmoid).then_inc(fn_out, 1)
                    c.up("sum", TT)
                    ahead(c["unit"] + RING)
                    for t in range(TT):
                        for b in range(2):
                            n = c["T"]
                            bank = t_read(n)
                            copy_t(conv_in[:, 4 * b:4 * b + 4, PAD + t * P:PAD + (t + 1) * P],
                                   bank[:, :].rearrange("p (k n) -> p k n", k=4), n)
                            c.up("T")
                    for t in range(TT):
                        for b in range(2):
                            n = c["T"]
                            bank = t_read(n)
                            copy_t(nrm[:, t, b * HALF:(b + 1) * HALF], bank[:, :], n)
                            c.up("T")
                    for t in range(TT):
                        for b in range(2):
                            n = c["T"]
                            bank = t_read(n)
                            for j in range(4):
                                k = 4 * b + j
                                ins = fn(conv_out[:, k, t * P:(t + 1) * P], bank[:, j * P:(j + 1) * P], ACT.Silu,
                                         bias=conv_cols[:, 2, k:k + 1], scale=conv_cols[:, 1, k:k + 1])
                            ins.then_inc(gelu_ready, 1)
                            c.up("T")
                    c.up("unit", KT)
                if kind in MIXERS:
                    ahead(c["unit"] - last_group(OUT_K[kind]) + RING)
                residual(kind in ("ffn", "mix_a", "mix_b", "mix_c"), last)

        @block.vector
        def _(dve):
            c = Counts()
            v = nc.vector

            def products(t):
                if t == 0:
                    dve.wait_ge(first_done, c.up("chunk"))
                else:
                    dve.wait_ge(unit_used, c["unit"])

            def link(ins):
                ins.then_inc(v_link, 1)
                dve.wait_ge(v_link, c.up("link"))

            def split_one(m, step=0, i=0):
                s_, w = m % RING, unit_cols[m]
                dve.wait_ge(hi_ready, split_no[m] + 1 + step * i)
                v.tensor_tensor(ring_lo[:, s_, :, 0:w], ring[:, s_, :, 0:w], ring_hi[:, s_, :, 0:w],
                                ALU.subtract).then_inc(lo_ready, 1)

            def ahead(limit):
                split_ahead(dve, c, split_one, limit)

            def normed(s):
                cols = pre_gain(s)
                for t in range(TT):
                    ts = slice(t * P, (t + 1) * P)
                    for b in range(2):
                        n = c["T"] + b
                        dve.wait_ge(t_full, n + 1)
                        v.tensor_tensor(
                            act_hi[:, 4 * b:4 * b + 4, ts], T[n % 2][:, :].rearrange("p (k n) -> p k n", k=4),
                            cols[:, 4 * b:4 * b + 4].unsqueeze(2).to_broadcast([P, 4, P]), ALU.mult)\
                            .then_inc(act_hi_in, 1)
                    for b in range(2):
                        n = c["T"]
                        dve.wait_ge(act_hi_in, c.up("act_hi"))
                        for j in range(4):
                            k = 4 * b + j
                            ins = v.scalar_tensor_tensor(act_lo[:, k, ts], T[n % 2][:, j * P:(j + 1) * P],
                                                         cols[:, k:k + 1], act_hi[:, k, ts], ALU.mult, ALU.subtract)
                        ins.then_inc(t_taken[n % 2], 1)
                        c.up("T")
                    yield

            def turned_lo(dst, hi, n, shape, step=0, i=0):
                dve.wait_ge(turn_hi, c["turn"] + 1 + step * i)
                v.tensor_tensor(dst, T[n % 2][:, :].rearrange("p (k s) -> p k s", k=shape), hi, ALU.subtract)\
                 .then_inc(t_taken[n % 2], 1)

            def turn_out(nk):
                for t in range(TT):
                    for b in range(nk // 4):
                        at = (slice(None), slice(4 * b, 4 * b + 4), slice(t * P, (t + 1) * P))
                        turned_lo(hid_lo[at], hid_hi[at], c["T"], 4)
                        c.up("turn")
                        c.up("T")

            def linear(width, dst, before=None):
                plan_ = chunks_of(width)
                ahead(c["unit"] + CHUNK_UNITS)
                for c0, w in plan_:
                    c.up("unit", CHUNK_UNITS)
                    for t in range(TT):
                        if c0 == 0 and before is not None:
                            next(before)
                            ahead(c["unit"] + CHUNK_UNITS)
                        products(t)
                        v.tensor_copy(dst[:, t, c0:c0 + w], G[:, t, (c0 // HALF) % 2, 0:w]).then_inc(g_taken[t], 1)
                    if (c0, w) != plan_[-1]:
                        ahead(c["unit"] + RING)
                c.up("g", len(plan_))

            def up(s, n_chunks, paired):
                n, ch = c["unit"], c["chunk"]
                w = SEQ if paired else HALF
                lo = SEQ if paired else 0
                per = 1 if paired else 2
                before = normed(s)

                gr = c["gated"]

                def one(par, d, step=0, i=0):
                    for t in range(TT):
                        dve.wait_ge(gated_ready, gr + TT * d + t + 1 + (TT * step // CHUNK_UNITS) * i)
                        v.tensor_tensor(hid[:, par, t, 0:w], G[:, t, par, lo:lo + w], gated[:, par, t, 0:w],
                                        ALU.mult).then_inc(g_taken[t], 1)

                def lows(d, step=0, i=0):
                    for b in range(per):
                        at = (d * per + b) * 2 + step * 2 * i
                        dve.wait_ge(turn_hi, turn0 + d * per + b + 1 + step * i)
                        n_ = tb + d * per + b
                        v.tensor_tensor(hid_lo[:, bass.ds(at, 2), :], T[n_ % 2][:, :].rearrange("p (k s) -> p k s", k=2),
                                        hid_hi[:, bass.ds(at, 2), :], ALU.subtract).then_inc(t_taken[n_ % 2], 1)

                def split_chunk(d, step=0, i=0):
                    for u in range(CHUNK_UNITS):
                        split_one(n + d * CHUNK_UNITS + u, step, i)

                ahead(n + CHUNK_UNITS)
                next(before)
                ahead(n + RING)
                next(before)
                tb, turn0 = c["T"], c["turn"]
                one(0, 0)
                split_chunk(2)
                pairs = (n_chunks - 1) // 2
                with dve.Fori(0, pairs) as i:
                    for d in (1, 2):
                        one(d % 2, d, RING, i)
                        lows(d - 1, 2 * per, i)
                        split_chunk(d + 2, RING, i)
                if (n_chunks - 1) % 2:
                    one((n_chunks - 1) % 2, n_chunks - 1)
                    lows(n_chunks - 2)
                    split_chunk(n_chunks + 1)
                lows(n_chunks - 1)
                c["split"] = n + (n_chunks + 2) * CHUNK_UNITS
                c["unit"], c["chunk"] = n + n_chunks * CHUNK_UNITS, ch + n_chunks
                c.up("T", n_chunks * per)
                c.up("turn", n_chunks * per)
                c.up("gated", TT * n_chunks)
                c.up("g", n_chunks)

            def memory(i):
                for k in range(KT):
                    ins = v.tensor_scalar(memn_hi[:, k, :], mem_t[:, k, :], mem_cols[:, i, k:k + 1], None, ALU.mult)
                link(ins)
                for k in range(KT):
                    ins = v.scalar_tensor_tensor(memn_lo[:, k, :], mem_t[:, k, :], mem_cols[:, i, k:k + 1],
                                                 memn_hi[:, k, :], ALU.mult, ALU.subtract)
                ins.then_inc(memn_ready, 1)

            def residual(s):
                post = stages[s][0] in POST
                c.up("g")
                for t in range(TT):
                    y = G[:, t, :, :].rearrange("p h n -> p (h n)")
                    if post:
                        if t == 0:
                            c.up("chunk")
                            dve.wait_ge(row_full, LOADED * c.up("row"))
                        dve.wait_ge(ry_ready, c.up("ry"))
                        factor = post_gain(s)[2]
                        v.scalar_tensor_tensor(scratch_v[:, t, :], y, small[:, t:t + 1], gain_row[:, :],
                                               ALU.mult, ALU.mult).then_inc(g_taken[t], 1)
                        dve.wait_ge(g_taken[t], c["g"])
                        v.scalar_tensor_tensor(x[:, t, :], scratch_v[:, t, :], factor, x[:, t, :],
                                               ALU.mult, ALU.add).then_inc(x_ready, 1)
                    else:
                        products(t)
                        v.tensor_tensor(x[:, t, :], y, x[:, t, :], ALU.add).then_inc(x_ready, 1)
                        dve.wait_ge(x_ready, c["x"] + 1)
                        dve.sem_inc(g_taken[t], 1)
                    c.up("x")

            def attention(heads):
                base = c["att"]
                n_heads = len(heads)

                def score(j):
                    h, b = heads[j], j % 2
                    w = N_CMP if h["k"][0] == "cmp" else SEQ
                    dve.wait_ge(s_full, base + j + 1)
                    dst, src = sc[:, b, :, 0:w], S[:, :, 0:w]
                    if h["mask"]:
                        ins = v.scalar_tensor_tensor(dst, src, h["scale"], mask[h["mask"]], ALU.mult, ALU.add)
                    else:
                        ins = v.tensor_scalar(dst, src, h["scale"], None, ALU.mult)
                    ins.then_inc(s_taken, 1)
                    dve.wait_ge(s_taken, base + j + 1)
                    v.tensor_reduce(mx[:, TT * j:TT * j + TT], dst, AX_X, ALU.max, negate=True)\
                     .then_inc(mx_ready, 1)

                def place(j):
                    h, dh = heads[j], heads[j]["dh"]
                    dve.wait_ge(o_full, base + j + 1)
                    link(v.reciprocal(recip[:, :], den[:, TT * j:TT * j + TT]))
                    if "gate" in h:
                        link(v.tensor_tensor(recip[:, :], recip[:, :], gates[:, :, h["gate"]], ALU.mult))
                        if h["first"]:
                            link(v.tensor_tensor(recip[:, :], recip[:, :], cmp_any, ALU.mult))
                    y = parts_o if h.get("part") else ymix
                    at = h["y"]
                    if h.get("first", True):
                        ins = v.tensor_tensor(y[:, :, at:at + dh], O[:, :, 0:dh],
                                              recip[:, :].unsqueeze(2).to_broadcast([P, TT, dh]), ALU.mult)
                    else:
                        for t in range(TT):
                            ins = v.scalar_tensor_tensor(y[:, t, at:at + dh], O[:, t, 0:dh], recip[:, t:t + 1],
                                                         y[:, t, at:at + dh], ALU.mult, ALU.add)
                    ins.then_inc(o_taken, 1)
                    dve.wait_ge(o_taken, base + j + 1)

                target = c["unit"] + RING
                for step in range(n_heads + 3):
                    if 0 <= step - 1 < n_heads:
                        score(step - 1)
                    if 0 <= step - 3 < n_heads:
                        place(step - 3)
                    ahead(min(c["split"] + 1, target))
                ahead(target)
                c["att"] = base + n_heads
                c.up("T", 2 * n_heads)

            def rope(block_, nh, ca, sa, cb, sb_):
                half = block_.shape[3]
                x1, x2 = block_[:, :, 0, :], block_[:, :, 1, :]
                tmp = scratch_v[:, :, :].rearrange("p a b -> p (a b)")[:, 0:4 * nh * half] \
                    .rearrange("p (k h n) -> p k h n", k=4, h=nh)

                def wide(tab):
                    return tab.unsqueeze(1).to_broadcast([P, nh, half])
                v.tensor_tensor(tmp[:, 0], x1, wide(ca), ALU.mult)
                v.tensor_tensor(tmp[:, 1], x2, wide(sa), ALU.mult)
                v.tensor_tensor(tmp[:, 2], x2, wide(cb), ALU.mult)
                link(v.tensor_tensor(tmp[:, 3], x1, wide(sb_), ALU.mult))
                v.tensor_tensor(x1, tmp[:, 0], tmp[:, 1], ALU.subtract)
                link(v.tensor_tensor(x2, tmp[:, 2], tmp[:, 3], ALU.add))

            def gain_tables(g):
                def half(n):
                    return head_gain[:, g, n * 64:(n + 1) * 64].unsqueeze(1).to_broadcast([P, TT, 64])
                v.tensor_tensor(tabs[:, 0], cos2, half(0), ALU.mult)
                v.tensor_tensor(tabs[:, 1], sin2, half(1), ALU.mult)
                v.tensor_tensor(tabs[:, 2], cos2, half(1), ALU.mult)
                link(v.tensor_tensor(tabs[:, 3], sin2, half(0), ALU.mult))

            def rs_wait():
                dve.wait_ge(small_ready, c.up("small"))

            def norm_rope(blocks):
                for t, c0, w, g in blocks:
                    nh = w // DH2
                    gain_tables(g)
                    dve.wait_ge(sq_ready, c.up("sq"))
                    v.tensor_reduce(head_sum[:, 0:nh], nrm[:, 0, 0:w].rearrange("p (h d) -> p h d", h=nh),
                                    AX_X, ALU.add).then_inc(sum_ready, 1)
                    c.up("sum")
                    rs_wait()
                    blk = proj[:, t, c0:c0 + w].rearrange("p (h d) -> p h d", h=nh)
                    link(v.tensor_tensor(blk, blk, head_rs[:, 0:nh].unsqueeze(2).to_broadcast([P, nh, DH2]),
                                         ALU.mult))
                    rope(proj[:, t, c0:c0 + w].rearrange("p (h two d) -> p h two d", h=nh, two=2), nh,
                         *[tabs[:, k, t, :] for k in range(4)])

            def done():
                dve.sem_inc(prep_ready, 1)

            def layer_norm(t, src, n, piece, dst):
                k = n // piece
                for j in range(k):
                    ins = v.bn_stats(bn[:, 6 * j:6 * j + 6], src[:, j * piece:(j + 1) * piece])
                link(ins)
                v.bn_aggr(mean_var[:, t, :], bn[:, 0:6 * k]).then_inc(sum_ready, 1)
                c.up("sum")
                rs_wait()
                return v.tensor_scalar(dst, src, mean_var[:, t, 0:1], head_rs[:, 0:1], ALU.subtract, ALU.mult)

            def turned(n_banks):
                c.up("T", n_banks)

            def mix_a(s):
                j = stages[s][2]
                linear(A_IN, proj, normed(s))
                for t in range(TT):
                    dve.wait_ge(gelu_ready, c.up("gelu"))
                    link(layer_norm(t, proj[:, t, MIX:2 * MIX], MIX, MIX // 2, scratch_v[:, t, 0:MIX]))
                    link(v.tensor_tensor(scratch_v[:, t, 0:MIX], scratch_v[:, t, 0:MIX], v_gain[:, j, :],
                                         ALU.mult))
                dve.wait_ge(spat_ready, c.up("spat"))
                done()
                dve.wait_ge(mix_full, c.up("mixf"))
                for g in range(HEADS1):
                    at = g * DH1
                    v.scalar_tensor_tensor(ymix[:, :, at:at + DH1],
                                           gflat[:, g * P:(g + 1) * P].rearrange("p (t d) -> p t d", t=TT),
                                           spat_b[:, j, g:g + 1], proj[:, :, at:at + DH1], ALU.add, ALU.mult)
                attention(plan("mix_a"))
                turn_out(KT)

            def mix_b(s):
                linear(B_IN, proj, normed(s))
                for t in range(TT):
                    for o in (0, MIX):
                        cs, sn = rope1[:, 0, t, :], rope1[:, 1, t, :]
                        rope(proj[:, t, o:o + MIX].rearrange("p (h two d) -> p h two d", h=HEADS1, two=2),
                             HEADS1, cs, sn, cs, sn)
                done()
                attention(plan("mix_b"))
                n = TT * HEADS1 // 3
                dve.sem_inc(fn_in, 1)
                dve.wait_ge(fn_out, c.up("fn_out"))
                link(v.tensor_tensor(shares[:, 0, :], shares[:, 0, :], mx[:, 0:TT * HEADS1], ALU.subtract))
                l = [shares[:, 0, g * n:(g + 1) * n] for g in range(3)]
                top = shares[:, 3, 0:n]
                link(v.tensor_tensor(top, l[0], l[1], ALU.max))
                link(v.tensor_tensor(top, top, l[2], ALU.max))
                v.tensor_tensor(shares[:, 1, :].rearrange("p (g n) -> p g n", g=3),
                                shares[:, 0, :].rearrange("p (g n) -> p g n", g=3),
                                top.unsqueeze(1).to_broadcast([P, 3, n]), ALU.subtract).then_inc(fn_in, 1)
                dve.wait_ge(fn_out, c.up("fn_out"))
                e = [shares[:, 2, g * n:(g + 1) * n] for g in range(3)]
                link(v.tensor_tensor(top, e[0], e[1], ALU.add))
                link(v.tensor_tensor(top, top, e[2], ALU.add))
                link(v.reciprocal(top, top))
                link(v.tensor_tensor(shares[:, 4, :].rearrange("p (g n) -> p g n", g=3),
                                     shares[:, 2, :].rearrange("p (g n) -> p g n", g=3),
                                     top.unsqueeze(1).to_broadcast([P, 3, n]), ALU.mult))
                share = shares[:, 4, :].rearrange("p (h t) -> p h t", t=TT)
                for t in range(TT):
                    o = parts_o[:, t, :].rearrange("p (h d) -> p h d", h=HEADS1)
                    link(v.tensor_tensor(o, o, share[:, :, t].unsqueeze(2).to_broadcast([P, HEADS1, DH1]),
                                         ALU.mult))
                link(v.tensor_tensor(ymix[:, :, 0:DIL_OUT], parts_o[:, :, 0:DIL_OUT],
                                     parts_o[:, :, DIL_OUT:2 * DIL_OUT], ALU.add))
                v.tensor_tensor(ymix[:, :, 0:DIL_OUT], ymix[:, :, 0:DIL_OUT],
                                parts_o[:, :, 2 * DIL_OUT:3 * DIL_OUT], ALU.add).then_inc(mix_ready, 1)
                turn_out(B_OUT // P)

            def mix_c(s):
                linear(C_IN, proj, normed(s))
                f = proj[:, :, 3 * MIX:3 * MIX + HEADS1]
                fb = forget_b[:, :].unsqueeze(1).to_broadcast([P, TT, HEADS1])
                for t in range(TT):
                    dve.wait_ge(g_taken[t], c["g"])
                link(v.tensor_tensor(fgt[:, 0], f, fb, ALU.add))
                v.scalar_tensor_tensor(fgt[:, 1], fgt[:, 0], -1.0, fgt[:, 0], ALU.mult, ALU.min).then_inc(fn_in, 1)
                dve.wait_ge(fn_out, c.up("fn_out"))
                link(v.tensor_scalar(fgt[:, 2], fgt[:, 0], -1.0 / SCALE1, 0.0, ALU.mult, ALU.max))
                link(v.scalar_tensor_tensor(fgt[:, 3], fgt[:, 1], 1.0 / SCALE1, fgt[:, 2], ALU.mult, ALU.add))
                done()
                attention(plan("mix_c"))
                turn_out(KT)

            def moba(s):
                linear(3 * D, proj, normed(s))
                norm_rope([(t, c0, D, 4 + c0 // D) for t in range(TT) for c0 in (0, D)])
                done()
                attention(plan("moba"))
                turn_out(KT)

            def nsa(s):
                linear(NSA_IN, proj, normed(s))
                c.up("fn_out")
                kvw = KVG * DH2
                norm_rope([(t, c0, w, g) for t in range(TT)
                           for c0, w, g in ((0, D, 0), (D, kvw, 1), (D + 2 * kvw, kvw, 2), (D + 4 * kvw, kvw, 3))])
                done()
                for s2 in range(2):
                    n = c["T"]
                    dve.wait_ge(t_taken[n % 2], n // 2 + 1)
                    c.up("T")
                for s2 in range(2):
                    for g in range(KVG):
                        seq = kv_t[:, s2, g, :].rearrange("p (m b) -> p b m", b=CMP_STRIDE)
                        for half in range(2):
                            ls = slice(half * CMP_STRIDE, (half + 1) * CMP_STRIDE)
                            ins = v.tensor_tensor(
                                cmp_in[:, s2, ls, g, :], seq[:, :, half:half + N_CMP],
                                nsa_pos[:, s2, ls].unsqueeze(2).to_broadcast([P, CMP_STRIDE, N_CMP]), ALU.add)
                link(ins)
                done()
                c.up("unit", 8)
                dve.wait_ge(unit_used, c["unit"])
                v.tensor_copy(kc_t[:, :, :].rearrange("p g n -> p (g n)"), S[:, 0, 0:KVG * N_CMP])
                link(v.tensor_copy(vc[0:N_CMP, :, :], G[0:N_CMP, :, 0, 0:DH2]))
                dve.wait_ge(fn_out, c["fn_out"])
                done()
                attention(plan("nsa"))
                turn_out(KT)

            def stick(s):
                linear(3 * D, proj, normed(s))
                for pair in range(H2 // 2):
                    turned(2)
                    for j in range(2):
                        dve.wait_ge(s_full, c.up("att"))
                        v.scalar_tensor_tensor(sc[:, j, :, :], S[:, :, :], SCALE2, mask["strict_add"],
                                               ALU.mult, ALU.add).then_inc(s_taken, 1)
                        dve.wait_ge(s_taken, c["att"])
                        flat = sc[:, j, :, :].rearrange("p t n -> p (t n)")
                        v.scalar_tensor_tensor(pt[:, j, :], flat, -1.0, flat, ALU.mult, ALU.min)\
                         .then_inc(mx_ready, 1)
                    for j in range(2):
                        flat = sc[:, j, :, :].rearrange("p t n -> p (t n)")
                        dve.wait_ge(fn_out, c.up("fn_out"))
                        link(v.scalar_tensor_tensor(pt[:, j, :], flat, 0.0, pt[:, j, :], ALU.max, ALU.add))
                        v.tensor_tensor(pt[:, j, :], pt[:, j, :], C("strict_one"), ALU.mult)\
                         .then_inc(prep_ready, 1)
                    for j in range(2):
                        dve.wait_ge(mix_full, c.up("mixf"))
                        v.tensor_tensor(pr[:, j, :, :], sc[:, j, :, :], G[:, j, :, 0:SEQ], ALU.subtract)\
                         .then_inc(arg_ready, 1)
                    for j in range(2):
                        h = 2 * pair + j
                        dve.wait_ge(o_full, c["att"] - 1 + j)
                        v.tensor_copy(ymix[:, :, h * DH2:(h + 1) * DH2], O[:, :, 0:DH2]).then_inc(o_taken, 1)
                    ahead(c["split"] + 1)
                turn_out(KT)

            def conv(s):
                v.memset(conv_in[:, :, 0:PAD], 0.0)
                linear(2 * D, proj, normed(s))
                for t in range(TT):
                    dve.wait_ge(fn_out, c.up("fn_out"))
                    v.tensor_tensor(ymix[:, t, :], proj[:, t, 0:D], proj[:, t, D:2 * D], ALU.mult)\
                     .then_inc(prep_ready, 1)
                ahead(c["unit"] + RING)
                for k in range(4):
                    n = c["T"]
                    dve.wait_ge(t_taken[n % 2], n // 2 + 1)
                    c.up("T")
                for k in range(KT):
                    ins = v.tensor_scalar(conv_acc[:, k, :], conv_in[:, k, 0:SEQ], conv_taps[:, k, 0:1],
                                          conv_cols[:, 0, k:k + 1], ALU.mult, ALU.add)
                link(ins)
                base = c["link"]
                with dve.Fori(0, CONV_W - 1) as i:
                    for k in range(KT):
                        ins = v.scalar_tensor_tensor(conv_acc[:, k, :], conv_in[:, k, bass.ds(i + 1, SEQ)],
                                                     conv_taps[:, k, bass.ds(i + 1, 1)], conv_acc[:, k, :],
                                                     ALU.mult, ALU.add)
                    ins.then_inc(v_link, 1)
                    dve.wait_ge(v_link, base + 1 + i)
                c["link"] = base + CONV_W - 1
                done()
                for k in range(4):
                    n = c["T"]
                    dve.wait_ge(t_taken[n % 2], n // 2 + 1)
                    c.up("T")
                for t in range(TT):
                    ins = layer_norm(t, nrm[:, t, :], D, HALF, ymix[:, t, :])
                    ins.then_inc(mix_ready, 1)
                for t in range(TT):
                    for b in range(2):
                        at = (slice(None), slice(4 * b, 4 * b + 4), slice(t * P, (t + 1) * P))
                        dve.wait_ge(gelu_ready, c.up("gelu"))
                        v.tensor_copy(hid_hi[at], conv_out[at]).then_inc(turn_hi, 1)
                        dve.wait_ge(turn_hi, c.up("turn"))
                        v.tensor_tensor(hid_lo[at], conv_out[at], hid_hi[at], ALU.subtract)\
                         .then_inc(t_taken[c["T"] % 2], 1)
                        c.up("T")

            ahead(CHUNK_UNITS)
            for t in range(TT):
                dve.sem_inc(g_taken[t], 1)
            c["g"] = 1
            c["ry"] = TT
            dve.wait_ge(gains_in, ALL_GAINS)
            dve.wait_ge(consts_in, ALL_CONSTS)
            link(v.tensor_copy(pos_f[:, :], pos_i[:, :]))
            for t in range(TT):
                ins = v.tensor_scalar(rtmp[:, 0, t, :], C("inv_freq"), pos_f[:, t:t + 1], None, ALU.mult)
            link(ins)
            ang = rtmp[:, 0]
            for j, quarter in ((0, 0.25), (1, 0.0)):
                k, r = rtmp[:, 1], rtmp[:, 2 + j]
                link(v.tensor_scalar(k, ang, 1.0 / TWO_PI, quarter, ALU.mult, ALU.add))
                link(v.tensor_scalar(k, k, ROUND, None, ALU.add))
                link(v.tensor_scalar(k, k, -ROUND, None, ALU.add))
                link(v.scalar_tensor_tensor(r, k, -PI_A, ang, ALU.mult, ALU.add))
                link(v.scalar_tensor_tensor(r, k, -PI_B, r, ALU.mult, ALU.add))
                link(v.scalar_tensor_tensor(r, k, -PI_C, r, ALU.mult, ALU.add))
                link(v.tensor_scalar(r, r, quarter * TWO_PI, PI_TOP, ALU.add, ALU.min))
                link(v.tensor_scalar(r, r, -PI_TOP, None, ALU.max))
            dve.sem_inc(fn_in, 1)
            dve.wait_ge(fn_out, c.up("fn_out", 2))
            c["T"] = 4

            for s, (kind, *arg) in enumerate(stages):
                if s == first_late and s:
                    dve.sem_inc(early_done, 1)
                    dve.wait_ge(late_in, LOADED * len(late_loads))
                if kind == "mem_kv":
                    if s == 0:
                        for n in range(4):
                            dve.wait_ge(t_taken[n % 2], n // 2 + 1)
                    if s == 0 or stages[s - 1][0] == "mem_kv":
                        memory(arg[0])
                    linear(2 * MEMW, memkv)
                    continue
                if kind == "ffn":
                    up(s, FF1 // SEQ, True)
                    c.up("unit", FF1 // P)
                elif kind == "mlp":
                    up(s, FF2 // HALF, False)
                    c.up("unit", FF2 // P)
                else:
                    {"mix_a": mix_a, "mix_b": mix_b, "mix_c": mix_c, "moba": moba, "nsa": nsa,
                     "stick": stick, "conv": conv}[kind](s)
                    c.up("unit", OUT_K[kind])
                if s + 1 < len(stages) and stages[s + 1][0] == "mem_kv":
                    memory(stages[s + 1][1])
                ahead(c["unit"] - last_group({"ffn": FF1 // P, "mlp": FF2 // P, **OUT_K}[kind]) + RING)
                residual(s)

        @block.gpsimd
        def _(pool):
            c = Counts()
            g_ = nc.gpsimd

            last_power = []

            def rsqrt(dst, src, scale, eps, n, done_):
                if last_power:
                    pool.wait_ge(*last_power)
                g_.tensor_scalar(pool_tmp[:, 0:n], src, scale, eps, ALU.mult, ALU.add).then_inc(p_link, 1)
                pool.wait_ge(p_link, c.up("link"))
                g_.tensor_tensor(dst, pool_tmp[:, 0:n], minus_half[:, 0:n], ALU.pow).then_inc(done_, 1)
                last_power[:] = [done_, c.up(done_.name)]

            def head(n, width):
                pool.wait_ge(sum_ready, c.up("sum"))
                rsqrt(head_rs[:, 0:n], head_sum[:, 0:n], 1.0 / width, RMS_EPS, n, small_ready)

            def variance(t, eps):
                pool.wait_ge(sum_ready, c.up("sum"))
                rsqrt(head_rs[:, 0:1], mean_var[:, t, 1:2], 1.0, eps, 1, small_ready)

            def row(s):
                i, j, _ = post_gain(s)
                if c["row"]:
                    pool.wait_ge(x_ready, c["row_x"])
                pool.dma_start(gain_row[:, :], a["norm_g"][i, j:j + 1, :].partition_broadcast(P)
                               .rearrange("p a d -> p (a d)")).then_inc(row_full, LOADED)
                c.up("row")

            def spatial(j):
                pool.dma_start(spat_w[:, :, :], a["a_spatial_t"][j]).then_inc(spat_in, LOADED)
                pool.wait_ge(spat_in, LOADED * c.up("spat"))
                g_.affine_select(out=spat_w[:, :, :], in_=spat_w[:, :, :], compare_op=ALU.is_ge, fill=0.0, base=0,
                                 pattern=[[0, HEADS1], [1, P]], channel_multiplier=-1).then_inc(spat_ready, 1)

            for dst, src in loads:
                pool.dma_start(dst, src).then_inc(gains_in, LOADED)
            pool.wait_ge(consts_in, ALL_CONSTS)
            for t in range(TT):
                pool.wait_ge(ssy_ready, c.up("ssy"))
                rsqrt(small[:, t:t + 1], sums[:, t:t + 1], 1.0 / D, RMS_EPS, 1, ry_ready)
            for t in range(TT):
                pool.wait_ge(ssx_ready, c.up("ssx"))
                rsqrt(small[:, 2 + t:3 + t], sums[:, 2 + t:3 + t], 1.0 / D, RMS_EPS, 1, rx_ready)
            seen_x = 0
            for s, (kind, *arg) in enumerate(stages):
                if kind == "mem_kv":
                    continue
                if s == first_late:
                    pool.wait_ge(early_done, 1)
                    for dst, src in late_loads:
                        pool.dma_start(dst, src).then_inc(late_in, LOADED)
                if kind in POST:
                    c["row_x"] = seen_x
                    row(s)
                if kind == "mix_a":
                    if seen_x:
                        pool.wait_ge(x_ready, seen_x)
                    spatial(arg[1])
                    for t in range(TT):
                        variance(t, LN_EPS)
                elif kind == "moba":
                    for _ in range(2 * TT):
                        head(H2, DH2)
                elif kind == "nsa":
                    for t in range(TT):
                        for n in (H2, KVG, KVG, KVG):
                            head(n, DH2)
                elif kind == "conv":
                    for t in range(TT):
                        variance(t, RMS_EPS)
                last = s == len(stages) - 1
                for t in range(TT):
                    if kind in POST:
                        pool.wait_ge(ssy_ready, c.up("ssy"))
                        rsqrt(small[:, t:t + 1], sums[:, t:t + 1], 1.0 / D, RMS_EPS, 1, ry_ready)
                    if not last:
                        pool.wait_ge(ssx_ready, c.up("ssx"))
                        rsqrt(small[:, 2 + t:3 + t], sums[:, 2 + t:3 + t], 1.0 / D, RMS_EPS, 1, rx_ready)
                seen_x += TT


STAGES = []
for _i, _kind in enumerate(("mix_a", "mix_b", "mix_c", "mix_a")):
    STAGES += ([("mem_kv", 0), ("ffn", 0, 0)] if _i == 0 else [("ffn", _i, 0), ("mem_kv", _i)]) \
        + [(_kind, _i, _i // 3), ("ffn", _i, 1)]
for _i, _kind in enumerate(("nsa", "stick", "conv", "moba")):
    STAGES += [(_kind, _i), ("mlp", _i)]

N_STAGES = len(STAGES)


def kernel(**inputs):
    from concourse import bacc
    from concourse.bass_utils import run_bass_kernel_spmd

    n = {k: np.asarray(v) for k, v in inputs.items()}
    raw = ("x", "mem", "norm_g", "w_mem_kv", "ffn_w_gate_up", "ffn_w_down", "a_w_in", "a_w_out", "b_w_in",
           "b_w_out", "c_w_in", "c_w_out", "c_forget_bias", "a_v_norm_g", "mlp_w_up_2", "mlp_w_down_2",
           "nsa_w_in_2", "nsa_w_out_2", "nsa_q_norm_2", "nsa_k_norm_2", "sb_w_in_2", "sb_w_out_2",
           "conv_w_in_2", "conv_w_out_2", "moba_w_in_2", "moba_w_out_2", "moba_q_norm_2", "moba_k_norm_2")
    arrays = {k: n[k] for k in raw}

    def cols(v):
        v = v.reshape(-1, KT, P)
        return v.transpose(2, 0, 1)

    arrays["consts"], arrays["consts_1"], arrays["consts_2"] = CONSTS, CONSTS_1, CONSTS_2
    arrays["pos"] = n["positions"].reshape(TT, P).T
    arrays["pre_cols"] = cols(n["norm_g"])
    arrays["mem_cols"] = cols(n["mem_norm_g"])
    arrays["an_cols"] = cols(n["attn_norm_2"])
    arrays["mn_cols"] = cols(n["mlp_norm_2"])
    arrays["conv_cols"] = np.concatenate([cols(n[k]) for k in ("conv_dw_b_2", "conv_ln_g_2", "conv_ln_b_2")], 1)
    arrays["conv_taps"] = n["conv_dw_w_2"][0].reshape(CONV_W, KT, P).transpose(2, 1, 0)
    arrays["a_spatial_t"] = n["a_spatial_w"].transpose(0, 3, 1, 2)
    arrays["a_spatial_bt"] = n["a_spatial_b"].transpose(2, 0, 1)
    arrays["nsa_pos"] = n["nsa_cmp_pos_2"][0].transpose(2, 0, 1)
    arrays["nsa_w_cmp_l"] = n["nsa_w_cmp_2"][0].transpose(2, 0, 1, 3)
    nc = bacc.Bacc("TRN2", target_bir_lowering=False, num_devices=1)
    arrays = {k: np.ascontiguousarray(v) for k, v in arrays.items()}
    a = {k: nc.dram_tensor(k, v.shape, mybir.dt.from_np(v.dtype), kind="ExternalInput").ap()
         for k, v in arrays.items()}
    out = nc.dram_tensor("out", (1, SEQ, D), F32, kind="ExternalOutput").ap()
    build(nc, a, out, STAGES[:N_STAGES])
    r = run_bass_kernel_spmd(nc, [arrays], core_ids=[0])
    return r.results[0]["out"]
```

```python
from contextlib import ExitStack

import numpy as np

import concourse.bass as bass
from concourse import mybir

ALU = mybir.AluOpType
ACT = mybir.ActivationFunctionType
F32 = mybir.dt.float32
F32R = mybir.dt.float32r
I32 = mybir.dt.int32
AX_X = mybir.AxisListType.X

P = 128
SEQ = 256
TT = SEQ // P
D = 1024
KT = D // P
DEPTH = 4
HALF = 512
RING = 8
UNIT_K = 2
CHUNK_UNITS = KT // UNIT_K
LOADED = 16

N_MEM = 256
DH1 = 64
HEADS1 = 12
MIX = HEADS1 * DH1
MEM_HEADS = 4
MEMW = MEM_HEADS * DH1
FF1 = 2816
A_IN = 2 * MIX + MEMW
B_IN = 3 * MIX + MEMW
C_IN = 3 * MIX + HEADS1 + MEMW
DIL_OUT = 4 * DH1
B_OUT = DIL_OUT + MEMW
RMS_EPS, LN_EPS = 1e-6, 1e-5
NEG = -1e30
SCALE1 = DH1 ** -0.5
WINDOW = 128

H2 = 8
DH2 = 128
FF2 = 4096
KVG = 2
HPG = H2 // KVG
CMP_L, CMP_STRIDE = 32, 16
N_CMP = (SEQ - CMP_L) // CMP_STRIDE + 1
NSA_IN = D + 6 * KVG * DH2 + 3 * H2
SCALE2 = DH2 ** -0.5
CONV_W = 31
PAD = CONV_W - 1
CONV_ORDER = (0, 2, 1, 3)
NSA_ORDER = (2, 0, 1, 3, 4, 5)
CONV_PE = 3
DIAGS = 16
EARLY_TAPS = 3

TWO_PI = 6.283185307179586
PI_A, PI_B = 6.28125, 0.0019350051879882812
PI_C = TWO_PI - PI_A - PI_B
PI_TOP = 3.1415925
ROUND = 12582912.0


def tables(names):
    q = np.arange(SEQ)[:, None]
    k = np.arange(SEQ)[None, :]
    s = np.arange(P)

    def additive(keep):
        m = np.where(keep, 0.0, NEG).astype(np.float32)
        return m.reshape(TT, P, -1).transpose(1, 0, 2).reshape(P, -1)

    dist = q - k
    cmp_end = np.arange(N_CMP)[None, :] * CMP_STRIDE + CMP_L - 1
    half2 = DH2 // 2
    inv2 = (np.float32(10000.0) ** (-np.arange(half2, dtype=np.float32) / np.float32(half2))).astype(np.float32)
    ang2 = (np.arange(SEQ, dtype=np.float32)[:, None] * inv2[None, :]).astype(np.float32)
    inv1 = (np.float32(10000.0) ** (-np.arange(0, DH1, 2, dtype=np.float32) / np.float32(DH1))).astype(np.float32)

    def rows(t):
        return t.astype(np.float32).reshape(TT, P, -1).transpose(1, 0, 2).reshape(P, -1)

    strict = (k > q)
    parts = [
        ("ident", np.eye(P)),
        ("upto", (s[:, None] <= np.arange(SEQ)[None, :])),
        ("from_on", (s[:, None] >= s[None, :])),
        ("ones", np.ones((P, P))),
        ("causal", additive(dist >= 0)),
        ("band", additive((dist >= 0) & (dist <= WINDOW))),
        ("dil4", additive((dist >= 0) & (dist % 4 == 0))),
        ("dil16", additive((dist >= 0) & (dist % 16 == 0))),
        ("cmp", additive(cmp_end <= q)),
        ("cmp_any", rows((q >= CMP_L - 1))),
        ("strict_add", additive(strict)),
        ("strict_one", rows(strict)),
        ("cos2", rows(np.cos(ang2.astype(np.float64)))),
        ("sin2", rows(np.sin(ang2.astype(np.float64)))),
        ("inv_freq", np.broadcast_to(inv1[None, :], (P, DH1 // 2))),
        ("minus_half", np.full((P, 16), -0.5)),
    ]
    where, at = {}, 0
    parts = [(name, a) for name, a in parts if name in names]
    for name, a in parts:
        where[name] = (at, a.shape[1])
        at += a.shape[1]
    return where, np.ascontiguousarray(np.concatenate([np.asarray(a, np.float32) for _, a in parts], 1))


WHERE, CONSTS = tables(("ident", "upto", "from_on", "ones", "causal", "cmp", "cmp_any", "inv_freq", "minus_half"))
WHERE_1, CONSTS_1 = tables(("band", "dil4", "dil16"))
WHERE_2, CONSTS_2 = tables(("strict_add", "strict_one", "cos2", "sin2"))


class Counts(dict):

    def __missing__(self, key):
        return 0

    def up(self, key, by=1):
        self[key] = self[key] + by
        return self[key]


def build(nc, a, out, stages):
    with ExitStack() as ctx:
        def sem(name):
            return ctx.enter_context(nc.semaphore(name))

        where = {}
        top = [-(-nc.sbuf_base // 32) * 32]

        def sb(name, shape, dt=F32, over=None, skip=0):
            size = int(np.prod(shape[1:])) * 4
            if over is None:
                at = top[0]
                top[0] += -(-size // 32) * 32
            else:
                at = where[over] + skip
            where[name] = at
            return nc.alloc_sbuf_tensor_at(name + "_sb", shape, dt, offset=at)

        ring = sb("ring", [P, RING, 2, HALF])
        ring_lo = sb("ring_lo", [P, RING, 2, HALF], F32R, over="ring")
        ring_hi = sb("ring_hi", [P, RING, 2, HALF], F32R)
        con = sb("con", [P, CONSTS.shape[1]])
        x = sb("x", [P, TT, D])
        nrm = sb("nrm", [P, TT, D])
        ymix = nrm
        act_hi = sb("act_hi", [P, KT, SEQ], F32R)
        act_lo = sb("act_lo", [P, KT, SEQ], F32R)
        hid_hi = sb("hid_hi", [P, 32, SEQ], F32R)
        proj = sb("proj", [P, TT, 3072])
        mem_t = sb("mem_t", [P, KT, SEQ])
        memn_hi = sb("memn_hi", [P, KT, SEQ], F32R)
        con_1 = sb("con_1", [P, CONSTS_1.shape[1]])
        memkv = sb("memkv", [P, TT, 2 * MEMW])
        work = sb("work", [P, 4, 2 * HALF])
        gated = work[:, 0:2, :].rearrange("p a (t n) -> p a t n", t=TT)
        hid = work[:, 2:4, :].rearrange("p a (t n) -> p a t n", t=TT)
        qk = work[:, 0, :].rearrange("p (b n) -> p b n", b=2)
        sc = work[:, 1, :].rearrange("p (b t n) -> p b t n", b=2, t=TT)
        pr = work[:, 2, :].rearrange("p (b t n) -> p b t n", b=2, t=TT)
        pt = work[:, 3, :].rearrange("p (b n) -> p b n", b=2)
        scratch_v = work[:, 2:4, :]
        memn_lo = sb("memn_lo", [P, KT, SEQ], F32R, over="work")
        conv_out = work[:, 0:2, :].rearrange("p a (k n) -> p (a k) n", n=SEQ)
        hid_lo = sb("hid_lo", [P, 32, SEQ], F32R, over="proj")
        conv_in = sb("conv_in", [P, KT, PAD + SEQ], over="mem_t")
        LATE = 2048
        con_2 = sb("con_2", [P, CONSTS_2.shape[1]], over="memn_hi", skip=LATE)
        head_gain = sb("head_gain", [P, 6, DH2], over="con_2", skip=4 * CONSTS_2.shape[1])
        tabs = sb("tabs", [P, 4, TT, DH2 // 2], over="head_gain", skip=4 * 6 * DH2)
        TILE = 4 * SEQ
        gain_row = sb("gain_row", [P, D], over="hid_hi", skip=FF1 // P * TILE)
        v_gain = sb("v_gain", [P, 2, MIX], over="gain_row", skip=4 * D)
        spat_w = sb("spat_w", [P, HEADS1, P], over="hid_hi", skip=8 * TILE)
        parts_o = sb("parts_o", [P, TT, MIX], over="hid_hi", skip=8 * TILE)
        cmp_in = sb("cmp_in", [P, 2, CMP_L, KVG, N_CMP], over="hid_hi", skip=8 * TILE)
        conv_acc = sb("conv_acc", [P, KT, SEQ], over="hid_hi", skip=8 * TILE)
        diags = sb("diags", [P, 2, DIAGS, P], over="hid_hi", skip=16 * TILE)
        kv_t = sb("kv_t", [P, 2, KVG, SEQ], over="hid_hi")
        pre_cols = sb("pre_cols", [P, 6 * DEPTH, KT])
        mem_cols = sb("mem_cols", [P, DEPTH, KT])
        an_cols = sb("an_cols", [P, DEPTH, KT])
        mn_cols = sb("mn_cols", [P, DEPTH, KT])
        small = sb("small", [P, 64])
        sums = sb("sums", [P, 64])
        den = sb("den", [P, 64])
        mx = sb("mx", [P, 64])
        head_sum = sb("head_sum", [P, 2 * TT, TT * H2])
        head_rs = sb("head_rs", [P, 2 * TT, TT * H2])
        pool_tmp = sb("pool_tmp", [P, 16])
        bn = sb("bn", [P, TT, 12])
        mean_var = sb("mean_var", [P, TT, 2])
        recip = sb("recip", [P, TT])
        shares = sb("shares", [P, 5, TT * HEADS1])
        pos_f = sb("pos_f", [P, TT])
        spat_b = sb("spat_b", [P, 2, HEADS1])
        forget_b = sb("forget_b", [P, HEADS1])
        pos_i = sb("pos_i", [P, TT], I32)
        rope1 = sb("rope1", [P, 2, TT, DH1 // 2])
        rtmp = sb("rtmp", [P, 4, TT, DH1 // 2])
        fgt = sb("fgt", [P, 4, TT, HEADS1])
        nsa_pos = sb("nsa_pos", [P, 2, CMP_L])
        conv_cols = sb("conv_cols", [P, 3, KT])
        conv_taps = sb("conv_taps", [P, KT, CONV_W])
        kc_t = sb("kc_t", [P, KVG, N_CMP])
        vc = sb("vc", [P, KVG, DH2])
        gates = sb("gates", [P, TT, 3 * H2])

        def C(name):
            for t, w in ((con, WHERE), (con_1, WHERE_1), (con_2, WHERE_2)):
                if name in w:
                    at, n = w[name]
                    return t[:, at:at + n]

        ident = C("ident")
        upto, from_on, ones = C("upto"), C("from_on"), C("ones")
        mask = {n: C(n).rearrange("p (t k) -> p t k", t=TT)
                for n in ("causal", "band", "dil4", "dil16", "cmp", "strict_add", "strict_one")}
        cos2 = C("cos2").rearrange("p (t k) -> p t k", t=TT)
        sin2 = C("sin2").rearrange("p (t k) -> p t k", t=TT)
        cmp_any = C("cmp_any")
        minus_half = C("minus_half")

        G = ctx.enter_context(nc.psum_tensor("G", [P, TT, 2, HALF], F32))
        T = [ctx.enter_context(nc.psum_tensor(f"T{b}", [P, HALF], F32)) for b in range(2)]
        S = ctx.enter_context(nc.psum_tensor("S", [P, TT, SEQ], F32))
        O = ctx.enter_context(nc.psum_tensor("O", [P, TT, SEQ], F32))
        gflat = G[:, :, :, :].rearrange("p a b c -> p (a b c)")

        unit_full = [sem(f"unit_full{s}") for s in range(RING)]
        hi_ready = sem("hi_ready")
        lo_ready = sem("lo_ready")
        pool_lo_ready = sem("pool_lo_ready")
        act_hi_in = sem("act_hi_in")
        turn_hi = sem("turn_hi")
        unit_used = sem("unit_used")
        first_done = sem("first_done")
        g_taken = [sem(f"g_taken{t}") for t in range(TT)]
        t_full = sem("t_full")
        t_taken = [sem(f"t_taken{b}") for b in range(2)]
        gated_ready = sem("gated_ready")
        ssy_ready = sem("ssy_ready")
        ssx_ready = sem("ssx_ready")
        ry_ready = sem("ry_ready")
        rx_ready = sem("rx_ready")
        x_ready = sem("x_ready")
        nrm_ready = sem("nrm_ready")
        row_full = sem("row_full")
        row_used = sem("row_used")
        mem_in = sem("mem_in")
        consts_in = sem("consts_in")
        x_in = sem("x_in")
        memn_ready = sem("memn_ready")
        small_ready = sem("small_ready")
        sq_ready = sem("sq_ready")
        head_ready = sem("head_ready")
        prep_ready = sem("prep_ready")
        s_full = sem("s_full")
        s_taken = sem("s_taken")
        mx_ready = sem("mx_ready")
        p_ready = sem("p_ready")
        o_full = sem("o_full")
        o_taken = sem("o_taken")
        diag_ready = sem("diag_ready")
        conv_ready = sem("conv_ready")
        gelu_ready = sem("gelu_ready")
        mix_full = sem("mix_full")
        mix_ready = sem("mix_ready")
        sum_ready = sem("sum_ready")
        arg_ready = sem("arg_ready")
        spat_in = sem("spat_in")
        spat_ready = sem("spat_ready")
        fn_in = sem("fn_in")
        fn_out = sem("fn_out")
        a_link = sem("a_link")
        v_link = sem("v_link")
        p_link = sem("p_link")
        out_done = sem("out_done")
        early_done = sem("early_done")
        late_in = sem("late_in")
        gains_in = sem("gains_in")

        def every(row):
            return row.partition_broadcast(P).rearrange("p a d -> p (a d)")

        loads = [(pre_cols[:, :, :], a["pre_cols"]),
                 (an_cols[:, :, :], a["an_cols"]), (mn_cols[:, :, :], a["mn_cols"]),
                 (conv_cols[:, :, :], a["conv_cols"]), (conv_taps[:, :, :], a["conv_taps"]),
                 (spat_b[:, :, :], a["a_spatial_bt"]), (nsa_pos[:, :, :], a["nsa_pos"]),
                 (con_1[:, :], a["consts_1"]), (pos_i[:, :], a["pos"]), (forget_b[:, :], every(a["c_forget_bias"]))]
        loads += [(v_gain[:, j, :], every(a["a_v_norm_g"][j:j + 1, :])) for j in range(2)]
        late_loads = [(con_2[:, :], a["consts_2"])]
        late_loads += [(head_gain[:, j, :], every(r)) for j, r in enumerate(
            [a["nsa_q_norm_2"]] + [a["nsa_k_norm_2"][0, k:k + 1, :] for k in range(3)]
            + [a["moba_q_norm_2"], a["moba_k_norm_2"]])]
        ALL_GAINS = LOADED * len(loads)

        def chunks_of(width):
            return [(c0, min(HALF, width - c0)) for c0 in range(0, width, HALF)]

        MIXERS = ("mix_a", "mix_b", "mix_c", "nsa", "stick", "conv", "moba")
        WIDTH = {"mix_a": A_IN, "mix_b": B_IN, "mix_c": C_IN, "nsa": NSA_IN, "stick": 3 * D,
                 "conv": 2 * D, "moba": 3 * D}
        OUT_K = {k: KT for k in MIXERS}
        OUT_K["mix_b"] = B_OUT // P

        unit_cols = []
        for kind, *arg in stages:
            if kind in ("ffn", "mlp"):
                n_chunks, nk = (FF1 // SEQ, FF1 // P) if kind == "ffn" else (FF2 // HALF, FF2 // P)
                unit_cols += [HALF] * (CHUNK_UNITS * n_chunks + nk)
                continue
            for _, w in chunks_of(2 * MEMW if kind == "mem_kv" else WIDTH[kind]):
                unit_cols += [w] * CHUNK_UNITS
            if kind == "nsa":
                unit_cols += [0] * 8
            if kind != "mem_kv":
                unit_cols += [HALF] * OUT_K[kind]
        by_pool, n = set(), 0
        for s, (kind, *arg) in enumerate(stages):
            if s and kind != "mem_kv" and stages[s - 1][0] != "mem_kv":
                by_pool |= {n + 5, n + 7}
            if kind in ("ffn", "mlp"):
                n_chunks, nk = (FF1 // SEQ, FF1 // P) if kind == "ffn" else (FF2 // HALF, FF2 // P)
                n += CHUNK_UNITS * n_chunks + nk
            elif kind == "mem_kv":
                n += CHUNK_UNITS
            else:
                n += CHUNK_UNITS * len(chunks_of(WIDTH[kind])) + 8 * (kind == "nsa") + OUT_K[kind]
        lo_no = [0]
        for m, w in enumerate(unit_cols):
            lo_no.append(lo_no[-1] + (w > 0 and m not in by_pool))
        split_no = [0]
        for w in unit_cols:
            split_no.append(split_no[-1] + (w > 0))
        first_late = min([s for s, (kind, *_) in enumerate(stages) if kind in ("nsa", "stick", "conv", "moba", "mlp")]
                         + [len(stages)])

        def split_ahead(engine, c, one, limit):
            limit = min(limit, len(unit_cols))
            rounds = (limit - c["split"]) // RING
            if rounds >= 2 and set(unit_cols[c["split"]:c["split"] + rounds * RING]) == {HALF}:
                with engine.Fori(0, rounds) as i:
                    for j in range(RING):
                        one(c["split"] + j, RING, i)
                c.up("split", rounds * RING)
            while c["split"] < limit:
                if unit_cols[c["split"]]:
                    one(c["split"])
                c.up("split")

        def down_groups(nk):
            if nk <= CHUNK_UNITS:
                return [nk]
            head = nk - 6
            return ([head % CHUNK_UNITS] if head % CHUNK_UNITS else []) + [CHUNK_UNITS] * (head // CHUNK_UNITS) + [6]

        def head_blocks(kind):
            kvw = KVG * DH2
            if kind == "moba":
                cols = ((1, 0, H2, 4), (3, D, H2, 5))
            else:
                cols = ((0, D, KVG, 1), (2, 0, H2, 0), (3, D + 2 * kvw, KVG, 2), (4, D + 4 * kvw, KVG, 3))
            return [(d, c0, nh, g, t) for d, c0, nh, g in cols for t in range(TT)]

        conv_sums = [G[:, t, h, 0:SEQ] for t in range(TT) for h in range(2)] + [S[:, 0, :]]
        diag_groups = [(k, i, min(DIAGS, CONV_W - i)) for k in range(CONV_PE, KT) for i in range(0, CONV_W, DIAGS)]

        def last_group(nk):
            return down_groups(nk)[-1]
        POST = {"ffn", "mix_a", "mix_b", "mix_c"}

        def pre_gain(s):
            kind, *arg = stages[s]
            if kind == "ffn":
                return pre_cols[:, 6 * arg[0] + 4 * arg[1], :]
            if kind == "mlp":
                return mn_cols[:, arg[0], :]
            if kind in ("mix_a", "mix_b", "mix_c"):
                return pre_cols[:, 6 * arg[0] + 2, :]
            return an_cols[:, arg[0], :]

        def post_gain(s):
            kind, *arg = stages[s]
            return (arg[0], 4 * arg[1] + 1, 0.5) if kind == "ffn" else (arg[0], 3, 1.0)

        stages_x = sum(kind != "mem_kv" for kind, *_ in stages)

        block = ctx.enter_context(nc.Block())

        @block.sync
        def _(sp):
            c = Counts()

            def load(src, dst_cols, n, step=0, i=0, whole=True):
                slot = n % RING
                if n >= RING:
                    sp.wait_ge(unit_used, (n + 1 - RING) + step * i)
                for k in range(UNIT_K):
                    sp.dma_start(dst_cols(slot, k), src(k)).then_inc(unit_full[slot], LOADED)

            def plain_chunk(w, c0, width, n, step=0, i=0):
                for u in range(CHUNK_UNITS):
                    load(lambda k: w[(2 * u + k) * P:(2 * u + k + 1) * P, bass.ds(c0, width)],
                         lambda s, k: ring[:, s, k, 0:width], n + u, step, i)

            def linear(w, width):
                full, rest = width // HALF, width % HALF
                pairs = full // 2
                n = c["unit"]
                if pairs:
                    with sp.Fori(0, pairs) as i:
                        for par in range(2):
                            plain_chunk(w, i * (2 * HALF) + par * HALF, HALF, n + par * CHUNK_UNITS, RING, i)
                n += pairs * RING
                if full % 2:
                    plain_chunk(w, pairs * 2 * HALF, HALF, n)
                    n += CHUNK_UNITS
                if rest:
                    plain_chunk(w, full * HALF, rest, n)
                    n += CHUNK_UNITS
                c["unit"] = n

            def pair_chunk(w, col, n, step=0, i=0):
                v = w.rearrange("p (two f) -> p two f", two=2)
                for u in range(CHUNK_UNITS):
                    load(lambda k: v[(2 * u + k) * P:(2 * u + k + 1) * P, :, bass.ds(col, SEQ)],
                         lambda s, k: ring[:, s, k, :].rearrange("p (two f) -> p two f", two=2), n + u, step, i)

            def up(w, n_chunks, paired):
                cols = SEQ if paired else HALF
                n = c["unit"]

                def one(col, n, step=0, i=0):
                    if paired:
                        pair_chunk(w, col, n, step, i)
                    else:
                        plain_chunk(w, col, HALF, n, step, i)

                one(0, n)
                pairs = (n_chunks - 1) // 2
                with sp.Fori(0, pairs) as i:
                    for par in range(2):
                        one(i * (2 * cols) + (par + 1) * cols, n + (par + 1) * CHUNK_UNITS, RING, i)
                if (n_chunks - 1) % 2:
                    one((n_chunks - 1) * cols, n + (n_chunks - 1) * CHUNK_UNITS)
                c["unit"] = n + n_chunks * CHUNK_UNITS

            def down(w, nk):
                for k in range(nk):
                    load(lambda h: w[k * P:(k + 1) * P, h * HALF:(h + 1) * HALF],
                         lambda s, h: ring[:, s, h, :], c["unit"])
                    c.up("unit")

            def compress(w):
                for kind in range(2):
                    for u in range(4):
                        load(lambda h: w[:, kind, 8 * u + 4 * h:8 * u + 4 * h + 4, :],
                             lambda s, h: ring[:, s, h, :].rearrange("p (l e) -> p l e", e=P), c["unit"])
                        c.up("unit")

            sp.wait_ge(mem_in, 2 * LOADED)
            for kind, *arg in stages:
                if kind == "mem_kv":
                    linear(a["w_mem_kv"][arg[0]], 2 * MEMW)
                elif kind == "ffn":
                    i, j = arg
                    up(a["ffn_w_gate_up"][i, j], FF1 // SEQ, True)
                    down(a["ffn_w_down"][i, j], FF1 // P)
                elif kind == "mlp":
                    up(a["mlp_w_up_2"][arg[0]], FF2 // HALF, False)
                    down(a["mlp_w_down_2"][arg[0]], FF2 // P)
                elif kind == "mix_a":
                    linear(a["a_w_in"][arg[1]], A_IN)
                    down(a["a_w_out"][arg[1]], KT)
                elif kind == "mix_b":
                    linear(a["b_w_in"][0], B_IN)
                    down(a["b_w_out"][0], B_OUT // P)
                elif kind == "mix_c":
                    linear(a["c_w_in"][0], C_IN)
                    down(a["c_w_out"][0], KT)
                elif kind == "nsa":
                    for d in NSA_ORDER:
                        plain_chunk(a["nsa_w_in_2"][0], d * HALF, min(HALF, NSA_IN - d * HALF), c["unit"])
                        c.up("unit", CHUNK_UNITS)
                    compress(a["nsa_w_cmp_l"])
                    down(a["nsa_w_out_2"][0], KT)
                elif kind == "stick":
                    linear(a["sb_w_in_2"][0], 3 * D)
                    down(a["sb_w_out_2"][0], KT)
                elif kind == "conv":
                    for d in CONV_ORDER:
                        plain_chunk(a["conv_w_in_2"][0], d * HALF, HALF, c["unit"])
                        c.up("unit", CHUNK_UNITS)
                    down(a["conv_w_out_2"][0], KT)
                elif kind == "moba":
                    linear(a["moba_w_in_2"][0], 3 * D)
                    down(a["moba_w_out_2"][0], KT)
            for t in range(TT):
                sp.wait_ge(x_ready, (stages_x - 1) * TT + t + 1)
                sp.dma_start(out[0, t * P:(t + 1) * P, :], x[:, t, :]).then_inc(out_done, LOADED)
            sp.wait_ge(out_done, TT * LOADED)

        def mem_heads(off, y_off):
            return [dict(q=off + h * DH1, k=("memkv", h * DH1), v=("memkv", MEMW + h * DH1), dh=DH1,
                         mask=None, y=y_off + h * DH1, scale=SCALE1) for h in range(MEM_HEADS)]

        def plan(kind):
            if kind == "mix_a":
                return mem_heads(2 * MIX, MIX)
            if kind == "mix_b":
                hs = [dict(q=h * DH1, k=("proj", MIX + h * DH1), v=("proj", 2 * MIX + h * DH1), dh=DH1,
                           mask=("band", "dil4", "dil16")[h // 4], y=h * DH1, scale=SCALE1, part=True)
                      for h in range(HEADS1)]
                return hs + mem_heads(3 * MIX, DIL_OUT)
            if kind == "mix_c":
                hs = [dict(q=h * DH1, k=("proj", MIX + h * DH1), v=("proj", 2 * MIX + h * DH1), dh=DH1,
                           mask="causal", y=h * DH1, scale=SCALE1, forget=h) for h in range(HEADS1)]
                return hs + mem_heads(3 * MIX + HEADS1, MIX)
            if kind == "moba":
                return [dict(q=h * DH2, k=("proj", D + h * DH2), v=("proj", 2 * D + h * DH2), dh=DH2,
                             mask="causal", y=h * DH2, scale=SCALE2) for h in range(H2)]
            if kind == "nsa":
                hs = []
                kvw = KVG * DH2
                for h in range(H2):
                    g = h // HPG
                    hs.append(dict(q=h * DH2, k=("cmp", g), v=("cmp", g), dh=DH2, mask="cmp", y=h * DH2,
                                   scale=SCALE2, gate=h, first=True))
                    for n, br in ((2, 1), (4, 2)):
                        hs.append(dict(q=h * DH2, k=("proj", D + n * kvw + g * DH2),
                                       v=("proj", D + (n + 1) * kvw + g * DH2), dh=DH2, mask="causal",
                                       y=h * DH2, scale=SCALE2, gate=br * H2 + h, first=False))
                return hs

        def rows_of(where, t, dh):
            buf, off = where
            return {"proj": proj, "memkv": memkv}[buf][:, t, off:off + dh]

        @block.tensor
        def _(pe):
            c = Counts()
            mm = nc.tensor.matmul

            def t_open(n, step=0, i=0):
                if n >= 2:
                    pe.wait_ge(t_taken[n % 2], n // 2 + (step // 2) * i)
                return T[n % 2]

            def transposes(tiles, n, step=0, i=0):
                bank, at = t_open(n, step, i), 0
                for k, src in enumerate(tiles):
                    m = src.shape[1]
                    last = nc.tensor.transpose(bank[0:m, at:at + P], src, ident)
                    at += P
                last.then_inc(t_full, 1)

            def turn_rows(t, rows, n_tiles):
                for b in range(n_tiles // 4):
                    transposes([rows[:, t, (4 * b + j) * P:(4 * b + j + 1) * P] for j in range(4)], c["T"])
                    c.up("T")

            def copied(n):
                pe.wait_ge(t_taken[n % 2], n // 2 + 1)

            def unit_split(m, step=0, i=0):
                if m in by_pool:
                    pe.wait_ge(pool_lo_ready, c.up("pool_lo"))
                else:
                    pe.wait_ge(lo_ready, lo_no[m] + 1 + step * i)

            ACT_PAIR, MEM_PAIR, HID_PAIR = (act_hi, act_lo), (memn_hi, memn_lo), (hid_hi, hid_lo)

            def hi_products(dst, lhs, kt, ts, slot, k, w, start):
                mm(dst, lhs[0][:, kt, ts], ring_hi[:, slot, k, 0:w], start=start, stop=False)
                mm(dst, lhs[0][:, kt, ts], ring_lo[:, slot, k, 0:w], start=False, stop=False)

            def lo_product(dst, lhs, kt, ts, slot, k, w, stop):
                return mm(dst, lhs[1][:, kt, ts], ring_hi[:, slot, k, 0:w], start=False, stop=stop)

            def half_chunk(lhs, t, par, width, n, g_wait, step=0, i=0, lo_later=False):
                ts, dst = slice(t * P, (t + 1) * P), G[:, t, par, 0:width]
                pe.wait_ge(g_taken[t], g_wait)
                for u in range(CHUNK_UNITS):
                    slot = (n + u) % RING
                    if t == 0:
                        unit_split(n + u, step, i)
                    if lo_later and u == CHUNK_UNITS // 2:
                        pe.wait_ge(act_hi_in, c["act_hi"])
                    for k in range(UNIT_K):
                        kt = UNIT_K * u + k
                        hi_products(dst, lhs, kt, ts, slot, k, width, kt == 0)
                        if not lo_later:
                            last = lo_product(dst, lhs, kt, ts, slot, k, width, kt == KT - 1)
                    if t == TT - 1 and not lo_later:
                        last.then_inc(unit_used, 1)
                if lo_later:
                    copied(c["T"] - 2)
                    copied(c["T"] - 1)
                    for kt in range(KT):
                        last = lo_product(dst, lhs, kt, ts, (n + kt // UNIT_K) % RING, kt % UNIT_K, width,
                                          kt == KT - 1)
                        if t == TT - 1 and kt % UNIT_K == UNIT_K - 1:
                            last.then_inc(unit_used, 1)
                if t == 0:
                    last.then_inc(first_done, 1)

            def chunk(lhs, par, width, n, g_wait, step=0, i=0):
                for t in range(TT):
                    half_chunk(lhs, t, par, width, n, g_wait, step, i)

            def opening(n, g):
                for t in range(TT):
                    normed(t)
                    for d in range(2):
                        half_chunk(ACT_PAIR, t, d, HALF, n + d * CHUNK_UNITS, g + max(d - 1, 0),
                                   lo_later=(d == 0))

            def normed(t):
                pe.wait_ge(nrm_ready, c.up("nrm"))
                turn_rows(t, nrm, KT)
                pe.wait_ge(act_hi_in, c.up("act_hi", 2) - 1)

            def linear(lhs, width, start=2, after={}):
                n, g = c["unit"], c["g"]
                full = width // HALF
                widths = [w for _, w in chunks_of(width)]
                if start:
                    opening(n, g)
                pairs = (full - start) // 2
                if pairs > 1:
                    with pe.Fori(0, pairs) as i:
                        for d in (start, start + 1):
                            chunk(lhs, d % 2, HALF, n + d * CHUNK_UNITS, g + max(d - 1, 0) + 2 * i, RING, i)
                for d in range(start + (2 * pairs if pairs > 1 else 0), len(widths)):
                    chunk(lhs, d % 2, widths[d], n + d * CHUNK_UNITS, g + max(d - 1, 0))
                    if d in after:
                        after[d]()
                c["unit"] = n + len(widths) * CHUNK_UNITS
                c["g"] = g + len(widths)

            def turn_hidden(par, paired, n, step, i, g_wait):
                for t in range(TT):
                    pe.wait_ge(g_taken[t], g_wait)
                for b in range(1 if paired else 2):
                    transposes([hid[:, par, t, (2 * b + f) * P:(2 * b + f + 1) * P]
                                for f in range(2) for t in range(TT)], n + b, step, i)

            def up_down(n_chunks, paired, nk):
                n, g = c["unit"], c["g"]
                opening(n, g)
                tb = c["T"]
                per = 1 if paired else 2
                turn_hidden(0, paired, tb, 0, 0, g + 1)
                pairs = (n_chunks - 2) // 2
                with pe.Fori(0, pairs) as i:
                    for d in (2, 3):
                        chunk(ACT_PAIR, d % 2, HALF, n + d * CHUNK_UNITS, g + d - 1 + 2 * i, RING, i)
                        turn_hidden((d - 1) % 2, paired, tb + (d - 1) * per, 2 * per, i, g + d + 2 * i)
                if n_chunks % 2:
                    d = n_chunks - 1
                    chunk(ACT_PAIR, d % 2, HALF, n + d * CHUNK_UNITS, g + d - 1)
                    turn_hidden((d - 1) % 2, paired, tb + (d - 1) * per, 0, 0, g + d)
                d = n_chunks - 1
                c["unit"] = n + n_chunks * CHUNK_UNITS
                c["g"] = g + n_chunks

                def late():
                    turn_hidden(d % 2, paired, tb + d * per, 0, 0, g + n_chunks)
                c["T"] = tb + n_chunks * per
                down(HID_PAIR, nk, late, tb)

            def down(lhs, nk, late=None, first_bank=None):
                n = c["unit"]
                grp = 0
                for size in down_groups(nk):
                    ks = range(grp, grp + size)
                    for t in range(TT):
                        if grp == 0:
                            pe.wait_ge(g_taken[t], c["g"])
                        if t == 0 and (late or grp == 0):
                            uses = first_bank + (ks[-1] + 2) // 2 if late else c["T"]
                            for b in range(2):
                                pe.wait_ge(t_taken[b], (uses + 1 - b) // 2)
                        for k in ks:
                            m = n + k
                            ts = slice(t * P, (t + 1) * P)
                            if t == 0:
                                unit_split(m)
                            for h in range(2):
                                hi_products(G[:, t, h, :], lhs, k, ts, m % RING, h, HALF, k == 0)
                                last = lo_product(G[:, t, h, :], lhs, k, ts, m % RING, h, HALF, k == nk - 1)
                            if t == TT - 1:
                                last.then_inc(unit_used, 1)
                        if t == 0 and ks[-1] == nk - 1:
                            last.then_inc(first_done, 1)
                    if grp == 0 and late:
                        late()
                    grp += size
                c.up("unit", nk)
                c.up("g")

            def proj_complete():
                for t in range(TT):
                    pe.wait_ge(g_taken[t], c["g"])

            def mixer_out(nk):
                for t in range(TT):
                    turn_rows(t, ymix, nk)
                down(HID_PAIR, nk)

            def attention(heads):
                base = c["att"]
                n_heads = len(heads)
                turned_qk, turned_p = [], []

                def turn_qk(j):
                    h = heads[j]
                    tiles = [proj[:, t, h["q"]:h["q"] + h["dh"]] for t in range(TT)]
                    if h["k"][0] != "cmp":
                        tiles += [rows_of(h["k"], t, h["dh"]) for t in range(TT)]
                    transposes(tiles, c["T"])
                    turned_qk.append(c["T"])
                    c.up("T")

                def score(j):
                    h, b, dh = heads[j], j % 2, heads[j]["dh"]
                    copied(turned_qk[j])
                    if base + j >= 1:
                        pe.wait_ge(s_taken, base + j)
                    for t in range(TT):
                        q = qk[0:dh, b, t * P:(t + 1) * P]
                        if h["k"][0] == "cmp":
                            last = mm(S[:, t, 0:N_CMP], q, kc_t[:, h["k"][1], :], start=True, stop=True,
                                      skip_group_check=True)
                            continue
                        f = h.get("forget")
                        last = mm(S[:, t, :], q, qk[0:dh, b, TT * P:2 * TT * P], start=(t == 0),
                                  stop=(f is None), skip_group_check=True)
                        if f is not None:
                            for st in range(TT):
                                n = SEQ - st * P
                                last = mm(S[:, t, st * P:SEQ], fgt_rows[:, st, f:f + 1].to_broadcast([P, P]),
                                          upto[:, 0:n], start=False, stop=(st == TT - 1), skip_group_check=True)
                    last.then_inc(s_full, 1)

                def turn_p(j):
                    h, b = heads[j], j % 2
                    pe.wait_ge(p_ready, base + j + 1)
                    if h["k"][0] == "cmp":
                        tiles = [pr[:, b, t, 0:N_CMP] for t in range(TT)]
                    elif h["mask"]:
                        tiles = [pr[:, b, 0, 0:P], pr[:, b, 1, 0:P], pr[:, b, 1, P:SEQ]]
                    else:
                        tiles = [pr[:, b, t, kt * P:(kt + 1) * P] for kt in range(2) for t in range(TT)]
                    transposes(tiles, c["T"])
                    turned_p.append(c["T"])
                    c.up("T")

                def weigh(j):
                    h, b, dh = heads[j], j % 2, heads[j]["dh"]
                    copied(turned_p[j])
                    if base + j >= 1:
                        pe.wait_ge(o_taken, base + j)
                    for t in range(TT):
                        if h["k"][0] == "cmp":
                            last = mm(O[:, t, 0:dh], pt[0:N_CMP, b, t * P:(t + 1) * P],
                                      vc[0:N_CMP, h["v"][1], :], start=True, stop=True, skip_group_check=True)
                            continue
                        kts = [0] if h["mask"] and t == 0 else [0, 1]
                        for kt in kts:
                            at = (0, P, 2 * P)[t + kt] if h["mask"] else (kt * TT + t) * P
                            last = mm(O[:, t, 0:dh], pt[:, b, at:at + P], rows_of(h["v"], kt, dh),
                                      start=(kt == 0), stop=(kt == kts[-1]), skip_group_check=True)
                    last.then_inc(o_full, 1)

                for step in range(n_heads + 4):
                    if step < n_heads:
                        turn_qk(step)
                    if 0 <= step - 3 < n_heads:
                        turn_p(step - 3)
                    if 0 <= step - 1 < n_heads:
                        score(step - 1)
                    if 0 <= step - 4 < n_heads:
                        weigh(step - 4)
                c["att"] = base + n_heads
                pe.wait_ge(o_taken, c["att"])

            fgt_rows = fgt[:, 3, :, :]

            def prepared():
                pe.wait_ge(prep_ready, c.up("prep"))

            def mix_a():
                linear(ACT_PAIR, A_IN)
                prepared()
                proj_complete()
                for g in range(HEADS1):
                    last = mm(gflat[:, g * P:(g + 1) * P].rearrange("p (t d) -> p t d", t=TT),
                              spat_w[:, g, :], scratch_v[:, :, g * DH1:(g + 1) * DH1],
                              start=True, stop=True, skip_group_check=True)
                last.then_inc(mix_full, 1)
                attention(plan("mix_a"))
                mixer_out(KT)

            def mix_bc(kind):
                linear(ACT_PAIR, WIDTH[kind])
                prepared()
                proj_complete()
                attention(plan(kind))
                if kind == "mix_b":
                    pe.wait_ge(mix_ready, c.up("mix"))
                mixer_out(OUT_K[kind])

            def nsa():
                kvw = KVG * DH2

                def turn_kv():
                    prepared()
                    for s in range(2):
                        transposes([proj[:, t, D + s * kvw + g * DH2:D + s * kvw + (g + 1) * DH2]
                                    for g in range(KVG) for t in range(TT)], c["T"])
                        c.up("T")
                linear(ACT_PAIR, NSA_IN, after={2: turn_kv})
                prepared()
                proj_complete()
                n = c["unit"]
                for s in range(2):
                    for u in range(4):
                        m = n + 4 * s + u
                        pe.wait_ge(unit_full[m % RING], 2 * LOADED * (m // RING + 1))
                        for h in range(2):
                            for j in range(4):
                                l = 8 * u + 4 * h + j
                                w = ring[:, m % RING, h, j * P:(j + 1) * P]
                                if s == 0:
                                    last = mm(S[:, 0, 0:KVG * N_CMP], w,
                                              cmp_in[:, 0, l, :, :].rearrange("p g n -> p (g n)"),
                                              start=(l == 0), stop=(l == CMP_L - 1))
                                else:
                                    for g in range(KVG):
                                        last = mm(G[0:N_CMP, g, 0, 0:DH2], cmp_in[:, 1, l, g, :], w,
                                                  start=(l == 0), stop=(l == CMP_L - 1))
                        last.then_inc(unit_used, 1)
                c["unit"] = n + 8
                prepared()
                attention(plan("nsa"))
                mixer_out(KT)

            def stick():
                linear(ACT_PAIR, 3 * D)
                proj_complete()
                base = c["att"]

                def scores(hs):
                    for h in hs:
                        transposes([proj[:, t, o + h * DH2:o + (h + 1) * DH2] for o in (0, D) for t in range(TT)],
                                   c["T"])
                        c.up("T")
                    for j, h in enumerate(hs):
                        copied(c["T"] - 2 + j)
                        if base + h:
                            pe.wait_ge(s_taken, base + h)
                        for st in range(TT):
                            last = mm(S[:, st, :], qk[:, j, (TT + st) * P:(TT + st + 1) * P], qk[:, j, 0:TT * P],
                                      start=(st == 0), stop=True, skip_group_check=True)
                        last.then_inc(s_full, 1)

                scores((0, 1))
                for pair in range(H2 // 2):
                    hs = [2 * pair, 2 * pair + 1]
                    for j, h in enumerate(hs):
                        prepared()
                        mm(G[:, j, 0, 0:SEQ], from_on, pt[:, j, 0:SEQ], start=True, stop=False)
                        mm(G[:, j, 0, 0:SEQ], ones, pt[:, j, SEQ:2 * SEQ], start=False, stop=True)
                        last = mm(G[:, j, 1, 0:SEQ], from_on, pt[:, j, SEQ:2 * SEQ], start=True, stop=True)
                        last.then_inc(mix_full, 1)
                    if pair < H2 // 2 - 1:
                        scores((2 * pair + 2, 2 * pair + 3))
                    for j, h in enumerate(hs):
                        pe.wait_ge(p_ready, base + h + 1)
                        if base + h:
                            pe.wait_ge(o_taken, base + h)
                        for t in range(TT):
                            for st in range(t + 1):
                                last = mm(O[:, t, 0:DH2], pr[:, j, st, t * P:(t + 1) * P],
                                          proj[:, st, 2 * D + h * DH2:2 * D + (h + 1) * DH2],
                                          start=(st == 0), stop=(st == t), skip_group_check=True)
                        last.then_inc(o_full, 1)
                c["att"] = base + H2
                pe.wait_ge(o_taken, c["att"])
                mixer_out(KT)

            def conv():
                def turn_gated(half):
                    for t in range(TT):
                        prepared()
                        transposes([ymix[:, t, (4 * half + j) * P:(4 * half + j + 1) * P] for j in range(4)], c["T"])
                        c.up("T")
                linear(ACT_PAIR, 2 * D, after={2: lambda: turn_gated(0)})
                proj_complete()
                for g, (k, first, n) in enumerate(diag_groups):
                    if first == 0 and k in (CONV_PE, 4):
                        copied(c["T"] - 2)
                        copied(c["T"] - 1)
                    pe.wait_ge(diag_ready, g + 1)
                    j = k - CONV_PE
                    for i in range(n):
                        tap = first + i
                        last = mm(conv_sums[j], diags[:, g % 2, i, :], conv_in[:, k, tap:tap + SEQ],
                                  start=(tap == 0), stop=(tap == CONV_W - 1))
                    last.then_inc(mix_full, 1)
                    if g == 0:
                        turn_gated(1)
                prepared()
                pe.wait_ge(conv_ready, KT - CONV_PE)
                for t in range(TT):
                    for b in range(2):
                        transposes([conv_acc[:, 4 * b + j, t * P:(t + 1) * P] for j in range(4)], c["T"])
                        c.up("T")
                for t in range(TT):
                    pe.wait_ge(mix_ready, c.up("mix"))
                    turn_rows(t, ymix, KT)
                down(HID_PAIR, KT)

            pe.wait_ge(consts_in, LOADED)
            for t in range(TT):
                pe.wait_ge(nrm_ready, c.up("nrm"))
                turn_rows(t, nrm, KT)
            c["g"] = 1
            for kind, *arg in stages:
                if kind == "mem_kv":
                    pe.wait_ge(memn_ready, c.up("memn"))
                    linear(MEM_PAIR, 2 * MEMW, start=0)
                elif kind == "ffn":
                    up_down(FF1 // SEQ, True, FF1 // P)
                elif kind == "mlp":
                    up_down(FF2 // HALF, False, FF2 // P)
                elif kind == "mix_a":
                    mix_a()
                elif kind in ("mix_b", "mix_c", "moba"):
                    mix_bc(kind)
                elif kind == "nsa":
                    nsa()
                elif kind == "stick":
                    stick()
                elif kind == "conv":
                    conv()

        @block.scalar
        def _(act):
            c = Counts()
            fn = nc.scalar.activation

            def products(t):
                if t == 0:
                    act.wait_ge(first_done, c.up("chunk"))
                else:
                    act.wait_ge(unit_used, c["unit"])

            def link(ins):
                ins.then_inc(a_link, 1)
                act.wait_ge(a_link, c.up("link"))

            def t_read(n, step=0, i=0):
                act.wait_ge(t_full, n + 1 + step * i)
                return T[n % 2]

            def copy_t(dst, src, n, step=0, i=0):
                fn(dst, src, ACT.Copy).then_inc(t_taken[n % 2], 1)

            def split_one(m, step=0, i=0):
                s_, w = m % RING, unit_cols[m]
                act.wait_ge(unit_full[s_], 2 * LOADED * (m // RING + 1) + 2 * LOADED * (step // RING) * i)
                fn(ring_hi[:, s_, :, 0:w], ring[:, s_, :, 0:w], ACT.Copy).then_inc(hi_ready, 1)

            def ahead(limit):
                split_ahead(act, c, split_one, limit)

            last_square = []

            def square(src, w, done_, accum, t=0):
                if last_square:
                    act.wait_ge(*last_square)
                fn(nrm[:, t, 0:w], src, ACT.Square, **accum).then_inc(done_, 1)
                last_square[:] = [done_, c.up(done_.name)]

            def norm_x(t, first=False, early=False):
                if not first:
                    act.wait_ge(x_ready, c.up("x"))
                square(x[:, t, :], D, ssx_ready, dict(accum_out=sums[:, 2 + t:3 + t]), t)
                if early:
                    ahead(c["unit"] + 3)
                act.wait_ge(rx_ready, c.up("rx"))
                fn(nrm[:, t, :], x[:, t, :], ACT.Copy, scale=small[:, 2 + t:3 + t]).then_inc(nrm_ready, 1)

            def residual(post, last):
                c.up("g")
                for t in range(TT):
                    if post:
                        products(t)
                        square(G[:, t, :, :].rearrange("p h n -> p (h n)"), D, ssy_ready,
                               dict(accum_out=sums[:, t:t + 1]), t)
                    elif t == 0:
                        c.up("chunk")
                    if t:
                        ahead(c["unit"] + RING)
                    if not last:
                        norm_x(t, early=post and t == 0)
                    if t == 0:
                        ahead(c["unit"] + CHUNK_UNITS)

            def up(n_chunks, paired):
                n, ch, tb = c["unit"], c["chunk"], c["T"]
                per = 1 if paired else 2
                f = ACT.Silu if paired else ACT.Relu
                w = SEQ if paired else HALF

                def gate(par, d, step=0, i=0):
                    act.wait_ge(first_done, ch + d + 1 + (step // CHUNK_UNITS) * i)
                    fn(gated[:, par, 0, 0:w], G[:, 0, par, 0:w], f).then_inc(gated_ready, 1)
                    act.wait_ge(unit_used, n + (d + 1) * CHUNK_UNITS + step * i)
                    fn(gated[:, par, 1, 0:w], G[:, 1, par, 0:w], f).then_inc(gated_ready, 1)

                def copies(d, step=0, i=0):
                    for b in range(per):
                        m = tb + d * per + b
                        bank = t_read(m, step, i)
                        at = (d * per + b) * 2 + step * 2 * i
                        fn(hid_hi[:, bass.ds(at, 2), :], bank[:, :].rearrange("p (k s) -> p k s", k=2), ACT.Copy)\
                            .then_inc(turn_hi, 1)

                def split_chunk(d, step=0, i=0):
                    for u in range(CHUNK_UNITS):
                        split_one(n + d * CHUNK_UNITS + u, step, i)

                ahead(n + RING)
                gate(0, 0)
                split_chunk(2)
                pairs = (n_chunks - 1) // 2
                with act.Fori(0, pairs) as i:
                    for d in (1, 2):
                        gate(d % 2, d, RING, i)
                        copies(d - 1, 2 * per, i)
                        split_chunk(d + 2, RING, i)
                if (n_chunks - 1) % 2:
                    gate((n_chunks - 1) % 2, n_chunks - 1)
                    copies(n_chunks - 2)
                    split_chunk(n_chunks + 1)
                copies(n_chunks - 1)
                c["split"] = n + (n_chunks + 2) * CHUNK_UNITS
                c["unit"], c["chunk"], c["T"] = n + n_chunks * CHUNK_UNITS, ch + n_chunks, tb + n_chunks * per
                c.up("g", n_chunks)

            def linear(width, after={}, lead=3):
                nch = len(chunks_of(width))
                for d in sorted(after):
                    ahead(c["unit"] + (d + lead) * CHUNK_UNITS)
                    for t in range(TT):
                        act.wait_ge(g_taken[t], c["g"] + d + 1)
                    after[d]()
                c.up("unit", nch * CHUNK_UNITS)
                ahead(c["unit"] + CHUNK_UNITS)
                c.up("chunk", nch)
                c.up("g", nch)

            def normed():
                c.up("T", 4)

            def turn_out(nk):
                for t in range(TT):
                    for b in range(nk // 4):
                        n = c["T"]
                        bank = t_read(n)
                        fn(hid_hi[:, 4 * b:4 * b + 4, t * P:(t + 1) * P],
                           bank[:, :].rearrange("p (k n) -> p k n", k=4), ACT.Copy).then_inc(turn_hi, 1)
                        c.up("T")
                c.up("unit", nk)

            def attention(heads, after=None):
                target = c["unit"] + RING
                base = c["att"]
                n_heads = len(heads)

                def copy_qk(j):
                    h, n = heads[j], c["T"]
                    w = TT * P if h["k"][0] == "cmp" else 2 * TT * P
                    bank = t_read(n)
                    copy_t(qk[0:h["dh"], j % 2, 0:w], bank[0:h["dh"], 0:w], n)
                    c.up("T")

                def exps(j):
                    h, b = heads[j], j % 2
                    act.wait_ge(mx_ready, base + j + 1)
                    w = N_CMP if h["k"][0] == "cmp" else SEQ
                    for t in range(TT):
                        col = TT * j + t
                        last = fn(pr[:, b, t, 0:w], sc[:, b, t, 0:w], ACT.Exp, bias=mx[:, col:col + 1],
                                  accum_out=den[:, col:col + 1])
                    last.then_inc(p_ready, 1)

                def copy_p(j):
                    h, n = heads[j], c["T"]
                    bank = t_read(n)
                    r, w = (N_CMP, 2 * P) if h["k"][0] == "cmp" else (P, 3 * P if h["mask"] else 4 * P)
                    copy_t(pt[0:r, j % 2, 0:w], bank[0:r, 0:w], n)
                    c.up("T")

                for step in range(n_heads + 4):
                    if step < n_heads:
                        copy_qk(step)
                    if 0 <= step - 3 < n_heads:
                        copy_p(step - 3)
                    if 0 <= step - 1 < n_heads:
                        exps(step - 1)
                    ahead(min(c["split"] + 1, target))
                    if after and step == HEADS1 + 3:
                        after()
                ahead(target)
                c["att"] = base + n_heads

            def head_squares(kind):
                def one(b, c0, nh, t):
                    if last_square:
                        act.wait_ge(*last_square)
                    for h in range(nh):
                        at = c0 + h * DH2
                        ins = fn(nrm[:, t, h * DH2:(h + 1) * DH2], proj[:, t, at:at + DH2], ACT.Square,
                                 accum_out=head_sum[:, b // TT, t * H2 + h:t * H2 + h + 1])
                    ins.then_inc(sq_ready, 1)
                    last_square[:] = [sq_ready, c.up("sq_ready")]

                def scale(b, c0, nh, t):
                    act.wait_ge(small_ready, c.up("small_ready"))
                    for h in range(nh):
                        blk = proj[:, t, c0 + h * DH2:c0 + (h + 1) * DH2]
                        ins = fn(blk, blk, ACT.Copy, scale=head_rs[:, b // TT, t * H2 + h:t * H2 + h + 1])
                    ins.then_inc(head_ready, 1)
                hooks = {}
                for b, (d, c0, nh, _, t) in enumerate(head_blocks(kind)):
                    hooks.setdefault(d, []).append((b, c0, nh, t))

                def run(todo):
                    return lambda: [f(*blk) for f in (one, scale) for blk in todo]
                return {d: run(todo) for d, todo in hooks.items()}

            def proj_complete():
                for t in range(TT):
                    act.wait_ge(g_taken[t], c["g"])

            def gelus():
                for cols in (slice(MIX, 2 * MIX), slice(0, MIX)):
                    for t in range(TT):
                        fn(proj[:, t, cols], proj[:, t, cols], ACT.Gelu_apprx_tanh).then_inc(gelu_ready, 1)

            def mix_a():
                normed()
                linear(A_IN, {2: gelus}, lead=2)
                c.up("small_ready", TT)
                attention(plan("mix_a"))
                turn_out(KT)

            mem_rows = proj[:, :, 0:D]
            act.dma_start(mem_rows, a["mem"][0].rearrange("(t p) d -> p t d", p=P)).then_inc(mem_in, LOADED)
            act.dma_start(mem_cols[:, :, :], a["mem_cols"]).then_inc(mem_in, LOADED)
            act.dma_start(con[:, :], a["consts"]).then_inc(consts_in, LOADED)
            act.dma_start(x[:, :, :], a["x"][0].rearrange("(t p) d -> p t d", p=P)).then_inc(x_in, LOADED)
            act.wait_ge(mem_in, 2 * LOADED)
            for t in range(TT):
                square(mem_rows[:, t, :], D, ssy_ready, dict(accum_out=sums[:, t:t + 1]), t)
                act.wait_ge(ry_ready, t + 1)
                fn(nrm[:, t, :], mem_rows[:, t, :], ACT.Copy, scale=small[:, t:t + 1]).then_inc(nrm_ready, 1)
            for t in range(TT):
                for b in range(2):
                    n = c["T"]
                    bank = t_read(n)
                    copy_t(mem_t[:, 4 * b:4 * b + 4, t * P:(t + 1) * P], bank[:, :].rearrange("p (k n) -> p k n", k=4), n)
                    c.up("T")
            ahead(CHUNK_UNITS)
            act.wait_ge(x_in, LOADED)
            for t in range(TT):
                norm_x(t, first=True)
            c["g"] = 1
            ahead(RING)
            act.wait_ge(fn_in, c.up("fn_in"))
            for j in range(2):
                fn(rope1[:, j, :, :], rtmp[:, 2 + j, :, :], ACT.Sin).then_inc(fn_out, 1)

            n_stage = len(stages)
            for s, (kind, *arg) in enumerate(stages):
                last = s == n_stage - 1
                if kind == "mem_kv":
                    linear(2 * MEMW)
                    continue
                if kind in ("ffn", "mlp"):
                    normed()
                    if kind == "ffn":
                        up(FF1 // SEQ, True)
                        c.up("unit", FF1 // P)
                    else:
                        up(FF2 // HALF, False)
                        c.up("unit", FF2 // P)
                    ahead(c["unit"] - last_group(FF1 // P if kind == "ffn" else FF2 // P) + RING)
                elif kind == "mix_a":
                    mix_a()
                elif kind == "mix_b":
                    normed()
                    linear(B_IN)

                    def group_shares():
                        act.wait_ge(fn_in, c.up("fn_in"))
                        fn(shares[:, 0, :], den[:, 0:TT * HEADS1], ACT.Ln).then_inc(fn_out, 1)
                        act.wait_ge(fn_in, c.up("fn_in"))
                        fn(shares[:, 2, :], shares[:, 1, :], ACT.Exp).then_inc(fn_out, 1)
                    attention(plan("mix_b"), group_shares)
                    turn_out(B_OUT // P)
                elif kind == "mix_c":
                    normed()
                    linear(C_IN)
                    act.wait_ge(fn_in, c.up("fn_in"))
                    link(fn(fgt[:, 2, :, :], fgt[:, 1, :, :], ACT.Exp))
                    fn(fgt[:, 1, :, :], fgt[:, 2, :, :], ACT.Ln, bias=1.0).then_inc(fn_out, 1)
                    attention(plan("mix_c"))
                    turn_out(KT)
                elif kind == "moba":
                    normed()
                    linear(3 * D, head_squares("moba"))
                    attention(plan("moba"))
                    turn_out(KT)
                elif kind == "nsa":
                    normed()
                    hooks = head_squares("nsa")

                    def copy_kv():
                        hooks[2]()
                        for s2 in range(2):
                            n = c["T"]
                            bank = t_read(n)
                            copy_t(kv_t[:, s2, :, :].rearrange("p g n -> p (g n)"), bank[:, :], n)
                            c.up("T")
                    linear(NSA_IN, {**hooks, 2: copy_kv})
                    proj_complete()
                    fn(gates[:, :, :], proj[:, :, NSA_IN - 3 * H2:NSA_IN], ACT.Sigmoid).then_inc(fn_out, 1)
                    c.up("unit", 8)
                    attention(plan("nsa"))
                    turn_out(KT)
                elif kind == "stick":
                    normed()
                    linear(3 * D)

                    def pair_qk():
                        for j in range(2):
                            n = c["T"]
                            bank = t_read(n)
                            copy_t(qk[:, j, :], bank[:, :], n)
                            c.up("T")
                    pair_qk()
                    for pair in range(H2 // 2):
                        first = c["link"]
                        for j in range(2):
                            act.wait_ge(mx_ready, c.up("att"))
                            fn(pt[:, j, :], pt[:, j, :], ACT.Exp).then_inc(a_link, 1)
                        for j in range(2):
                            act.wait_ge(a_link, first + j + 1)
                            fn(pt[:, j, :], pt[:, j, :], ACT.Ln, bias=1.0).then_inc(fn_out, 1)
                        c["link"] = first + 2
                        if pair < H2 // 2 - 1:
                            pair_qk()
                        for j in range(2):
                            act.wait_ge(arg_ready, c.up("arg"))
                            fn(pr[:, j, :, :], pr[:, j, :, :], ACT.Exp).then_inc(p_ready, 1)
                        ahead(c["split"] + 1)
                    turn_out(KT)
                elif kind == "conv":
                    normed()

                    def sigmoids(half):
                        for t in range(TT):
                            cols = slice(D + half * HALF, D + (half + 1) * HALF)
                            fn(proj[:, t, cols], proj[:, t, cols], ACT.Sigmoid).then_inc(fn_out, 1)

                    def channels(half):
                        for t in range(TT):
                            n = c["T"]
                            bank = t_read(n)
                            copy_t(conv_in[:, 4 * half:4 * half + 4, PAD + t * P:PAD + (t + 1) * P],
                                   bank[:, :].rearrange("p (k n) -> p k n", k=4), n)
                            c.up("T")

                    def diagonal(g):
                        k, first, n = diag_groups[g]
                        if g >= 2:
                            act.wait_ge(mix_full, c["mixf"] + g - 1)
                        for i in range(n):
                            ins = fn(diags[:, g % 2, i, :], ident, ACT.Copy, scale=conv_taps[:, k, first + i:first + i + 1])
                        ins.then_inc(diag_ready, 1)

                    linear(2 * D, {1: lambda: sigmoids(0), 2: lambda: channels(0)}, lead=2)
                    diagonal(0)
                    proj_complete()
                    sigmoids(1)
                    diagonal(1)
                    channels(1)
                    ahead(c["unit"] + RING)
                    c.up("small_ready", TT)
                    per = -(-CONV_W // DIAGS)
                    c["mixf"] = H2 * sum(k == "stick" for k, *_ in stages[:s]) + sum(k == "mix_a" for k, *_ in stages[:s])
                    for g in range(2, len(diag_groups) + per):
                        if g < len(diag_groups):
                            diagonal(g)
                        if g % per == per - 1 and g >= 2 * per - 1:
                            k = CONV_PE + g // per - 1
                            j = k - CONV_PE
                            act.wait_ge(mix_full, c["mixf"] + g // per * per)
                            fn(conv_acc[:, k, :], conv_sums[j], ACT.Identity,
                               bias=conv_cols[:, 0, k:k + 1]).then_inc(conv_ready, 1)
                    for t in range(TT):
                        for b in range(2):
                            n = c["T"]
                            bank = t_read(n)
                            copy_t(nrm[:, t, b * HALF:(b + 1) * HALF], bank[:, :], n)
                            c.up("T")
                    for t in range(TT):
                        for b in range(2):
                            n = c["T"]
                            bank = t_read(n)
                            for j in range(4):
                                k = 4 * b + j
                                ins = fn(conv_out[:, k, t * P:(t + 1) * P], bank[:, j * P:(j + 1) * P], ACT.Silu,
                                         bias=conv_cols[:, 2, k:k + 1], scale=conv_cols[:, 1, k:k + 1])
                            ins.then_inc(gelu_ready, 1)
                            c.up("T")
                    c.up("unit", KT)
                if kind in MIXERS:
                    ahead(c["unit"] - last_group(OUT_K[kind]) + RING)
                residual(kind in ("ffn", "mix_a", "mix_b", "mix_c"), last)

        @block.vector
        def _(dve):
            c = Counts()
            v = nc.vector

            def products(t):
                if t == 0:
                    dve.wait_ge(first_done, c.up("chunk"))
                else:
                    dve.wait_ge(unit_used, c["unit"])

            def link(ins):
                ins.then_inc(v_link, 1)
                dve.wait_ge(v_link, c.up("link"))

            def split_one(m, step=0, i=0):
                if m in by_pool:
                    return
                s_, w = m % RING, unit_cols[m]
                dve.wait_ge(hi_ready, split_no[m] + 1 + step * i)
                v.tensor_tensor(ring_lo[:, s_, :, 0:w], ring[:, s_, :, 0:w], ring_hi[:, s_, :, 0:w],
                                ALU.subtract).then_inc(lo_ready, 1)

            def ahead(limit):
                split_ahead(dve, c, split_one, limit)

            def normed(s):
                cols = pre_gain(s)
                for t in range(TT):
                    ts = slice(t * P, (t + 1) * P)
                    for b in range(2):
                        n = c["T"] + b
                        dve.wait_ge(t_full, n + 1)
                        v.tensor_tensor(
                            act_hi[:, 4 * b:4 * b + 4, ts], T[n % 2][:, :].rearrange("p (k n) -> p k n", k=4),
                            cols[:, 4 * b:4 * b + 4].unsqueeze(2).to_broadcast([P, 4, P]), ALU.mult)\
                            .then_inc(act_hi_in, 1)
                    yield
                    for b in range(2):
                        n = c["T"]
                        dve.wait_ge(act_hi_in, c.up("act_hi"))
                        for j in range(4):
                            k = 4 * b + j
                            ins = v.scalar_tensor_tensor(act_lo[:, k, ts], T[n % 2][:, j * P:(j + 1) * P],
                                                         cols[:, k:k + 1], act_hi[:, k, ts], ALU.mult, ALU.subtract)
                        ins.then_inc(t_taken[n % 2], 1)
                        c.up("T")
                    yield

            def turned_lo(dst, hi, n, shape, step=0, i=0):
                dve.wait_ge(turn_hi, c["turn"] + 1 + step * i)
                v.tensor_tensor(dst, T[n % 2][:, :].rearrange("p (k s) -> p k s", k=shape), hi, ALU.subtract)\
                 .then_inc(t_taken[n % 2], 1)

            def turn_out(nk):
                for t in range(TT):
                    for b in range(nk // 4):
                        at = (slice(None), slice(4 * b, 4 * b + 4), slice(t * P, (t + 1) * P))
                        turned_lo(hid_lo[at], hid_hi[at], c["T"], 4)
                        c.up("turn")
                        c.up("T")

            def linear(width, dst, before=None, after={}, order=None, hook_first=()):
                plan_ = chunks_of(width)
                if order:
                    plan_ = [plan_[d] for d in order]
                ahead(c["unit"] + CHUNK_UNITS)
                if before is not None:
                    ahead(c["unit"] + RING)
                    next(before)
                    next(before)
                for d, (c0, w) in enumerate(plan_):
                    c.up("unit", CHUNK_UNITS)
                    for t in range(TT):
                        products(t)
                        v.tensor_copy(dst[:, t, c0:c0 + w], G[:, t, d % 2, 0:w]).then_inc(g_taken[t], 1)
                    if d < len(plan_) - 1 and d not in hook_first:
                        ahead(c["unit"] + RING)
                    if d in after:
                        after[d]()
                c.up("g", len(plan_))

            def up(s, n_chunks, paired):
                n, ch = c["unit"], c["chunk"]
                w = SEQ if paired else HALF
                lo = SEQ if paired else 0
                per = 1 if paired else 2
                before = started.pop(s)

                gr = c["gated"]

                def one(par, d, step=0, i=0):
                    for t in range(TT):
                        dve.wait_ge(gated_ready, gr + TT * d + t + 1 + (TT * step // CHUNK_UNITS) * i)
                        v.tensor_tensor(hid[:, par, t, 0:w], G[:, t, par, lo:lo + w], gated[:, par, t, 0:w],
                                        ALU.mult).then_inc(g_taken[t], 1)

                def lows(d, step=0, i=0):
                    for b in range(per):
                        at = (d * per + b) * 2 + step * 2 * i
                        dve.wait_ge(turn_hi, turn0 + d * per + b + 1 + step * i)
                        n_ = tb + d * per + b
                        v.tensor_tensor(hid_lo[:, bass.ds(at, 2), :], T[n_ % 2][:, :].rearrange("p (k s) -> p k s", k=2),
                                        hid_hi[:, bass.ds(at, 2), :], ALU.subtract).then_inc(t_taken[n_ % 2], 1)

                def split_chunk(d, step=0, i=0):
                    for u in range(CHUNK_UNITS):
                        split_one(n + d * CHUNK_UNITS + u, step, i)

                ahead(n + RING)
                next(before)
                next(before)
                tb, turn0 = c["T"], c["turn"]
                one(0, 0)
                split_chunk(2)
                pairs = (n_chunks - 1) // 2
                with dve.Fori(0, pairs) as i:
                    for d in (1, 2):
                        one(d % 2, d, RING, i)
                        lows(d - 1, 2 * per, i)
                        split_chunk(d + 2, RING, i)
                if (n_chunks - 1) % 2:
                    one((n_chunks - 1) % 2, n_chunks - 1)
                    lows(n_chunks - 2)
                    split_chunk(n_chunks + 1)
                lows(n_chunks - 1)
                c["split"] = n + (n_chunks + 2) * CHUNK_UNITS
                c["unit"], c["chunk"] = n + n_chunks * CHUNK_UNITS, ch + n_chunks
                c.up("T", n_chunks * per)
                c.up("turn", n_chunks * per)
                c.up("gated", TT * n_chunks)
                c.up("g", n_chunks)

            def memory(i):
                for k in range(KT):
                    ins = v.tensor_scalar(memn_hi[:, k, :], mem_t[:, k, :], mem_cols[:, i, k:k + 1], None, ALU.mult)
                link(ins)
                for k in range(KT):
                    ins = v.scalar_tensor_tensor(memn_lo[:, k, :], mem_t[:, k, :], mem_cols[:, i, k:k + 1],
                                                 memn_hi[:, k, :], ALU.mult, ALU.subtract)
                ins.then_inc(memn_ready, 1)

            started = {}

            def start(s):
                if s < len(stages) and stages[s][0] != "mem_kv":
                    started[s] = normed(s)
                    next(started[s])
                    ahead(c["unit"] + CHUNK_UNITS)
                    next(started[s])
                ahead(c["unit"] + CHUNK_UNITS + 1)

            def residual(s):
                post = stages[s][0] in POST
                c.up("g")
                for t in range(TT):
                    if t:
                        if post:
                            ahead(c["unit"] + 3)
                        start(s + 1)
                    y = G[:, t, :, :].rearrange("p h n -> p (h n)")
                    if post:
                        if t == 0:
                            c.up("chunk")
                            dve.wait_ge(row_full, LOADED * c.up("row"))
                        dve.wait_ge(ry_ready, c.up("ry"))
                        factor = post_gain(s)[2]
                        v.scalar_tensor_tensor(scratch_v[:, t, :], y, small[:, t:t + 1], gain_row[:, :],
                                               ALU.mult, ALU.mult).then_inc(g_taken[t], 1)
                        dve.wait_ge(g_taken[t], c["g"])
                        v.scalar_tensor_tensor(x[:, t, :], scratch_v[:, t, :], factor, x[:, t, :],
                                               ALU.mult, ALU.add).then_inc(x_ready, 1)
                    else:
                        products(t)
                        v.tensor_tensor(x[:, t, :], y, x[:, t, :], ALU.add).then_inc(x_ready, 1)
                        dve.wait_ge(x_ready, c["x"] + 1)
                        dve.sem_inc(g_taken[t], 1)
                    c.up("x")

            def attention(heads, after=None):
                base = c["att"]
                n_heads = len(heads)

                def score(j):
                    h, b = heads[j], j % 2
                    w = N_CMP if h["k"][0] == "cmp" else SEQ
                    dve.wait_ge(s_full, base + j + 1)
                    dst, src = sc[:, b, :, 0:w], S[:, :, 0:w]
                    if h["mask"]:
                        ins = v.scalar_tensor_tensor(dst, src, h["scale"], mask[h["mask"]], ALU.mult, ALU.add)
                    else:
                        ins = v.tensor_scalar(dst, src, h["scale"], None, ALU.mult)
                    ins.then_inc(s_taken, 1)
                    dve.wait_ge(s_taken, base + j + 1)
                    v.tensor_reduce(mx[:, TT * j:TT * j + TT], dst, AX_X, ALU.max, negate=True)\
                     .then_inc(mx_ready, 1)

                def place(j):
                    h, dh = heads[j], heads[j]["dh"]
                    dve.wait_ge(o_full, base + j + 1)
                    link(v.reciprocal(recip[:, :], den[:, TT * j:TT * j + TT]))
                    if "gate" in h:
                        link(v.tensor_tensor(recip[:, :], recip[:, :], gates[:, :, h["gate"]], ALU.mult))
                        if h["first"]:
                            link(v.tensor_tensor(recip[:, :], recip[:, :], cmp_any, ALU.mult))
                    y = parts_o if h.get("part") else ymix
                    at = h["y"]
                    if h.get("first", True):
                        ins = v.tensor_tensor(y[:, :, at:at + dh], O[:, :, 0:dh],
                                              recip[:, :].unsqueeze(2).to_broadcast([P, TT, dh]), ALU.mult)
                    else:
                        for t in range(TT):
                            ins = v.scalar_tensor_tensor(y[:, t, at:at + dh], O[:, t, 0:dh], recip[:, t:t + 1],
                                                         y[:, t, at:at + dh], ALU.mult, ALU.add)
                    ins.then_inc(o_taken, 1)
                    dve.wait_ge(o_taken, base + j + 1)

                target = c["unit"] + RING
                for step in range(n_heads + 4):
                    if 0 <= step - 1 < n_heads:
                        score(step - 1)
                    if 0 <= step - 4 < n_heads:
                        place(step - 4)
                    ahead(min(c["split"] + 1, target))
                    if after and step == HEADS1 + 3:
                        after()
                ahead(target)
                c["att"] = base + n_heads
                c.up("T", 2 * n_heads)

            def rope(block_, nh, ca, sa, cb, sb_):
                half = block_.shape[3]
                x1, x2 = block_[:, :, 0, :], block_[:, :, 1, :]
                tmp = scratch_v[:, :, :].rearrange("p a b -> p (a b)")[:, 0:4 * nh * half] \
                    .rearrange("p (k h n) -> p k h n", k=4, h=nh)

                def wide(tab):
                    return tab.unsqueeze(1).to_broadcast([P, nh, half])
                v.tensor_tensor(tmp[:, 0], x1, wide(ca), ALU.mult)
                v.tensor_tensor(tmp[:, 1], x2, wide(sa), ALU.mult)
                v.tensor_tensor(tmp[:, 2], x2, wide(cb), ALU.mult)
                link(v.tensor_tensor(tmp[:, 3], x1, wide(sb_), ALU.mult))
                v.tensor_tensor(x1, tmp[:, 0], tmp[:, 1], ALU.subtract)
                link(v.tensor_tensor(x2, tmp[:, 2], tmp[:, 3], ALU.add))

            def late():
                dve.wait_ge(late_in, LOADED * len(late_loads))

            def gain_tables(g):
                def half(n):
                    return head_gain[:, g, n * 64:(n + 1) * 64].unsqueeze(1).to_broadcast([P, TT, 64])
                v.tensor_tensor(tabs[:, 0], cos2, half(0), ALU.mult)
                v.tensor_tensor(tabs[:, 1], sin2, half(1), ALU.mult)
                v.tensor_tensor(tabs[:, 2], cos2, half(1), ALU.mult)
                link(v.tensor_tensor(tabs[:, 3], sin2, half(0), ALU.mult))

            def rs_wait():
                dve.wait_ge(small_ready, c.up("small"))

            def norm_rope(kind, wanted):
                blocks = head_blocks(kind)
                for b in wanted:
                    _, c0, nh, g, t = blocks[b]
                    late()
                    if c["gain"] != g + 1:
                        gain_tables(g)
                        c["gain"] = g + 1
                    dve.wait_ge(head_ready, c["head"] + b + 1)
                    if b == len(blocks) - 1:
                        c.up("head", len(blocks))
                        c.up("small", len(blocks))
                    rope(proj[:, t, c0:c0 + nh * DH2].rearrange("p (h two d) -> p h two d", h=nh, two=2), nh,
                         *[tabs[:, k, t, :] for k in range(4)])

            def done():
                dve.sem_inc(prep_ready, 1)

            def layer_stats(t, src, n, piece):
                k = n // piece
                for j in range(k):
                    ins = v.bn_stats(bn[:, t, 6 * j:6 * j + 6], src[:, j * piece:(j + 1) * piece])
                link(ins)
                v.bn_aggr(mean_var[:, t, :], bn[:, t, 0:6 * k]).then_inc(sum_ready, 1)

            def layer_norm(t, src, dst):
                rs_wait()
                return v.tensor_scalar(dst, src, mean_var[:, t, 0:1], head_rs[:, 0, t:t + 1], ALU.subtract, ALU.mult)

            def turned(n_banks):
                c.up("T", n_banks)

            def mix_a(s):
                j = stages[s][2]

                def norm_v():
                    for t in range(TT):
                        dve.wait_ge(gelu_ready, c.up("gelu"))
                        layer_stats(t, proj[:, t, MIX:2 * MIX], MIX, MIX // 2)
                    for t in range(TT):
                        link(layer_norm(t, proj[:, t, MIX:2 * MIX], scratch_v[:, t, 0:MIX]))
                        link(v.tensor_tensor(scratch_v[:, t, 0:MIX], scratch_v[:, t, 0:MIX], v_gain[:, j, :],
                                             ALU.mult))
                    dve.wait_ge(gelu_ready, c.up("gelu", TT))
                linear(A_IN, proj, started.pop(s), {2: norm_v}, hook_first=(2,))
                dve.wait_ge(spat_ready, c.up("spat"))
                done()
                dve.wait_ge(mix_full, c.up("mixf"))
                for g in range(HEADS1):
                    at = g * DH1
                    v.scalar_tensor_tensor(ymix[:, :, at:at + DH1],
                                           gflat[:, g * P:(g + 1) * P].rearrange("p (t d) -> p t d", t=TT),
                                           spat_b[:, j, g:g + 1], proj[:, :, at:at + DH1], ALU.add, ALU.mult)
                attention(plan("mix_a"))
                turn_out(KT)

            def mix_b(s):

                def turn(o):
                    for t in range(TT):
                        cs, sn = rope1[:, 0, t, :], rope1[:, 1, t, :]
                        dve.wait_ge(g_taken[t], c["g"] + (o + MIX - 1) // HALF + 1)
                        rope(proj[:, t, o:o + MIX].rearrange("p (h two d) -> p h two d", h=HEADS1, two=2),
                             HEADS1, cs, sn, cs, sn)
                linear(B_IN, proj, started.pop(s), {1: lambda: turn(0), 2: lambda: turn(MIX)})
                done()

                def merge():
                    n = TT * HEADS1 // 3
                    dve.sem_inc(fn_in, 1)
                    dve.wait_ge(fn_out, c.up("fn_out"))
                    link(v.tensor_tensor(shares[:, 0, :], shares[:, 0, :], mx[:, 0:TT * HEADS1], ALU.subtract))
                    l = [shares[:, 0, g * n:(g + 1) * n] for g in range(3)]
                    top = shares[:, 3, 0:n]
                    link(v.tensor_tensor(top, l[0], l[1], ALU.max))
                    link(v.tensor_tensor(top, top, l[2], ALU.max))
                    v.tensor_tensor(shares[:, 1, :].rearrange("p (g n) -> p g n", g=3),
                                    shares[:, 0, :].rearrange("p (g n) -> p g n", g=3),
                                    top.unsqueeze(1).to_broadcast([P, 3, n]), ALU.subtract).then_inc(fn_in, 1)
                    dve.wait_ge(fn_out, c.up("fn_out"))
                    e = [shares[:, 2, g * n:(g + 1) * n] for g in range(3)]
                    link(v.tensor_tensor(top, e[0], e[1], ALU.add))
                    link(v.tensor_tensor(top, top, e[2], ALU.add))
                    link(v.reciprocal(top, top))
                    link(v.tensor_tensor(shares[:, 4, :].rearrange("p (g n) -> p g n", g=3),
                                         shares[:, 2, :].rearrange("p (g n) -> p g n", g=3),
                                         top.unsqueeze(1).to_broadcast([P, 3, n]), ALU.mult))
                    share = shares[:, 4, :].rearrange("p (h t) -> p h t", t=TT)
                    for t in range(TT):
                        o = parts_o[:, t, :].rearrange("p (h d) -> p h d", h=HEADS1)
                        link(v.tensor_tensor(o, o, share[:, :, t].unsqueeze(2).to_broadcast([P, HEADS1, DH1]),
                                             ALU.mult))
                    link(v.tensor_tensor(ymix[:, :, 0:DIL_OUT], parts_o[:, :, 0:DIL_OUT],
                                         parts_o[:, :, DIL_OUT:2 * DIL_OUT], ALU.add))
                    v.tensor_tensor(ymix[:, :, 0:DIL_OUT], ymix[:, :, 0:DIL_OUT],
                                    parts_o[:, :, 2 * DIL_OUT:3 * DIL_OUT], ALU.add).then_inc(mix_ready, 1)
                attention(plan("mix_b"), merge)
                turn_out(B_OUT // P)

            def mix_c(s):
                linear(C_IN, proj, started.pop(s), {4: forgets})
                done()
                attention(plan("mix_c"))
                turn_out(KT)

            def forgets():
                f = proj[:, :, 3 * MIX:3 * MIX + HEADS1]
                fb = forget_b[:, :].unsqueeze(1).to_broadcast([P, TT, HEADS1])
                for t in range(TT):
                    dve.wait_ge(g_taken[t], c["g"] + 5)
                link(v.tensor_tensor(fgt[:, 0], f, fb, ALU.add))
                v.scalar_tensor_tensor(fgt[:, 1], fgt[:, 0], -1.0, fgt[:, 0], ALU.mult, ALU.min).then_inc(fn_in, 1)
                dve.wait_ge(fn_out, c.up("fn_out"))
                link(v.tensor_scalar(fgt[:, 2], fgt[:, 0], -1.0 / SCALE1, 0.0, ALU.mult, ALU.max))
                link(v.scalar_tensor_tensor(fgt[:, 3], fgt[:, 1], 1.0 / SCALE1, fgt[:, 2], ALU.mult, ALU.add))

            def moba(s):
                linear(3 * D, proj, started.pop(s),
                       {2: lambda: norm_rope("moba", (0, 1)), 4: lambda: norm_rope("moba", (2, 3))}, hook_first=(4,))
                done()
                attention(plan("moba"))
                turn_out(KT)

            def nsa(s):
                def keys():
                    norm_rope("nsa", (0, 1))
                    done()

                def windows():
                    for s2 in range(2):
                        n = c["T"]
                        dve.wait_ge(t_taken[n % 2], n // 2 + 1)
                        c.up("T")
                    for s2 in range(2):
                        for g in range(KVG):
                            seq = kv_t[:, s2, g, :].rearrange("p (m b) -> p b m", b=CMP_STRIDE)
                            for half in range(2):
                                ls = slice(half * CMP_STRIDE, (half + 1) * CMP_STRIDE)
                                ins = v.tensor_tensor(
                                    cmp_in[:, s2, ls, g, :], seq[:, :, half:half + N_CMP],
                                    nsa_pos[:, s2, ls].unsqueeze(2).to_broadcast([P, CMP_STRIDE, N_CMP]), ALU.add)
                    link(ins)
                    done()
                    norm_rope("nsa", (2,))
                linear(NSA_IN, proj, started.pop(s), {1: keys, 3: windows, 4: lambda: norm_rope("nsa", (3,))},
                       NSA_ORDER)
                norm_rope("nsa", (4, 5, 6, 7))
                c.up("fn_out")
                c.up("unit", 8)
                dve.wait_ge(unit_used, c["unit"])
                v.tensor_copy(kc_t[:, :, :].rearrange("p g n -> p (g n)"), S[:, 0, 0:KVG * N_CMP])
                link(v.tensor_copy(vc[0:N_CMP, :, :], G[0:N_CMP, :, 0, 0:DH2]))
                dve.wait_ge(fn_out, c["fn_out"])
                done()
                attention(plan("nsa"))
                turn_out(KT)

            def stick(s):
                linear(3 * D, proj, started.pop(s))
                late()
                base = c["att"]

                def scores():
                    turned(2)
                    for j in range(2):
                        dve.wait_ge(s_full, c.up("att"))
                        v.scalar_tensor_tensor(sc[:, j, :, :], S[:, :, :], SCALE2, mask["strict_add"],
                                               ALU.mult, ALU.add).then_inc(s_taken, 1)
                        dve.wait_ge(s_taken, c["att"])
                        flat = sc[:, j, :, :].rearrange("p t n -> p (t n)")
                        v.scalar_tensor_tensor(pt[:, j, :], flat, -1.0, flat, ALU.mult, ALU.min)\
                         .then_inc(mx_ready, 1)

                scores()
                for pair in range(H2 // 2):
                    for j in range(2):
                        flat = sc[:, j, :, :].rearrange("p t n -> p (t n)")
                        dve.wait_ge(fn_out, c.up("fn_out"))
                        link(v.scalar_tensor_tensor(pt[:, j, :], flat, 0.0, pt[:, j, :], ALU.max, ALU.add))
                        v.tensor_tensor(pt[:, j, :], pt[:, j, :], C("strict_one"), ALU.mult)\
                         .then_inc(prep_ready, 1)
                    for j in range(2):
                        dve.wait_ge(mix_full, c.up("mixf"))
                        v.tensor_tensor(pr[:, j, :, :], sc[:, j, :, :], G[:, j, :, 0:SEQ], ALU.subtract)\
                         .then_inc(arg_ready, 1)
                        dve.wait_ge(arg_ready, c.up("arg"))
                    if pair < H2 // 2 - 1:
                        scores()
                    for j in range(2):
                        h = 2 * pair + j
                        dve.wait_ge(o_full, base + h + 1)
                        v.tensor_copy(ymix[:, :, h * DH2:(h + 1) * DH2], O[:, :, 0:DH2]).then_inc(o_taken, 1)
                    ahead(c["split"] + 1)
                turn_out(KT)

            def conv(s):
                link(v.memset(conv_in[:, :, 0:PAD], 0.0))

                def gate(half):
                    for t in range(TT):
                        dve.wait_ge(fn_out, c.up("fn_out"))
                        at = half * HALF
                        v.tensor_tensor(ymix[:, t, at:at + HALF], proj[:, t, at:at + HALF],
                                        proj[:, t, D + at:D + at + HALF], ALU.mult).then_inc(prep_ready, 1)

                def channels():
                    for t in range(TT):
                        n = c["T"]
                        dve.wait_ge(t_taken[n % 2], n // 2 + 1)
                        c.up("T")

                def taps(lo, hi):
                    base, pairs = c["link"], (hi - lo) // 2
                    with dve.Fori(0, pairs) as i:
                        for odd in (0, 1):
                            for k in range(CONV_PE):
                                ins = v.scalar_tensor_tensor(
                                    conv_acc[:, k, :], conv_in[:, k, bass.ds(2 * i + lo + odd, SEQ)],
                                    conv_taps[:, k, bass.ds(2 * i + lo + odd, 1)], conv_acc[:, k, :], ALU.mult, ALU.add)
                            ins.then_inc(v_link, 1)
                            dve.wait_ge(v_link, base + 1 + odd + 2 * i)
                    c["link"] = base + 2 * pairs

                def early():
                    channels()
                    for k in range(CONV_PE):
                        ins = v.tensor_scalar(conv_acc[:, k, :], conv_in[:, k, 0:SEQ], conv_taps[:, k, 0:1],
                                              conv_cols[:, 0, k:k + 1], ALU.mult, ALU.add)
                    link(ins)
                    taps(1, EARLY_TAPS)
                linear(2 * D, proj, started.pop(s), {1: lambda: gate(0), 2: early}, CONV_ORDER)
                gate(1)
                channels()
                ahead(c["unit"] + RING)
                taps(EARLY_TAPS, CONV_W)
                done()
                for t in range(TT):
                    for b in range(2):
                        n = c["T"]
                        dve.wait_ge(t_taken[n % 2], n // 2 + 1)
                        c.up("T")
                    layer_stats(t, nrm[:, t, :], D, HALF)
                for t in range(TT):
                    layer_norm(t, nrm[:, t, :], ymix[:, t, :]).then_inc(mix_ready, 1)
                for t in range(TT):
                    for b in range(2):
                        at = (slice(None), slice(4 * b, 4 * b + 4), slice(t * P, (t + 1) * P))
                        dve.wait_ge(gelu_ready, c.up("gelu"))
                        v.tensor_copy(hid_hi[at], conv_out[at]).then_inc(turn_hi, 1)
                        dve.wait_ge(turn_hi, c.up("turn"))
                        v.tensor_tensor(hid_lo[at], conv_out[at], hid_hi[at], ALU.subtract)\
                         .then_inc(t_taken[c["T"] % 2], 1)
                        c.up("T")

            def position_tables():
                dve.wait_ge(gains_in, ALL_GAINS)
                dve.wait_ge(consts_in, LOADED)
                link(v.tensor_copy(pos_f[:, :], pos_i[:, :]))
                for t in range(TT):
                    ins = v.tensor_scalar(rtmp[:, 0, t, :], C("inv_freq"), pos_f[:, t:t + 1], None, ALU.mult)
                link(ins)
                ang = rtmp[:, 0]
                for j, quarter in ((0, 0.25), (1, 0.0)):
                    k, r = rtmp[:, 1], rtmp[:, 2 + j]
                    link(v.tensor_scalar(k, ang, 1.0 / TWO_PI, quarter, ALU.mult, ALU.add))
                    link(v.tensor_scalar(k, k, ROUND, None, ALU.add))
                    link(v.tensor_scalar(k, k, -ROUND, None, ALU.add))
                    link(v.scalar_tensor_tensor(r, k, -PI_A, ang, ALU.mult, ALU.add))
                    link(v.scalar_tensor_tensor(r, k, -PI_B, r, ALU.mult, ALU.add))
                    link(v.scalar_tensor_tensor(r, k, -PI_C, r, ALU.mult, ALU.add))
                    link(v.tensor_scalar(r, r, quarter * TWO_PI, PI_TOP, ALU.add, ALU.min))
                    link(v.tensor_scalar(r, r, -PI_TOP, None, ALU.max))
                dve.sem_inc(fn_in, 1)
                dve.wait_ge(fn_out, c.up("fn_out", 2))

            for t in range(TT):
                dve.sem_inc(g_taken[t], 1)
            c["g"] = 1
            c["ry"] = TT
            dve.wait_ge(mem_in, 2 * LOADED)
            dve.wait_ge(consts_in, LOADED)
            c["T"] = 4

            for s, (kind, *arg) in enumerate(stages):
                if s == first_late and s:
                    dve.sem_inc(early_done, 1)
                if kind == "mem_kv":
                    if s == 0:
                        for n in range(4):
                            dve.wait_ge(t_taken[n % 2], n // 2 + 1)
                    if s == 0 or stages[s - 1][0] == "mem_kv":
                        memory(arg[0])
                    if s == 0:
                        ahead(RING)
                        position_tables()
                    linear(2 * MEMW, memkv)
                    start(s + 1)
                    continue
                if kind == "ffn":
                    up(s, FF1 // SEQ, True)
                    c.up("unit", FF1 // P)
                elif kind == "mlp":
                    up(s, FF2 // HALF, False)
                    c.up("unit", FF2 // P)
                else:
                    {"mix_a": mix_a, "mix_b": mix_b, "mix_c": mix_c, "moba": moba, "nsa": nsa,
                     "stick": stick, "conv": conv}[kind](s)
                    c.up("unit", OUT_K[kind])
                if s + 1 < len(stages) and stages[s + 1][0] == "mem_kv":
                    memory(stages[s + 1][1])
                ahead(c["unit"] - last_group({"ffn": FF1 // P, "mlp": FF2 // P, **OUT_K}[kind]) + RING)
                residual(s)

        @block.gpsimd
        def _(pool):
            c = Counts()
            g_ = nc.gpsimd

            last_power = []

            def rsqrt(dst, src, scale, eps, n, done_):
                if last_power:
                    pool.wait_ge(*last_power)
                g_.tensor_scalar(pool_tmp[:, 0:n], src, scale, eps, ALU.mult, ALU.add).then_inc(p_link, 1)
                pool.wait_ge(p_link, c.up("link"))
                g_.tensor_tensor(dst, pool_tmp[:, 0:n], minus_half[:, 0:n], ALU.pow).then_inc(done_, 1)
                last_power[:] = [done_, c.up(done_.name)]

            def heads(kind):
                for b, (_, _, nh, _, t) in enumerate(head_blocks(kind)):
                    pool.wait_ge(sq_ready, c.up("sq"))
                    cols = slice(t * H2, t * H2 + nh)
                    rsqrt(head_rs[:, b // TT, cols], head_sum[:, b // TT, cols], 1.0 / DH2, RMS_EPS, nh, small_ready)

            def variance(t, eps):
                pool.wait_ge(sum_ready, c.up("sum"))
                rsqrt(head_rs[:, 0, t:t + 1], mean_var[:, t, 1:2], 1.0, eps, 1, small_ready)

            def row(s):
                i, j, _ = post_gain(s)
                if c["row"]:
                    pool.wait_ge(x_ready, c["row_x"])
                pool.dma_start(gain_row[:, :], a["norm_g"][i, j:j + 1, :].partition_broadcast(P)
                               .rearrange("p a d -> p (a d)")).then_inc(row_full, LOADED)
                c.up("row")

            def spatial(j):
                pool.dma_start(spat_w[:, :, :], a["a_spatial_t"][j]).then_inc(spat_in, LOADED)
                pool.wait_ge(spat_in, LOADED * c.up("spat"))
                g_.affine_select(out=spat_w[:, :, :], in_=spat_w[:, :, :], compare_op=ALU.is_ge, fill=0.0, base=0,
                                 pattern=[[0, HEADS1], [1, P]], channel_multiplier=-1).then_inc(spat_ready, 1)

            finished = sorted(by_pool)

            def finish_units(s):
                if stages[s][0] == "mem_kv":
                    return
                for m in finished[c["finished"]:c["finished"] + 2]:
                    s_, w = m % RING, unit_cols[m]
                    pool.wait_ge(hi_ready, split_no[m] + 1)
                    g_.tensor_tensor(ring_lo[:, s_, :, 0:w], ring[:, s_, :, 0:w], ring_hi[:, s_, :, 0:w],
                                     ALU.subtract).then_inc(pool_lo_ready, 1)
                c.up("finished", 2)

            for dst, src in loads:
                pool.dma_start(dst, src).then_inc(gains_in, LOADED)
            pool.wait_ge(consts_in, LOADED)
            for t in range(TT):
                pool.wait_ge(ssy_ready, c.up("ssy"))
                rsqrt(small[:, t:t + 1], sums[:, t:t + 1], 1.0 / D, RMS_EPS, 1, ry_ready)
            for t in range(TT):
                pool.wait_ge(ssx_ready, c.up("ssx"))
                rsqrt(small[:, 2 + t:3 + t], sums[:, 2 + t:3 + t], 1.0 / D, RMS_EPS, 1, rx_ready)
            seen_x = 0
            for s, (kind, *arg) in enumerate(stages):
                if kind == "mem_kv":
                    continue
                if s == first_late:
                    pool.wait_ge(early_done, 1)
                    for dst, src in late_loads:
                        pool.dma_start(dst, src).then_inc(late_in, LOADED)
                if kind in POST:
                    c["row_x"] = seen_x
                    row(s)
                if kind == "mix_a":
                    if seen_x:
                        pool.wait_ge(x_ready, seen_x)
                    spatial(arg[1])
                    for t in range(TT):
                        variance(t, LN_EPS)
                elif kind in ("moba", "nsa"):
                    heads(kind)
                elif kind == "conv":
                    for t in range(TT):
                        variance(t, RMS_EPS)
                last = s == len(stages) - 1
                for t in range(TT):
                    if kind in POST:
                        pool.wait_ge(ssy_ready, c.up("ssy"))
                        rsqrt(small[:, t:t + 1], sums[:, t:t + 1], 1.0 / D, RMS_EPS, 1, ry_ready)
                    if t and not last:
                        finish_units(s + 1)
                    if not last:
                        pool.wait_ge(ssx_ready, c.up("ssx"))
                        rsqrt(small[:, 2 + t:3 + t], sums[:, 2 + t:3 + t], 1.0 / D, RMS_EPS, 1, rx_ready)
                seen_x += TT


STAGES = []
for _i, _kind in enumerate(("mix_a", "mix_b", "mix_c", "mix_a")):
    STAGES += ([("mem_kv", 0), ("ffn", 0, 0)] if _i == 0 else [("ffn", _i, 0), ("mem_kv", _i)]) \
        + [(_kind, _i, _i // 3), ("ffn", _i, 1)]
for _i, _kind in enumerate(("nsa", "stick", "conv", "moba")):
    STAGES += [(_kind, _i), ("mlp", _i)]

N_STAGES = len(STAGES)


def kernel(**inputs):
    from concourse import bacc
    from concourse.bass_utils import run_bass_kernel_spmd

    n = {k: np.asarray(v) for k, v in inputs.items()}
    raw = ("x", "mem", "norm_g", "w_mem_kv", "ffn_w_gate_up", "ffn_w_down", "a_w_in", "a_w_out", "b_w_in",
           "b_w_out", "c_w_in", "c_w_out", "c_forget_bias", "a_v_norm_g", "mlp_w_up_2", "mlp_w_down_2",
           "nsa_w_in_2", "nsa_w_out_2", "nsa_q_norm_2", "nsa_k_norm_2", "sb_w_in_2", "sb_w_out_2",
           "conv_w_in_2", "conv_w_out_2", "moba_w_in_2", "moba_w_out_2", "moba_q_norm_2", "moba_k_norm_2")
    arrays = {k: n[k] for k in raw}

    def cols(v):
        v = v.reshape(-1, KT, P)
        return v.transpose(2, 0, 1)

    arrays["consts"], arrays["consts_1"], arrays["consts_2"] = CONSTS, CONSTS_1, CONSTS_2
    arrays["pos"] = n["positions"].reshape(TT, P).T
    arrays["pre_cols"] = cols(n["norm_g"])
    arrays["mem_cols"] = cols(n["mem_norm_g"])
    arrays["an_cols"] = cols(n["attn_norm_2"])
    arrays["mn_cols"] = cols(n["mlp_norm_2"])
    arrays["conv_cols"] = np.concatenate([cols(n[k]) for k in ("conv_dw_b_2", "conv_ln_g_2", "conv_ln_b_2")], 1)
    arrays["conv_taps"] = n["conv_dw_w_2"][0].reshape(CONV_W, KT, P).transpose(2, 1, 0)
    arrays["a_spatial_t"] = n["a_spatial_w"].transpose(0, 3, 1, 2)
    arrays["a_spatial_bt"] = n["a_spatial_b"].transpose(2, 0, 1)
    arrays["nsa_pos"] = n["nsa_cmp_pos_2"][0].transpose(2, 0, 1)
    arrays["nsa_w_cmp_l"] = n["nsa_w_cmp_2"][0].transpose(2, 0, 1, 3)
    nc = bacc.Bacc("TRN2", target_bir_lowering=False, num_devices=1)
    arrays = {k: np.ascontiguousarray(v) for k, v in arrays.items()}
    a = {k: nc.dram_tensor(k, v.shape, mybir.dt.from_np(v.dtype), kind="ExternalInput").ap()
         for k, v in arrays.items()}
    out = nc.dram_tensor("out", (1, SEQ, D), F32, kind="ExternalOutput").ap()
    build(nc, a, out, STAGES[:N_STAGES])
    r = run_bass_kernel_spmd(nc, [arrays], core_ids=[0])
    return r.results[0]["out"]
```
